# Optimizing a Trainium2 kernel written in Bass

```python
import jax
import jax.numpy as jnp
from jax import lax
import numpy as np

D_MODEL = 1024
BATCH = 1
SEQ = 128
DEPTH = 2
DEC_BATCH = 1
DEC_SEQ = 512
PAST_LEN = 128

GRID_W = 64
GD_H = 4
GD_DK = 128
GD_DV = 128
GD_CHUNK = 64
CONV_K = 3
ROPE_BASE = 10000.0
NA_H = 8
NA_D = 64
NA_WR = 8
NA_WC = 16
NA_QC = 16
NA_KC = 32
Q_BLOCK = 128
HG_H = 4
HG_DK = 128
HG_DV = 128
HG_CHUNK = 32
RW_H = 8
RW_D = 64
RW_DECAY_LORA = 64
RW_AAA_LORA = 64
RW_GATE_LORA = 128
RW_GN_EPS = 64e-5
RW_IN_W = 3 * RW_H * RW_D + 2 * RW_DECAY_LORA + RW_AAA_LORA + RW_GATE_LORA
N_BRANCH = 4
BRANCH_W = 512
PEER_HEADS = 8
PEER_NKEYS = 128
PEER_DK = 256
PEER_TOPK = 16
PEER_BLOCK = 128
N_EXPERTS = PEER_NKEYS * PEER_NKEYS
LN_EPS = 1e-5
NORM_EPS = 1e-6

IN_LAYOUT = (
    ('gdn_qkv', 2 * GD_H * GD_DK + GD_H * GD_DV),
    ('gdn_g', GD_H * GD_DV),
    ('gdn_a', 2 * GD_H),
    ('gdn_b', 2 * GD_H),
    ('na_q', NA_H * NA_D),
    ('na_k', NA_H * NA_D),
    ('na_v', NA_H * NA_D),
    ('hg_q', HG_H * HG_DK),
    ('hg_f', 2 * HG_H * HG_DK),
    ('hg_i', HG_H * HG_DV),
    ('hg_g', HG_H * HG_DV),
    ('rw', RW_IN_W),
    ('merge', N_BRANCH * D_MODEL),
)
IN_W = sum(w for _, w in IN_LAYOUT)

kernel_name = 'hybrid_flow_backbone_step'

def layer_norm(x, g, b):
    xf = x.astype(jnp.float32)
    mu = jnp.mean(xf, -1, keepdims=True)
    var = jnp.mean(jnp.square(xf - mu), -1, keepdims=True)
    return ((xf - mu) * lax.rsqrt(var + LN_EPS) * g + b).astype(x.dtype)

def rms_norm(x, w):
    xf = x.astype(jnp.float32)
    return xf * lax.rsqrt(jnp.mean(xf * xf, -1, keepdims=True) + NORM_EPS) * w

def l2_normalize(x):
    xf = x.astype(jnp.float32)
    return xf * lax.rsqrt(jnp.sum(xf * xf, -1, keepdims=True) + NORM_EPS)

def to_heads(t, n):
    B, L, _ = t.shape
    return jnp.moveaxis(t.reshape(B, L, n, -1), 2, 1)

def from_heads(t):
    B, H, L, d = t.shape
    return jnp.moveaxis(t, 1, 2).reshape(B, L, H * d)

def flip_seq(t):
    return jnp.flip(t, axis=2)

def split_in(p):
    out, off = {}, 0
    for name, w in IN_LAYOUT:
        out[name] = p[..., off:off + w]
        off += w
    return out

def centred_dwconv(x, w):
    pad = CONV_K // 2
    L = x.shape[1]
    xp = jnp.pad(x, ((0, 0), (pad, pad), (0, 0)))
    return sum(xp[:, j:j + L] * w[j] for j in range(CONV_K))

def centred_shift(x):
    zero = jnp.zeros_like(x[:, :1])
    return jnp.concatenate([zero, x[:, :-1]], 1), jnp.concatenate([x[:, 1:], zero], 1)

def axial_rope(x):
    L, dh = x.shape[-2], x.shape[-1]
    half = dh // 2
    nf = half // 2
    inv = ROPE_BASE ** (-jnp.arange(nf, dtype=jnp.float32) / nf)
    t = jnp.arange(L)

    def rot(xa, pos):
        ang = pos.astype(jnp.float32)[:, None] * inv[None, :]
        cos, sin = jnp.cos(ang), jnp.sin(ang)
        x1, x2 = xa[..., :nf], xa[..., nf:]
        return jnp.concatenate([x1 * cos - x2 * sin, x1 * sin + x2 * cos], -1)

    return jnp.concatenate([rot(x[..., :half], t // GRID_W), rot(x[..., half:], t % GRID_W)], -1)

def gdn_chunk_scan(q, k, v, log_a, beta, s0):
    B, H, L, dk = q.shape
    dv = v.shape[-1]
    C = GD_CHUNK
    n = L // C
    q = q.reshape(B, H, n, C, dk)
    k = k.reshape(B, H, n, C, dk)
    v = v.reshape(B, H, n, C, dv)
    beta = beta.reshape(B, H, n, C, 1)
    g = jnp.cumsum(log_a.reshape(B, H, n, C), axis=-1)
    incl = jnp.tril(jnp.ones((C, C), bool))
    strict = jnp.tril(jnp.ones((C, C), bool), -1)
    decay = jnp.exp(jnp.where(incl, g[..., :, None] - g[..., None, :], -jnp.inf))
    a_mat = jnp.where(strict, beta * jnp.einsum('bhncd,bhnjd->bhncj', k, k) * decay, 0.0)
    eye = jnp.eye(C, dtype=jnp.float32)
    rhs = jnp.concatenate([beta * v, beta * jnp.exp(g)[..., None] * k], -1)
    sol = lax.linalg.triangular_solve(eye + a_mat, rhs, left_side=True, lower=True, unit_diagonal=True)
    u, w = sol[..., :dv], sol[..., dv:]
    attn = jnp.einsum('bhncd,bhnjd->bhncj', q, k) * decay
    q_dec = q * jnp.exp(g)[..., None]
    g_last = g[..., -1]
    k_dec = k * jnp.exp(g_last[..., None] - g)[..., None]

    def step(S, xs):
        u_c, w_c, attn_c, qd_c, kd_c, gl_c = xs
        v_new = u_c - jnp.einsum('bhcd,bhde->bhce', w_c, S)
        o = jnp.einsum('bhcd,bhde->bhce', qd_c, S) + jnp.einsum('bhcj,bhje->bhce', attn_c, v_new)
        S = S * jnp.exp(gl_c)[..., None, None] + jnp.einsum('bhcd,bhce->bhde', kd_c, v_new)
        return S, o

    mv = lambda t: jnp.moveaxis(t, 2, 0)
    S, o = lax.scan(step, s0.astype(jnp.float32), (mv(u), mv(w), mv(attn), mv(q_dec), mv(k_dec), mv(g_last)))
    return jnp.moveaxis(o, 0, 2).reshape(B, H, L, dv), S

def hgrn_chunk_scan(q, kf, logf, i, s0):
    B, H, L, dk = q.shape
    dv = i.shape[-1]
    C = HG_CHUNK
    n = L // C
    chunks = lambda t: jnp.moveaxis(t.reshape(B, H, n, C, t.shape[-1]), 2, 0)
    b = jnp.cumsum(logf.reshape(B, H, n, C, dk), axis=3)
    incl = jnp.tril(jnp.ones((C, C), bool))[:, :, None]

    def step(S, xs):
        q_c, k_c, b_c, i_c = xs
        dec = jnp.exp(jnp.where(incl, b_c[:, :, :, None, :] - b_c[:, :, None, :, :], -jnp.inf))
        attn = jnp.einsum('bhtc,bhjc,bhtjc->bhtj', q_c, k_c, dec)
        b_last = b_c[:, :, -1:, :]
        o = jnp.einsum('bhtc,bhce->bhte', q_c * jnp.exp(b_c), S) + jnp.einsum('bhtj,bhje->bhte', attn, i_c)
        S = jnp.exp(b_last[:, :, 0, :, None]) * S + jnp.einsum('bhjc,bhje->bhce', k_c * jnp.exp(b_last - b_c), i_c)
        return S, o

    S, o = lax.scan(step, s0.astype(jnp.float32), (chunks(q), chunks(kf), jnp.moveaxis(b, 2, 0), chunks(i)))
    return jnp.moveaxis(o, 0, 2).reshape(B, H, L, dv), S

def rwkv_scan(r, dec, k, v, kk, a, s0, reverse):
    def step(S, xs):
        r_t, w_t, k_t, v_t, kk_t, a_t = xs
        sa = jnp.einsum('bhvk,bhk->bhv', S, -kk_t)
        S = S * w_t[:, :, None, :] + sa[..., None] * (kk_t * a_t)[:, :, None, :] + v_t[..., None] * k_t[:, :, None, :]
        return S, jnp.einsum('bhvk,bhk->bhv', S, r_t)

    xs = tuple(jnp.moveaxis(t, 1, 0) for t in (r, dec, k, v, kk, a))
    S, y = lax.scan(step, s0.astype(jnp.float32), xs, reverse=reverse)
    return jnp.moveaxis(y, 0, 1), S

def na_context(q, k, v):
    B, H, L, d = q.shape
    nb = L // Q_BLOCK
    qb = jnp.moveaxis(q.reshape(B, H, nb, Q_BLOCK, d), 2, 0)

    def block(qi):
        s = jnp.einsum('bhqd,bhkd->bhqk', qi, k).astype(jnp.float32)
        p = jax.nn.softmax(s, -1).astype(v.dtype)
        return jnp.einsum('bhqk,bhkd->bhqd', p, v)

    o = lax.map(block, qb)
    return jnp.moveaxis(o, 0, 2).reshape(B, H, L, d)

def na_latent(q, k, v, k_ctx, v_ctx, rpb):
    B, H, L, d = q.shape
    rows = L // GRID_W
    wr = min(NA_WR, rows)
    ncb = GRID_W // NA_QC
    qcol = np.arange(GRID_W).reshape(ncb, NA_QC)
    kc0 = np.clip(np.arange(ncb) * NA_QC - NA_WC // 2, 0, GRID_W - NA_KC)
    kcol = kc0[:, None] + np.arange(NA_KC)
    qs = np.clip(qcol - NA_WC // 2, 0, GRID_W - NA_WC)
    col_ok = (kcol[:, None, :] >= qs[..., None]) & (kcol[:, None, :] < qs[..., None] + NA_WC)
    col_bias = np.clip(kcol[:, None, :] - qcol[..., None] + NA_WC - 1, 0, 2 * NA_WC - 2)
    kg = k.reshape(B, H, rows, GRID_W, d)[:, :, :, kcol]
    vg = v.reshape(B, H, rows, GRID_W, d)[:, :, :, kcol]
    qr = jnp.moveaxis(q.reshape(B, H, rows, ncb, NA_QC, d), 2, 0)
    rpb = rpb.astype(jnp.float32)
    nwin = wr * NA_KC

    def row(xs):
        q_r, r = xs
        s0 = jnp.clip(r - wr // 2, 0, rows - wr)
        k_b = lax.dynamic_slice_in_dim(kg, s0, wr, axis=2)
        v_b = lax.dynamic_slice_in_dim(vg, s0, wr, axis=2)
        s_win = jnp.einsum('bhnqd,bhwnkd->bhnqwk', q_r, k_b).astype(jnp.float32)
        roff = s0 + jnp.arange(wr) - r + NA_WR - 1
        bias = jnp.transpose(rpb[:, roff][:, :, col_bias], (0, 2, 3, 1, 4))
        s_win = jnp.where(col_ok[:, :, None, :], s_win + bias, -jnp.inf)
        s_ctx = jnp.einsum('bhnqd,bhkd->bhnqk', q_r, k_ctx).astype(jnp.float32)
        s = jnp.concatenate([s_win.reshape(B, H, ncb, NA_QC, nwin), s_ctx], -1)
        p = jax.nn.softmax(s, -1).astype(v.dtype)
        p_win = p[..., :nwin].reshape(B, H, ncb, NA_QC, wr, NA_KC)
        return (jnp.einsum('bhnqwk,bhwnkd->bhnqd', p_win, v_b)
                + jnp.einsum('bhnqk,bhkd->bhnqd', p[..., nwin:], v_ctx))

    o = lax.map(row, (qr, jnp.arange(rows)))
    return jnp.moveaxis(o, 0, 2).reshape(B, H, L, d)

def token_mixing(h, lp, lb, cache):
    latent = cache is not None
    B, L, _ = h.shape
    dt = h.dtype
    f32 = jnp.float32
    P = split_in(h @ lp['w_in'])
    if latent:
        s_gdn, s_hg, s_rw, k_ctx, v_ctx = cache
    else:
        s_gdn = jnp.zeros((B, 2, GD_H, GD_DK, GD_DV), f32)
        s_hg = jnp.zeros((B, 2, HG_H, HG_DK, HG_DV), f32)
        s_rw = jnp.zeros((B, 2, RW_H, RW_D, RW_D), f32)

    qkv = jax.nn.silu(centred_dwconv(P['gdn_qkv'], lp['gdn_conv']))
    q, k, v = jnp.split(qkv, [GD_H * GD_DK, 2 * GD_H * GD_DK], axis=-1)
    q = l2_normalize(to_heads(q, GD_H))
    k = l2_normalize(to_heads(k, GD_H))
    if latent:
        q, k = axial_rope(q), axial_rope(k)
    q = q * GD_DK ** -0.5
    v = to_heads(v, GD_H).astype(f32)
    a_in = P['gdn_a'].astype(f32).reshape(B, L, 2, GD_H)
    log_a = jnp.moveaxis(-jnp.exp(lp['gdn_A_log'].astype(f32)) * jax.nn.softplus(a_in + lp['gdn_dt_bias']), 1, -1)
    beta = jnp.moveaxis(jax.nn.sigmoid(P['gdn_b'].astype(f32).reshape(B, L, 2, GD_H)), 1, -1)
    o_f, sg_f = gdn_chunk_scan(q, k, v, log_a[:, 0], beta[:, 0], s_gdn[:, 0])
    o_b, sg_b = gdn_chunk_scan(flip_seq(q), flip_seq(k), flip_seq(v), flip_seq(log_a[:, 1]),
                               flip_seq(beta[:, 1]), s_gdn[:, 1])
    o = o_f + flip_seq(o_b)
    y_a = from_heads(rms_norm(o, lp['gdn_norm']) * jax.nn.silu(to_heads(P['gdn_g'], GD_H).astype(f32))).astype(dt)

    qn = to_heads(P['na_q'], NA_H) * NA_D ** -0.5
    kn = to_heads(P['na_k'], NA_H)
    vn = to_heads(P['na_v'], NA_H)
    on = na_latent(qn, kn, vn, k_ctx, v_ctx, lp['na_rpb']) if latent else na_context(qn, kn, vn)
    y_b = from_heads(on).astype(dt)

    qh = to_heads(P['hg_q'], HG_H).astype(f32)
    ih = to_heads(P['hg_i'], HG_H).astype(f32)
    z = jnp.transpose(P['hg_f'].astype(f32).reshape(B, L, 2, HG_H, HG_DK), (0, 2, 3, 1, 4))
    lbh = lb.reshape(HG_H, 1, HG_DK)
    logf = jnp.logaddexp(jnp.log(lbh), jnp.log1p(-lbh) + jax.nn.log_sigmoid(z))
    kf = (1.0 - lbh) * jax.nn.sigmoid(-z)
    o_f, sh_f = hgrn_chunk_scan(qh, kf[:, 0], logf[:, 0], ih, s_hg[:, 0])
    o_b, sh_b = hgrn_chunk_scan(flip_seq(qh), flip_seq(kf[:, 1]), flip_seq(logf[:, 1]), flip_seq(ih), s_hg[:, 1])
    o = o_f + flip_seq(o_b)
    y_c = from_heads(rms_norm(o, lp['hg_norm']) * jax.nn.silu(to_heads(P['hg_g'], HG_H).astype(f32))).astype(dt)

    xr = P['rw']
    prev, nxt = centred_shift(xr)
    xr = (xr + lp['rw_mu'][0] * (prev - xr) + lp['rw_mu'][1] * (nxt - xr)).astype(f32)
    RW = RW_H * RW_D
    r, kr, vr = xr[..., :RW], xr[..., RW:2 * RW], xr[..., 2 * RW:3 * RW]
    o0 = 3 * RW
    wl = xr[..., o0:o0 + 2 * RW_DECAY_LORA]
    o0 += 2 * RW_DECAY_LORA
    al = xr[..., o0:o0 + RW_AAA_LORA]
    o0 += RW_AAA_LORA
    gl = xr[..., o0:o0 + RW_GATE_LORA]
    a = jax.nn.sigmoid(lp['rw_a0'] + al @ lp['rw_a2'])
    gate = jax.nn.sigmoid(gl) @ lp['rw_g2']
    sp = lambda t: t.reshape(B, L, RW_H, RW_D)
    kk = l2_normalize(sp(kr * lp['rw_kk']))
    kr = kr * (1.0 + (a - 1.0) * lp['rw_ka'])
    r4, k4, v4, a4 = sp(r), sp(kr), sp(vr), sp(a)

    def decay(dirn):
        wd = wl[..., dirn * RW_DECAY_LORA:(dirn + 1) * RW_DECAY_LORA]
        wlog = -jax.nn.softplus(-(lp['rw_w0'][dirn] + jnp.tanh(wd) @ lp['rw_w2'][dirn])) - 0.5
        return sp(jnp.exp(-jnp.exp(wlog)))

    yr_f, sr_f = rwkv_scan(r4, decay(0), k4, v4, kk, a4, s_rw[:, 0], False)
    yr_b, sr_b = rwkv_scan(r4, decay(1), k4, v4, kk, a4, s_rw[:, 1], True)
    y = yr_f + yr_b
    mu = jnp.mean(y, -1, keepdims=True)
    var = jnp.mean(jnp.square(y - mu), -1, keepdims=True)
    y = ((y - mu) * lax.rsqrt(var + RW_GN_EPS)).reshape(B, L, RW) * lp['rw_gn_w'] + lp['rw_gn_b']
    y = y + (jnp.sum(r4 * k4 * lp['rw_rk'], -1, keepdims=True) * v4).reshape(B, L, RW)
    y_d = (y * gate).astype(dt)

    gates = jax.nn.sigmoid(P['merge'].astype(f32)).reshape(B, L, N_BRANCH, D_MODEL)
    branches = jnp.stack([y_a, y_b, y_c, y_d], axis=2)
    proj = jnp.einsum('blmc,mcd->blmd', branches, lp['w_branch'])
    out = jnp.sum(gates * proj, axis=2).astype(dt) @ lp['w_out']
    if latent:
        return out, None
    return out, (jnp.stack([sg_f, sg_b], 1), jnp.stack([sh_f, sh_b], 1), jnp.stack([sr_f, sr_b], 1), kn, vn)

def peer(h, wq, keys, u_tab, v_tab):
    B, L, D = h.shape
    xt = h.reshape(-1, PEER_BLOCK, D)
    half = PEER_DK // 2
    keys = keys.astype(jnp.float32)

    def block(xb):
        t = xb.shape[0]
        qh = (xb @ wq).reshape(t, PEER_HEADS, 2, half).astype(jnp.float32)
        s = jnp.einsum('thpd,hpnd->thpn', qh, keys)
        sv, si = lax.top_k(s, PEER_TOPK)
        cand = (sv[:, :, 0, :, None] + sv[:, :, 1, None, :]).reshape(t, PEER_HEADS, -1)
        cidx = (si[:, :, 0, :, None] * PEER_NKEYS + si[:, :, 1, None, :]).reshape(t, PEER_HEADS, -1)
        best, pos = lax.top_k(cand, PEER_TOPK)
        e = jnp.take_along_axis(cidx, pos, -1)
        g = jax.nn.softmax(best, -1)
        act = jax.nn.gelu(jnp.einsum('thkd,td->thk', u_tab[e], xb).astype(jnp.float32))
        return jnp.einsum('thk,thkd->td', (g * act).astype(xb.dtype), v_tab[e])

    return lax.map(block, xt).reshape(B, L, D)

def trunk_layer(x, mod, lp, lb, cache, alpha):
    sh1, sc1, g1, sh2, sc2, g2 = mod
    h = x * (1 + sc1) + sh1
    y, ctx_out = token_mixing(h, lp, lb, cache)
    x = layer_norm(alpha * x + g1 * y, lp['ln1_g'], lp['ln1_b'])
    h = x * (1 + sc2) + sh2
    y = peer(h, lp['peer_wq'], lp['peer_keys'], lp['peer_u'], lp['peer_v'])
    x = layer_norm(alpha * x + g2 * y, lp['ln2_g'], lp['ln2_b'])
    return x, ctx_out

def setup_inputs(seed: int = 0) -> dict:
    key = jax.random.key(seed)
    ks = iter(jax.random.split(key, 48))
    f32 = jnp.float32
    D = D_MODEL
    RW = RW_H * RW_D
    beta_dn = (8.0 * DEPTH) ** -0.25

    def nrm(shape, scale=1.0):
        return scale * jax.random.normal(next(ks), shape, f32)

    def unif(shape, lo, hi):
        return jax.random.uniform(next(ks), shape, f32, lo, hi)

    return {
        'x_prompt': nrm((BATCH, SEQ, D)),
        'x_sample': nrm((DEC_BATCH, DEC_SEQ, D)),
        'c': nrm((DEC_BATCH, D)),
        'c_ctx': nrm((D,)),
        'state_gdn': nrm((DEC_BATCH, DEPTH, 2, GD_H, GD_DK, GD_DV), 0.1),
        'state_hgrn': nrm((DEC_BATCH, DEPTH, 2, HG_H, HG_DK, HG_DV), 0.3),
        'state_rwkv': nrm((DEC_BATCH, DEPTH, 2, RW_H, RW_D, RW_D), 0.3),
        'cache_k_na': nrm((DEC_BATCH, DEPTH, NA_H, PAST_LEN, NA_D)),
        'cache_v_na': nrm((DEC_BATCH, DEPTH, NA_H, PAST_LEN, NA_D)),
        'w_mod': nrm((DEPTH, D, 6 * D), 0.5 * D ** -0.5),
        'b_mod': nrm((DEPTH, 6 * D), 0.02),
        'w_in': nrm((DEPTH, D, IN_W), D ** -0.5),
        'gdn_conv': nrm((DEPTH, CONV_K, 2 * GD_H * GD_DK + GD_H * GD_DV), CONV_K ** -0.5),
        'gdn_A_log': jnp.log(unif((DEPTH, 2, GD_H), 1.0, 16.0)),
        'gdn_dt_bias': jnp.log(jnp.expm1(unif((DEPTH, 2, GD_H), 0.001, 0.1))),
        'gdn_norm': 1.0 + nrm((DEPTH, GD_DV), 0.1),
        'na_rpb': nrm((DEPTH, NA_H, 2 * NA_WR - 1, 2 * NA_WC - 1), 0.1),
        'hg_lb_logits': nrm((DEPTH, HG_H * HG_DK)),
        'hg_norm': 1.0 + nrm((DEPTH, HG_DV), 0.1),
        'rw_mu': unif((DEPTH, 2, RW_IN_W), 0.0, 0.5),
        'rw_w0': nrm((DEPTH, 2, RW), 0.5),
        'rw_w2': nrm((DEPTH, 2, RW_DECAY_LORA, RW), 0.1),
        'rw_a0': nrm((DEPTH, RW), 0.5),
        'rw_a2': nrm((DEPTH, RW_AAA_LORA, RW), 0.1),
        'rw_g2': nrm((DEPTH, RW_GATE_LORA, RW), RW_GATE_LORA ** -0.5),
        'rw_kk': 1.0 + nrm((DEPTH, RW), 0.1),
        'rw_ka': 1.0 + nrm((DEPTH, RW), 0.1),
        'rw_rk': nrm((DEPTH, RW_H, RW_D), 0.1),
        'rw_gn_w': 1.0 + nrm((DEPTH, RW), 0.1),
        'rw_gn_b': nrm((DEPTH, RW), 0.02),
        'w_branch': nrm((DEPTH, N_BRANCH, BRANCH_W, D), BRANCH_W ** -0.5),
        'w_out': nrm((DEPTH, D, D), beta_dn * D ** -0.5),
        'ln1_g': 1.0 + nrm((DEPTH, D), 0.1),
        'ln1_b': nrm((DEPTH, D), 0.02),
        'ln2_g': 1.0 + nrm((DEPTH, D), 0.1),
        'ln2_b': nrm((DEPTH, D), 0.02),
        'peer_wq': nrm((DEPTH, D, PEER_HEADS * PEER_DK), D ** -0.5),
        'peer_keys': nrm((DEPTH, PEER_HEADS, 2, PEER_NKEYS, PEER_DK // 2), (PEER_DK // 2) ** -0.5),
        'peer_u': nrm((DEPTH, N_EXPERTS, D), D ** -0.5),
        'peer_v': nrm((DEPTH, N_EXPERTS, D), beta_dn),
    }

def reference(x_prompt, x_sample, c, c_ctx, state_gdn, state_hgrn, state_rwkv, cache_k_na, cache_v_na,
              w_mod, b_mod, w_in, gdn_conv, gdn_A_log, gdn_dt_bias, gdn_norm, na_rpb, hg_lb_logits, hg_norm,
              rw_mu, rw_w0, rw_w2, rw_a0, rw_a2, rw_g2, rw_kk, rw_ka, rw_rk, rw_gn_w, rw_gn_b,
              w_branch, w_out, ln1_g, ln1_b, ln2_g, ln2_b, peer_wq, peer_keys, peer_u, peer_v):
    alpha = (2.0 * DEPTH) ** 0.25
    lb_all = jnp.cumsum(jax.nn.softmax(hg_lb_logits.astype(jnp.float32), axis=0), axis=0)
    lb_all = lb_all - lb_all[0]
    y_prompt, y_sample = x_prompt, x_sample
    gdn_l, hg_l, rw_l, k_l, v_l = [], [], [], [], []
    for l in range(DEPTH):
        lp = {
            'w_in': w_in[l], 'gdn_conv': gdn_conv[l], 'gdn_A_log': gdn_A_log[l], 'gdn_dt_bias': gdn_dt_bias[l],
            'gdn_norm': gdn_norm[l], 'na_rpb': na_rpb[l], 'hg_norm': hg_norm[l], 'rw_mu': rw_mu[l],
            'rw_w0': rw_w0[l], 'rw_w2': rw_w2[l], 'rw_a0': rw_a0[l], 'rw_a2': rw_a2[l], 'rw_g2': rw_g2[l],
            'rw_kk': rw_kk[l], 'rw_ka': rw_ka[l], 'rw_rk': rw_rk[l], 'rw_gn_w': rw_gn_w[l], 'rw_gn_b': rw_gn_b[l],
            'w_branch': w_branch[l], 'w_out': w_out[l], 'ln1_g': ln1_g[l], 'ln1_b': ln1_b[l],
            'ln2_g': ln2_g[l], 'ln2_b': ln2_b[l], 'peer_wq': peer_wq[l], 'peer_keys': peer_keys[l],
            'peer_u': peer_u[l], 'peer_v': peer_v[l],
        }
        mod_ctx = jnp.split(jax.nn.silu(c_ctx) @ w_mod[l] + b_mod[l], 6, axis=-1)
        mod_lat = [m[:, None, :] for m in jnp.split(jax.nn.silu(c) @ w_mod[l] + b_mod[l], 6, axis=-1)]
        y_prompt, ctx_out = trunk_layer(y_prompt, mod_ctx, lp, lb_all[l], None, alpha)
        cache = (state_gdn[:, l], state_hgrn[:, l], state_rwkv[:, l], cache_k_na[:, l], cache_v_na[:, l])
        y_sample, _ = trunk_layer(y_sample, mod_lat, lp, lb_all[l], cache, alpha)
        gdn_l.append(ctx_out[0])
        hg_l.append(ctx_out[1])
        rw_l.append(ctx_out[2])
        k_l.append(ctx_out[3])
        v_l.append(ctx_out[4])
    new_state_gdn = jnp.stack(gdn_l, 1)
    new_state_hgrn = jnp.stack(hg_l, 1)
    new_state_rwkv = jnp.stack(rw_l, 1)
    new_cache_k_na = jnp.stack(k_l, 1)
    new_cache_v_na = jnp.stack(v_l, 1)
    return (y_prompt, y_sample, new_state_gdn, new_state_hgrn, new_state_rwkv, new_cache_k_na, new_cache_v_na)


_drawn_inputs = setup_inputs


def setup_inputs(seed=0):
    import zlib

    import numpy as np

    out = dict(_drawn_inputs(seed))
    spreads = {}
    factors = {'state_gdn': 8.0,
     'state_hgrn': 8.0,
     'state_rwkv': 8.0,
     'cache_k_na': 6.837,
     'cache_v_na': 5.956,
     'gdn_norm': 6.982,
     'na_rpb': 64.0,
     'hg_norm': 6.748,
     'rw_rk': 5.344,
     'rw_gn_w': 7.533,
     'rw_gn_b': 40.637}
    for name, (base, spread) in spreads.items():
        noise = np.random.default_rng([zlib.crc32(name.encode()), seed]).standard_normal(out[name].shape)
        drawn = base * np.exp(spread * noise) if base else spread * noise
        out[name] = jnp.asarray(drawn.astype(out[name].dtype))
    for name, factor in factors.items():
        out[name] = (out[name] * factor).astype(out[name].dtype)
    return out
```

```python
from collections import namedtuple
from contextlib import ExitStack

import numpy as np
import concourse.bass as bass
from concourse import mybir

F32 = mybir.dt.float32
I32 = mybir.dt.int32
U32 = mybir.dt.uint32
ALU = mybir.AluOpType
ACT = mybir.ActivationFunctionType
AX = mybir.AxisListType

P = 128
D = 1024
KD = D // P
DEPTH = 2
CTX, LAT = 128, 512
TILES = (CTX + LAT) // P
LAT_TILES = LAT // P
GRID_W = 64
CHUNK = 512
GD_H = HG_H = 4
NA_H, NA_D = 8, 64
NA_WC = 16
RW_H, RW_D = 8, 64
RW = RW_H * RW_D
N_BRANCH, BRANCH_W = 4, 512
HEADS, NKEYS, TOPK = 8, 128, 16
HALF = 128
PICKS = HEADS * TOPK
N_EXPERTS = NKEYS * NKEYS
LN_EPS, NORM_EPS, RW_GN_EPS = 1e-5, 1e-6, 64e-5
ALPHA = float((2.0 * DEPTH) ** 0.25)

WIDTHS = (('gdn_qkv', 1536), ('gdn_g', 512), ('gdn_a', 8), ('gdn_b', 8), ('na_q', 512), ('na_k', 512),
          ('na_v', 512), ('hg_q', 512), ('hg_f', 1024), ('hg_i', 512), ('hg_g', 512), ('rw', 1856),
          ('merge', 4096))
COL, IN_W = {}, 0
for _name, _w in WIDTHS:
    COL[_name] = IN_W
    IN_W += _w
RW_W = 1856

ROW_CTX, ROW_LAT = 1, 2 + CTX
P_ROWS = 3 + CTX + LAT
LEVELS = 7


class Stage:

    count = 0

    def __init__(self, nc, name):
        self.nc, self.name, self.ctx, self.sems = nc, f"{name}{Stage.count}", ExitStack(), []
        Stage.count += 1

    def __enter__(self):
        return self

    def sb(self, name, shape, dt=F32):
        return self.ctx.enter_context(self.nc.sbuf_tensor(f"{self.name}_{name}", shape, dt))

    def ps(self, name, shape, dt=F32):
        return self.ctx.enter_context(self.nc.psum_tensor(f"{self.name}_{name}", shape, dt))

    def sem(self, name):
        self.sems.append(self.ctx.enter_context(self.nc.semaphore(f"{self.name}_{name}")))
        return self.sems[-1]

    def __exit__(self, *exc):
        if exc[0] is None:
            for s in self.sems:
                self.nc.gpsimd.sem_clear(s)
            self.nc.all_engine_barrier()
            self.ctx.close()


class Chain:

    def __init__(self, eng, sem):
        self.eng, self.sem, self.n = eng, sem, 0

    def __call__(self, ins):
        self.n += 1
        ins.then_inc(self.sem, 1)
        self.eng.wait_ge(self.sem, self.n)


class Loads:

    def __init__(self, eng, sem):
        self.eng, self.sem, self.n = eng, sem, 0

    def __call__(self, dst, src):
        self.n += 1
        self.eng.dma_start(dst, src).then_inc(self.sem, 16)

    def wait(self):
        self.eng.wait_ge(self.sem, 16 * self.n)


def named(**items):
    return namedtuple("Named", items)(**items)


def rows(ap, start, size=P):
    return ap[bass.ds(start, size), :]


def start_stage(nc, e):
    with Stage(nc, "start") as st:
        zeros = st.sb("zeros", [1, IN_W])
        s_zero, s_dma = st.sem("zero"), st.sem("dma")
        with nc.Block() as block:
            @block.vector
            def _(dve):
                dve.memset(zeros[:], 0.0).then_inc(s_zero, 1)

            @block.sync
            def _(sp):
                ld = Loads(sp, s_dma)
                ld(e.X[0:CTX, :], e.x_prompt)
                ld(e.X[CTX:, :], e.x_sample)
                sp.wait_ge(s_zero, 1)
                for r in (0, ROW_LAT - 1, P_ROWS - 1):
                    ld(e.PR[r:r + 1, :], zeros[:])
                ld.wait()


def mod_stage(nc, e, l):
    n_chunks = 6 * D // CHUNK
    with Stage(nc, "mod") as st:
        c_in, c_sig = st.sb("c_in", [P, KD, 2]), st.sb("c_sig", [P, KD, 2])
        w = st.sb("w", [P, 2, KD, CHUNK])
        bias, mod = st.sb("bias", [2, 6 * D]), st.sb("mod", [2, 6 * D])
        lg, lb = st.sb("lg", [1, 2, 512]), st.sb("lb", [1, 4, 512])
        ps = st.ps("ps", [P, 2, CHUNK])
        s_in, s_w, s_out = st.sem("in"), [st.sem("w0"), st.sem("w1")], st.sem("out")
        s_sig, s_silu, s_mm, s_add = st.sem("sig"), st.sem("silu"), st.sem("mm"), st.sem("add")
        s_diff, s_lb, s_dve, s_scaled = st.sem("diff"), st.sem("lbsig"), st.sem("dve"), st.sem("scaled")
        with nc.Block() as block:
            @block.sync
            def _(sp):
                ld = Loads(sp, s_in)
                ld(c_in[:], e.c_cols)
                for g in range(2):
                    ld(bias[g:g + 1, :], e.b_mod[l, :].unsqueeze(0))
                ld(lg[:], e.hg_lb_logits.unsqueeze(0))
                for j in range(n_chunks):
                    if j >= 2:
                        sp.wait_ge(s_mm, j - 1)
                    sp.dma_start(w[:, j % 2], e.w_mod[l, :, j * CHUNK:(j + 1) * CHUNK]
                                 .rearrange("(k p) n -> p k n", p=P)).then_inc(s_w[j % 2], 16)
                sp.wait_ge(s_scaled, 1)
                out = Loads(sp, s_out)
                for m in range(TILES):
                    g = 0 if m == 0 else 1
                    out(e.MOD[m:m + 1, :], mod[g:g + 1, :])
                out(e.LB.unsqueeze(0), lb[:, 2:4, :])
                out.wait()

            @block.scalar
            def _(act):
                act.wait_ge(s_in, 64)
                act.activation(c_sig[:], c_in[:], ACT.Sigmoid).then_inc(s_sig, 1)
                act.wait_ge(s_diff, 1)
                act.activation(lb[:, 1, :], lb[:, 0, :], ACT.Sigmoid).then_inc(s_lb, 1)

            @block.tensor
            def _(pe):
                pe.wait_ge(s_silu, 1)
                for j in range(n_chunks):
                    pe.wait_ge(s_w[j % 2], 16 * (j // 2 + 1))
                    if j >= 2:
                        pe.wait_ge(s_add, j - 1)
                    for k in range(KD):
                        mm = pe.matmul(ps[0:2, j % 2, :], c_in[:, k, :], w[:, j % 2, k, :],
                                       start=(k == 0), stop=(k == KD - 1))
                    mm.then_inc(s_mm, 1)

            @block.vector
            def _(dve):
                step = Chain(dve, s_dve)
                dve.wait_ge(s_in, 64)
                dve.tensor_tensor(lb[:, 0, :], lg[:, 1, :], lg[:, 0, :], ALU.subtract).then_inc(s_diff, 1)
                dve.wait_ge(s_sig, 1)
                dve.tensor_tensor(c_in[:], c_in[:], c_sig[:], ALU.mult).then_inc(s_silu, 1)
                dve.wait_ge(s_lb, 1)
                step(dve.memset(lb[:, 2, :], 0.0))
                step(dve.tensor_copy(lb[:, 3, :], lb[:, 1, :]))
                for j in range(n_chunks):
                    cols = slice(j * CHUNK, (j + 1) * CHUNK)
                    dve.wait_ge(s_mm, j + 1)
                    dve.tensor_tensor(mod[:, cols], ps[0:2, j % 2, :], bias[:, cols], ALU.add).then_inc(s_add, 1)
                dve.wait_ge(s_add, n_chunks)
                for part in (1, 4):
                    ins = dve.tensor_scalar(mod[:, part * D:(part + 1) * D], mod[:, part * D:(part + 1) * D],
                                            1.0, None, ALU.add)
                    if part == 1:
                        step(ins)
                ins.then_inc(s_scaled, 1)


def project_stage(nc, e, l, part, w_src, n_cols, dst_lat, dst_ctx):
    sizes = [CHUNK] * (n_cols // CHUNK) + ([n_cols % CHUNK] if n_cols % CHUNK else [])
    n = len(sizes)
    with Stage(nc, "proj") as st:
        x = st.sb("x", [P, TILES, D])
        hT = st.sb("hT", [P, KD, TILES * P])
        mrows, mcols = st.sb("mrows", [4 * KD, P]), st.sb("mcols", [P, 2, 2, KD])
        ident = st.sb("ident", [P, P])
        w = st.sb("w", [P, 2, KD, CHUNK])
        o = st.sb("o", [P, 2, TILES, CHUNK])
        ps = st.ps("ps", [P, TILES, CHUNK])
        pt = st.ps("pt", [P, 2, CHUNK])
        s_in, s_w, s_out = st.sem("in"), [st.sem("w0"), st.sem("w1")], [st.sem("o0"), st.sem("o1")]
        s_mt, s_mc = st.sem("mt"), st.sem("mc")
        s_t, s_h, s_mm, s_a, s_v = st.sem("t"), st.sem("h"), st.sem("mm"), st.sem("a"), st.sem("v")
        groups = [(0, 0), (1, 0), (1, 1)]
        ev = [[m for m in range(TILES) if m % 2 == k] for k in range(2)]
        with nc.Block() as block:
            @block.sync
            def _(sp):
                ld = Loads(sp, s_in)
                ld(ident[:], e.ident)
                ld(x[:], e.X.rearrange("(m p) d -> p m d", p=P))
                for g in range(2):
                    ld(mrows[2 * KD * g:2 * KD * (g + 1), :],
                       e.MOD[g, part * D:(part + 2) * D].rearrange("(k p) -> k p", p=P))

                def store(j):
                    sp.wait_ge(s_a, len(ev[0]) * (j + 1))
                    sp.wait_ge(s_v, len(ev[1]) * (j + 1))
                    cols = slice(j * CHUNK, j * CHUNK + sizes[j])
                    sp.dma_start(dst_ctx[:, cols], o[:, j % 2, 0, 0:sizes[j]]).then_inc(s_out[j % 2], 16)
                    sp.dma_start(dst_lat[:, cols].rearrange("(m p) n -> p m n", p=P),
                                 o[:, j % 2, 1:TILES, 0:sizes[j]]).then_inc(s_out[j % 2], 16)

                for j in range(n):
                    if j >= 2:
                        sp.wait_ge(s_mm, TILES * (j - 1))
                    sp.dma_start(w[:, j % 2, :, 0:sizes[j]], w_src[:, j * CHUNK:j * CHUNK + sizes[j]]
                                 .rearrange("(k p) n -> p k n", p=P)).then_inc(s_w[j % 2], 16)
                    if j >= 2:
                        store(j - 2)
                for j in range(max(0, n - 2), n):
                    store(j)
                for b in range(2):
                    sp.wait_ge(s_out[b], 32 * ((n + 1 - b) // 2))

            @block.tensor
            def _(pe):
                pe.wait_ge(s_in, 16 * 4)
                pe.transpose(ps[:, 0, 0:4 * KD], mrows[:], ident[0:4 * KD, 0:4 * KD]).then_inc(s_mt, 1)
                for i in range(2 * TILES):
                    m, half = i // 2, i % 2
                    if i >= 2:
                        pe.wait_ge(s_h, i - 1)
                    for q in range(4):
                        t = pe.transpose(pt[:, i % 2, q * P:(q + 1) * P],
                                         x[:, m, (4 * half + q) * P:(4 * half + q + 1) * P], ident[:])
                    t.then_inc(s_t, 1)
                pe.wait_ge(s_h, 2 * TILES)
                for j in range(n):
                    pe.wait_ge(s_w[j % 2], 16 * (j // 2 + 1))
                    for m in range(TILES):
                        if j >= 1:
                            pe.wait_ge((s_a, s_v)[m % 2], len(ev[m % 2]) * (j - 1) + m // 2 + 1)
                        for k in range(KD):
                            mm = pe.matmul(ps[:, m, 0:sizes[j]], hT[:, k, m * P:(m + 1) * P],
                                           w[:, j % 2, k, 0:sizes[j]], start=(k == 0), stop=(k == KD - 1))
                        mm.then_inc(s_mm, 1)

            def read_out(eng, copy, which, s):
                for j in range(n):
                    if j >= 2:
                        eng.wait_ge(s_out[j % 2], 32 * (j // 2))
                    for m in ev[which]:
                        eng.wait_ge(s_mm, TILES * j + m + 1)
                        copy(o[:, j % 2, m, 0:sizes[j]], ps[:, m, 0:sizes[j]]).then_inc(s, 1)

            @block.vector
            def _(dve):
                dve.wait_ge(s_mt, 1)
                dve.tensor_copy(mcols[:].rearrange("p g w k -> p (g w k)"), ps[:, 0, 0:4 * KD]).then_inc(s_mc, 1)
                dve.wait_ge(s_mc, 1)
                for i in range(2 * TILES):
                    m, half = i // 2, i % 2
                    g = 0 if m == 0 else 1
                    dve.wait_ge(s_t, i + 1)
                    for q in range(4):
                        k = 4 * half + q
                        ins = dve.tensor_scalar(hT[:, k, m * P:(m + 1) * P], pt[:, i % 2, q * P:(q + 1) * P],
                                                mcols[:, g, 1, k:k + 1], mcols[:, g, 0, k:k + 1], ALU.mult, ALU.add)
                    ins.then_inc(s_h, 1)
                read_out(dve, dve.tensor_copy, 1, s_v)

            @block.scalar
            def _(act):
                read_out(act, act.copy, 0, s_a)


def route_stage(nc, e, l, i):
    HP, F = 2 * HEADS, TOPK * TOPK
    LOW = -3.0e38
    with Stage(nc, "route") as st:
        q, qT, keys = st.sb("q", [P, HP, HALF]), st.sb("qT", [P, HP, P]), st.sb("keys", [P, HP, NKEYS])
        ident, base = st.sb("ident", [P, P]), st.sb("base", [P, 1])
        sc = st.sb("sc", [P, HP, NKEYS])
        left = st.sb("left", [P, NKEYS])
        sv, si = st.sb("sv", [P, HP, TOPK]), st.sb("si", [P, HP, TOPK], U32)
        cand, cleft = st.sb("cand", [P, HEADS, TOPK, TOPK]), st.sb("cleft", [P, F])
        best, pos = st.sb("best", [P, HEADS, TOPK]), st.sb("pos", [P, HEADS, TOPK], U32)
        part, partf, sif = st.sb("part", [P, 2, PICKS], U32), st.sb("partf", [P, 2, PICKS]), st.sb("sif", [P, HP, TOPK])
        iota = st.sb("iota", [P, TOPK])
        hot, ids = st.sb("hot", [P, PICKS, TOPK]), st.sb("ids", [P, 3, PICKS])
        idx = st.sb("idx", [P, PICKS], I32)
        ex, tot = st.sb("ex", [P, HEADS, TOPK]), st.sb("tot", [P, 2, HEADS])
        pt, ps = st.ps("pt", [P, 4, CHUNK]), st.ps("ps", [P, 4, CHUNK])
        s_in, s_t, s_q, s_mm, s_sc = st.sem("in"), st.sem("t"), st.sem("q"), st.sem("mm"), st.sem("sc")
        s_dve, s_best, s_exp, s_idx, s_g, s_out = (st.sem(x) for x in ("dve", "best", "exp", "idx", "g", "out"))
        with nc.Block() as block:
            @block.sync
            def _(sp):
                ld = Loads(sp, s_in)
                ld(ident[:], e.ident)
                ld(q[:].rearrange("p a b -> p (a b)"), rows(e.QH, i * P))
                ld(keys[:], e.keys_t[l])
                ld(base[:], e.layer_base[l])
                ld(iota[:], e.iota16)
                sp.wait_ge(s_idx, 1)
                out = Loads(sp, s_out)
                out(rows(e.EIDX, i * P), idx[:])
                sp.wait_ge(s_g, 1)
                out(rows(e.G, i * P), ex[:].rearrange("p h k -> p (h k)"))
                out.wait()

            @block.tensor
            def _(pe):
                pe.wait_ge(s_in, 80)
                for b in range(HP):
                    t = pe.transpose(pt[:, b // 4, (b % 4) * P:(b % 4 + 1) * P], q[:, b, :], ident[:])
                    if b % 4 == 3:
                        t.then_inc(s_t, 1)
                for b in range(HP):
                    if b % 4 == 0:
                        pe.wait_ge(s_q, b // 4 + 1)
                    mm = pe.matmul(ps[:, b // 4, (b % 4) * P:(b % 4 + 1) * P], qT[:, b, :], keys[:, b, :],
                                   start=True, stop=True)
                    if b % 4 == 3:
                        mm.then_inc(s_mm, 1)

            @block.scalar
            def _(act):
                for b in range(4):
                    act.wait_ge(s_t, b + 1)
                    act.copy(qT[:, 4 * b:4 * b + 4, :].rearrange("p a b -> p (a b)"), pt[:, b, :]).then_inc(s_q, 1)
                for b in range(4):
                    act.wait_ge(s_mm, b + 1)
                    act.copy(sc[:, 4 * b:4 * b + 4, :].rearrange("p a b -> p (a b)"), ps[:, b, :]).then_inc(s_sc, 1)
                act.wait_ge(s_best, 1)
                act.activation(ex[:], best[:], ACT.Exp).then_inc(s_exp, 1)

            @block.vector
            def _(dve):
                step = Chain(dve, s_dve)

                def top16(vals, left, v16, i16):
                    step(dve.max(v16[:, 0:8], vals))
                    step(dve.max_index(i16[:, 0:8], v16[:, 0:8], vals))
                    step(dve.match_replace(left, v16[:, 0:8], vals, LOW))
                    step(dve.max(v16[:, 8:16], left))
                    step(dve.max_index(i16[:, 8:16], v16[:, 8:16], left))

                for b in range(HP):
                    dve.wait_ge(s_sc, b // 4 + 1)
                    top16(sc[:, b, :], left[:], sv[:, b, :], si[:, b, :])
                svh = sv[:].rearrange("p (h s) k -> p h s k", s=2)
                step(dve.tensor_tensor(cand[:], svh[:, :, 0, :].unsqueeze(3).to_broadcast([P, HEADS, TOPK, TOPK]),
                                       svh[:, :, 1, :].unsqueeze(2).to_broadcast([P, HEADS, TOPK, TOPK]), ALU.add))
                for h in range(HEADS):
                    top16(cand[:, h].rearrange("p a b -> p (a b)"), cleft[:], best[:, h, :], pos[:, h, :])
                step(dve.tensor_copy(tot[:, 0, :], best[:, :, 0]))
                dve.tensor_tensor(best[:], best[:], tot[:, 0, :].unsqueeze(2).to_broadcast([P, HEADS, TOPK]),
                                  ALU.subtract).then_inc(s_best, 1)
                posf = pos[:].rearrange("p h k -> p (h k)")
                step(dve.tensor_single_scalar(part[:, 0, :], posf, 4, ALU.logical_shift_right))
                step(dve.tensor_single_scalar(part[:, 1, :], posf, 15, ALU.bitwise_and))
                step(dve.tensor_copy(partf[:], part[:]))
                step(dve.tensor_copy(sif[:], si[:]))
                sih = sif[:].rearrange("p (h s) k -> p h s k", s=2)
                for s in range(2):
                    step(dve.tensor_tensor(hot[:], partf[:, s, :].unsqueeze(2).to_broadcast([P, PICKS, TOPK]),
                                           iota[:].unsqueeze(1).to_broadcast([P, PICKS, TOPK]), ALU.is_equal))
                    hv = hot[:].rearrange("p (h k) c -> p h k c", h=HEADS)
                    step(dve.tensor_tensor(hv, hv, sih[:, :, s, :].unsqueeze(2)
                                           .to_broadcast([P, HEADS, TOPK, TOPK]), ALU.mult))
                    step(dve.tensor_reduce(ids[:, s, :], hot[:], AX.X, ALU.add))
                step(dve.tensor_scalar(ids[:, 2, :], ids[:, 0, :], float(NKEYS), base[:, 0:1], ALU.mult, ALU.add))
                dve.tensor_tensor(idx[:], ids[:, 2, :], ids[:, 1, :], ALU.add).then_inc(s_idx, 1)
                dve.wait_ge(s_exp, 1)
                step(dve.tensor_reduce(tot[:, 0, :], ex[:], AX.X, ALU.add))
                step(dve.reciprocal(tot[:, 1, :], tot[:, 0, :]))
                dve.tensor_tensor(ex[:], ex[:], tot[:, 1, :].unsqueeze(2).to_broadcast([P, HEADS, TOPK]),
                                  ALU.mult).then_inc(s_g, 1)


def norm_steps(dve, step, s_var, s_std, t, stats, mv, gamma, beta, base=0):
    for c in range(2):
        step(dve.bn_stats(stats[:, c, :], t[:, c * CHUNK:(c + 1) * CHUNK]))
    step(dve.bn_aggr(mv[:, 0:2], stats[:].rearrange("p c s -> p (c s)")))
    dve.tensor_scalar(mv[:, 2:3], mv[:, 1:2], LN_EPS, None, ALU.add).then_inc(s_var, 1)
    dve.wait_ge(s_std, base + 1)
    step(dve.reciprocal(mv[:, 4:5], mv[:, 3:4]))
    step(dve.tensor_scalar(t[:], t[:], mv[:, 0:1], mv[:, 4:5], ALU.subtract, ALU.mult))
    step(dve.tensor_tensor(t[:], t[:], gamma[:], ALU.mult))
    return dve.tensor_tensor(t[:], t[:], beta[:], ALU.add)


SLOTS = 16


def expert_stage(nc, e, l, i, s_rows):
    per_tile = 2 * PICKS // SLOTS
    turn = l * TILES + i
    with Stage(nc, "expert") as st:
        x, h, junk, acc = (st.sb(n, [P, D]) for n in ("x", "h", "junk", "acc"))
        shift, scale, gate, gamma, beta = (st.sb(n, [P, D]) for n in ("shift", "scale", "gate", "gamma", "beta"))
        row = st.sb("row", [P, SLOTS, D])
        idx, g = st.sb("idx", [P, PICKS], I32), st.sb("g", [P, PICKS])
        hid, cub, th, wt = (st.sb(n, [P, PICKS]) for n in ("hid", "cub", "th", "wt"))
        stats, mv = st.sb("stats", [P, 2, 6]), st.sb("mv", [P, 5])
        s_idx, s_in, s_used, s_dve, s_cub, s_tanh, s_var, s_std, s_x, s_out = (
            st.sem(n) for n in ("idx", "in", "used", "dve", "cub", "tanh", "var", "std", "x", "out"))
        with nc.Block() as block:
            @block.sync
            def _(sp):
                sp.dma_start(idx[:], rows(e.EIDX, i * P)).then_inc(s_idx, 16)
                ld = Loads(sp, s_in)
                ld(x[:], rows(e.X, i * P))
                for buf, part in ((shift, 3), (scale, 4), (gate, 5)):
                    ld(buf[:], e.MOD[i, part * D:(part + 1) * D].partition_broadcast(P))
                ld(gamma[:], e.ln2_g[l].partition_broadcast(P))
                ld(beta[:], e.ln2_b[l].partition_broadcast(P))
                ld(g[:], rows(e.G, i * P))
                sp.wait_ge(s_x, 1)
                sp.dma_start(rows(e.X, i * P), acc[:]).then_inc(s_out, 16)
                sp.wait_ge(s_out, 16)

            @block.gpsimd
            def _(pool):
                pool.wait_ge(s_idx, 16)
                for n in range(2 * PICKS):
                    if n >= SLOTS:
                        pool.wait_ge(s_used, n - SLOTS + 1)
                    k = n % PICKS
                    pool.indirect_dma_start(
                        out=row[:, n % SLOTS, :], out_offset=None, in_=e.peer_u if n < PICKS else e.peer_v,
                        in_offset=bass.IndirectOffsetOnAxis(ap=idx[:, k:k + 1], axis=0),
                    ).then_inc(s_rows[n % SLOTS], 16)

            @block.scalar
            def _(act):
                act.wait_ge(s_cub, 1)
                act.activation(th[:], cub[:], ACT.Tanh, scale=0.7978845608028654).then_inc(s_tanh, 1)
                act.wait_ge(s_var, 1)
                act.activation(mv[:, 3:4], mv[:, 2:3], ACT.Sqrt).then_inc(s_std, 1)

            @block.vector
            def _(dve):
                step = Chain(dve, s_dve)
                dve.wait_ge(s_in, 16 * 7)
                step(dve.tensor_tensor(h[:], x[:], scale[:], ALU.mult))
                step(dve.tensor_tensor(h[:], h[:], shift[:], ALU.add))

                def arrived(n):
                    dve.wait_ge(s_rows[n % SLOTS], turn * (16 * per_tile) + 16 * (n // SLOTS + 1))

                for n in range(PICKS):
                    arrived(n)
                    if n:
                        dve.wait_ge(s_used, n)
                    dve.tensor_tensor_reduce(junk[:], row[:, n % SLOTS, :], h[:], 1.0, 0.0, ALU.mult, ALU.add,
                                             hid[:, n:n + 1]).then_inc(s_used, 1)
                dve.wait_ge(s_used, PICKS)
                step(dve.tensor_tensor(cub[:], hid[:], hid[:], ALU.mult))
                step(dve.tensor_scalar(cub[:], cub[:], 0.044715, 1.0, ALU.mult, ALU.add))
                dve.tensor_tensor(cub[:], cub[:], hid[:], ALU.mult).then_inc(s_cub, 1)
                step(dve.tensor_tensor(wt[:], hid[:], g[:], ALU.mult))
                dve.wait_ge(s_tanh, 1)
                step(dve.tensor_scalar(th[:], th[:], 0.5, 0.5, ALU.mult, ALU.add))
                step(dve.tensor_tensor(wt[:], wt[:], th[:], ALU.mult))
                for n in range(PICKS, 2 * PICKS):
                    arrived(n)
                    k = n - PICKS
                    if k == 0:
                        ins = dve.tensor_scalar(acc[:], row[:, n % SLOTS, :], wt[:, 0:1], None, ALU.mult)
                    else:
                        dve.wait_ge(s_used, n)
                        ins = dve.scalar_tensor_tensor(out=acc[:], in0=row[:, n % SLOTS, :], scalar=wt[:, k:k + 1],
                                                       in1=acc[:], op0=ALU.mult, op1=ALU.add)
                    ins.then_inc(s_used, 1)
                dve.wait_ge(s_used, 2 * PICKS)
                step(dve.tensor_tensor(acc[:], acc[:], gate[:], ALU.mult))
                step(dve.scalar_tensor_tensor(out=acc[:], in0=x[:], scalar=ALPHA, in1=acc[:], op0=ALU.mult,
                                              op1=ALU.add))
                norm_steps(dve, step, s_var, s_std, acc, stats, mv, gamma, beta).then_inc(s_x, 1)


def merge_stage(nc, e, l):
    CB = BRANCH_W // P
    turns = [("A", 0)]
    for m in range(TILES):
        turns += ([("A", m + 1)] if m + 1 < TILES else []) + [("B", m)]
    with Stage(nc, "merge") as st:
        ident = st.sb("ident", [P, P])
        wb, wo = st.sb("wb", [P, N_BRANCH * CB, D]), st.sb("wo", [P, KD, D])
        y, yT = st.sb("y", [P, 2, N_BRANCH * BRANCH_W]), st.sb("yT", [P, N_BRANCH * CB, P])
        gates, mix, mixT = st.sb("gates", [P, N_BRANCH * D]), st.sb("mix", [P, 2, D]), st.sb("mixT", [P, KD, P])
        tmp, t, x = st.sb("tmp", [P, CHUNK]), st.sb("t", [P, D]), st.sb("x", [P, D])
        gate, gamma, beta = st.sb("gate", [P, D]), st.sb("gamma", [P, D]), st.sb("beta", [P, D])
        stats, mv = st.sb("stats", [P, 2, 6]), st.sb("mv", [P, 5])
        pt, ps = st.ps("pt", [P, 2, CHUNK]), st.ps("ps", [P, 4, CHUNK])
        s_id, s_y = st.sem("id"), [st.sem("y0"), st.sem("y1")]
        s_w, s_wo, s_g, s_x, s_out = (st.sem(n) for n in ("w", "wo", "g", "x", "out"))
        s_t, s_tc, s_mm, s_used, s_sig, s_mix = (st.sem(n) for n in ("t", "tc", "mm", "used", "sig", "mix"))
        s_dve, s_var, s_std, s_new, s_a, s_bm = (st.sem(n) for n in ("dve", "var", "std", "new", "a", "bm"))
        with nc.Block() as block:
            @block.sync
            def _(sp):
                sp.dma_start(ident[:], e.ident).then_inc(s_id, 16)

                def load_tile(m):
                    if m >= 2:
                        sp.wait_ge(s_a, m - 1)
                    sp.dma_start(y[:, m % 2], e.Y[m * P:(m + 1) * P, :]).then_inc(s_y[m % 2], 16)
                    if m >= 1:
                        sp.wait_ge(s_mix, m)
                    r = ROW_CTX if m == 0 else ROW_LAT + (m - 1) * P
                    sp.dma_start(gates[:], e.PR[r:r + P, COL['merge']:COL['merge'] + N_BRANCH * D]).then_inc(s_g, 16)

                load_tile(0)
                for b in range(N_BRANCH):
                    sp.dma_start(wb[:, b * CB:(b + 1) * CB, :],
                                 e.w_branch[l, b].rearrange("(c p) d -> p c d", p=P)).then_inc(s_w, 16)
                sp.dma_start(wo[:], e.w_out[l].rearrange("(k p) d -> p k d", p=P)).then_inc(s_wo, 16)
                sp.dma_start(gamma[:], e.ln1_g[l].partition_broadcast(P)).then_inc(s_wo, 16)
                sp.dma_start(beta[:], e.ln1_b[l].partition_broadcast(P)).then_inc(s_wo, 16)
                for kind, m in turns:
                    if kind == "A":
                        if m:
                            load_tile(m)
                        continue
                    if m:
                        sp.wait_ge(s_new, m)
                    sp.dma_start(x[:], e.X[m * P:(m + 1) * P, :]).then_inc(s_x, 16)
                    sp.dma_start(gate[:], e.MOD[m, 2 * D:3 * D].partition_broadcast(P)).then_inc(s_x, 16)
                    if m:
                        sp.dma_start(e.X[(m - 1) * P:m * P, :], t[:]).then_inc(s_out, 16)
                sp.wait_ge(s_new, TILES)
                sp.dma_start(e.X[(TILES - 1) * P:, :], t[:]).then_inc(s_out, 16)
                sp.wait_ge(s_out, 16 * TILES)

            @block.tensor
            def _(pe):
                n_t, n_mm = 0, 0
                for kind, m in turns:
                    n_groups = N_BRANCH * CB // 4 if kind == "A" else KD // 4
                    if kind == "A":
                        pe.wait_ge(s_id, 16)
                        pe.wait_ge(s_y[m % 2], 16 * (m // 2 + 1))
                    else:
                        pe.wait_ge(s_mix, m + 1)
                    for q in range(n_groups):
                        if n_t >= 2:
                            pe.wait_ge(s_tc, n_t - 1)
                        src = y[:, m % 2] if kind == "A" else mix[:, m % 2]
                        for c in range(4):
                            tr = pe.transpose(pt[:, n_t % 2, c * P:(c + 1) * P],
                                              src[:, (4 * q + c) * P:(4 * q + c + 1) * P], ident[:])
                        n_t += 1
                        tr.then_inc(s_t, 1)
                    if kind == "A":
                        pe.wait_ge(s_t, n_t)
                        pe.sem_inc(s_a, 1)
                    pe.wait_ge(s_tc, n_t)
                    if kind == "B":
                        pe.wait_ge(s_wo, 48)
                    for b in range(N_BRANCH if kind == "A" else 1):
                        if kind == "A" and m == 0:
                            pe.wait_ge(s_w, 16 * N_BRANCH)
                        for half in range(2):
                            if n_mm >= 4:
                                pe.wait_ge(s_used, n_mm - 3)
                            cols = slice(half * CHUNK, (half + 1) * CHUNK)
                            depth = CB if kind == "A" else KD
                            for c in range(depth):
                                lhs = yT[:, b * CB + c, :] if kind == "A" else mixT[:, c, :]
                                rhs = wb[:, b * CB + c, cols] if kind == "A" else wo[:, c, cols]
                                mm = pe.matmul(ps[:, n_mm % 4, :], lhs, rhs, start=(c == 0), stop=(c == depth - 1))
                            n_mm += 1
                            mm.then_inc(s_mm, 1)

            @block.scalar
            def _(act):
                n_t, n_mm = 0, 0
                for kind, m in turns:
                    n_groups = N_BRANCH * CB // 4 if kind == "A" else KD // 4
                    if kind == "A":
                        act.wait_ge(s_g, 16 * (m + 1))
                        act.activation(gates[:], gates[:], ACT.Sigmoid).then_inc(s_sig, 1)
                    act.wait_ge(s_mm, n_mm)
                    for q in range(n_groups):
                        act.wait_ge(s_t, n_t + 1)
                        dst = yT if kind == "A" else mixT
                        act.copy(dst[:, 4 * q:4 * q + 4, :].rearrange("p a b -> p (a b)"),
                                 pt[:, n_t % 2, :]).then_inc(s_tc, 1)
                        n_t += 1
                    n_mm += 2 * N_BRANCH if kind == "A" else 2
                    if kind == "B":
                        act.wait_ge(s_var, m + 1)
                        act.activation(mv[:, 3:4], mv[:, 2:3], ACT.Sqrt).then_inc(s_std, 1)

            @block.vector
            def _(dve):
                step = Chain(dve, s_dve)
                n_mm = 0
                for kind, m in turns:
                    if kind == "A":
                        dve.wait_ge(s_sig, m + 1)
                        for b in range(N_BRANCH):
                            for half in range(2):
                                cols = slice(half * CHUNK, (half + 1) * CHUNK)
                                gcols = slice(b * D + half * CHUNK, b * D + (half + 1) * CHUNK)
                                dve.wait_ge(s_mm, n_mm + 1)
                                dst = mix[:, m % 2, cols] if b == 0 else tmp[:]
                                dve.tensor_tensor(dst, ps[:, n_mm % 4, :], gates[:, gcols], ALU.mult)\
                                   .then_inc(s_used, 1)
                                n_mm += 1
                                dve.wait_ge(s_used, n_mm)
                                if b:
                                    step(dve.tensor_tensor(mix[:, m % 2, cols], mix[:, m % 2, cols], tmp[:],
                                                           ALU.add))
                        dve.sem_inc(s_mix, 1)
                        continue
                    dve.wait_ge(s_x, 32 * (m + 1))
                    dve.wait_ge(s_wo, 48)
                    if m:
                        dve.wait_ge(s_out, 16 * m)
                    for half in range(2):
                        cols = slice(half * CHUNK, (half + 1) * CHUNK)
                        dve.wait_ge(s_mm, n_mm + 1)
                        dve.tensor_tensor(t[:, cols], ps[:, n_mm % 4, :], gate[:, cols], ALU.mult).then_inc(s_used, 1)
                        n_mm += 1
                    dve.wait_ge(s_used, n_mm)
                    step(dve.scalar_tensor_tensor(out=t[:], in0=x[:], scalar=ALPHA, in1=t[:], op0=ALU.mult,
                                                  op1=ALU.add))
                    norm_steps(dve, step, s_var, s_std, t, stats, mv, gamma, beta, base=m).then_inc(s_new, 1)


def attention_stage(nc, e, l):
    B, RB = 4, 15
    units = [(m, h) for m in range(1, TILES) for h in range(NA_H)] + [(0, h) for h in range(NA_H)]
    groups = [(kind, m) for m in range(TILES) for kind in "qk"] + [("k", TILES)]
    KEYS = LAT + P + CTX
    NT = GRID_W // 4
    key_at = lambda m: (m - 1) * P if 1 <= m <= LAT_TILES else (LAT + P if m == 0 else LAT)
    q_at = lambda m: m * P
    with Stage(nc, "na") as st:
        ident = st.sb("ident", [P, P])
        x, kc = st.sb("x", [P, TILES, 3 * 512]), st.sb("kc", [P, 512])
        vc = st.sb("vc", [P, 512])
        qT, kT = st.sb("qT", [P, B, TILES * P]), st.sb("kT", [P, B, KEYS])
        rpb, shift = st.sb("rpb", [32, NA_H * RB]), st.sb("shift", [32, GRID_W * P])
        bias = st.sb("bias", [P, NA_H, RB + 1, GRID_W])
        s, pT = st.sb("s", [P, 2, 640]), st.sb("pT", [P, 2, 640])
        nmax, tot = st.sb("nmax", [P, 40]), st.sb("tot", [P, 2, 40])
        y = st.sb("y", [P, TILES, 512])
        ps, pt, po = st.ps("ps", [P, 2, 2, CHUNK]), st.ps("pt", [P, 2, CHUNK]), st.ps("po", [P, 2, CHUNK])
        s_one, s_b, s_x, s_kc, s_out = (st.sem(n) for n in ("one", "b", "x", "kc", "out"))
        s_bias, s_blo, s_bhi, s_t, s_tc = (st.sem(n) for n in ("bias", "blo", "bhi", "t", "tc"))
        s_s, s_add, s_ctx, s_max, s_exp, s_rec, s_p, s_pc, s_pv, s_y = (
            st.sem(n) for n in ("s", "add", "ctx", "max", "exp", "rec", "p", "pc", "pv", "y"))
        with nc.Block() as block:
            @block.sync
            def _(sp):
                sp.wait_ge(s_one, 1)
                b = Loads(sp, s_b)
                b(ident[:], e.ident)
                b(rpb[1:32, :], e.rpb_t[l])
                b(shift[:], e.key_shift)
                ld = Loads(sp, s_x)
                cols = slice(COL['na_q'], COL['na_q'] + 1536)
                ld(x[:, 0, :], e.PR[ROW_CTX:ROW_CTX + CTX, cols])
                ld(x[:, 1:, :], e.PR[ROW_LAT:ROW_LAT + LAT, cols].rearrange("(m p) n -> p m n", p=P))
                kc_ld = Loads(sp, s_kc)
                kc_ld(kc[:].rearrange("p (h d) -> p h d", h=NA_H), e.cache_k[l].rearrange("h j d -> j h d"))
                kc_ld(vc[:].rearrange("p (h d) -> p h d", h=NA_H), e.cache_v[l].rearrange("h j d -> j h d"))
                out = Loads(sp, s_out)
                for k, dst in ((1, e.new_k), (2, e.new_v)):
                    c0 = COL['na_q'] + 512 * k
                    out(dst[l].rearrange("h j d -> j h d"),
                        e.PR[ROW_CTX:ROW_CTX + CTX, c0:c0 + 512].rearrange("j (h d) -> j h d", h=NA_H))
                for n, m in enumerate(list(range(1, TILES)) + [0]):
                    sp.wait_ge(s_y, NA_H * (n + 1))
                    out(e.Y[m * P:(m + 1) * P, 512:1024], y[:, m, :])
                out.wait()

            @block.tensor
            def _(pe):
                pe.wait_ge(s_b, 48)
                for n in range(NT):
                    if n >= 2:
                        pe.wait_ge(s_blo, n - 1)
                        pe.wait_ge(s_bhi, n - 1)
                    for c in range(4):
                        ck = 4 * n + c
                        mm = pe.matmul(po[:, n % 2, c * 120:(c + 1) * 120], shift[:, ck * P:(ck + 1) * P], rpb[:],
                                       start=True, stop=True)
                    mm.then_inc(s_bias, 1)
                pe.wait_ge(s_x, 32)
                pe.wait_ge(s_kc, 32)
                for n, (kind, m) in enumerate(groups):
                    if n >= 2:
                        pe.wait_ge(s_tc, n - 1)
                    for c in range(B):
                        src = kc[:, c * P:(c + 1) * P] if m == TILES else \
                            x[:, m, (0 if kind == "q" else 512) + c * P:][:, 0:P]
                        tr = pe.transpose(pt[:, n % 2, c * P:(c + 1) * P], src, ident[:])
                    tr.then_inc(s_t, 1)
                pe.wait_ge(s_tc, len(groups))

                def scores(u):
                    m, h = units[u]
                    r = slice(64 * (h % 2), 64 * (h % 2) + 64)
                    if u >= 2:
                        pe.wait_ge(s_add, u - 1)
                        pe.wait_ge(s_ctx, u - 1)
                    q = qT[r, h // 2, q_at(m):q_at(m) + P]
                    if m:
                        pe.matmul(ps[:, u % 2, 0, :], q, kT[r, h // 2, 0:LAT], start=True, stop=True)
                    k0 = LAT if m else LAT + P
                    pe.matmul(ps[:, u % 2, 1, 0:P], q, kT[r, h // 2, k0:k0 + P], start=True, stop=True)\
                      .then_inc(s_s, 1)

                def values(u):
                    m, h = units[u]
                    blocks = range(5) if m else [4]
                    pe.wait_ge(s_exp, u + 1)
                    if u >= 1:
                        pe.wait_ge(s_pc, u)
                    for b in blocks:
                        tr = pe.transpose(pt[:, b // 4, (b % 4) * P:(b % 4 + 1) * P], s[:, u % 2, b * P:(b + 1) * P],
                                          ident[:])
                    tr.then_inc(s_p, 1)
                    pe.wait_ge(s_pc, u + 1)
                    if u >= 2:
                        pe.wait_ge(s_y, u - 1)
                    for b in blocks:
                        v = x[:, b + 1, 1024 + h * NA_D:1024 + (h + 1) * NA_D] if b < 4 else \
                            (vc[:, h * NA_D:(h + 1) * NA_D] if m else x[:, 0, 1024 + h * NA_D:1024 + (h + 1) * NA_D])
                        mm = pe.matmul(po[:, u % 2, 0:NA_D], pT[:, u % 2, b * P:(b + 1) * P], v,
                                       start=(b == blocks[0]), stop=(b == 4))
                    mm.then_inc(s_pv, 1)

                for u in range(len(units) + 1):
                    if u < len(units):
                        scores(u)
                    if u:
                        values(u - 1)

            def keep_bias(eng, copy, half, s_done):
                r = slice(64 * half, 64 * half + 64)
                for n in range(NT):
                    eng.wait_ge(s_bias, n + 1)
                    copy(bias[r, :, half:half + RB, 4 * n:4 * n + 4],
                         po[r, n % 2, 0:480].rearrange("p (c h r) -> p h r c", c=4, h=NA_H)).then_inc(s_done, 1)

            @block.scalar
            def _(act):
                keep_bias(act, act.copy, 0, s_blo)
                for n, (kind, m) in enumerate(groups):
                    act.wait_ge(s_t, n + 1)
                    if kind == "q":
                        ins = act.mul(qT[:, :, q_at(m):q_at(m) + P],
                                      pt[:, n % 2, :].rearrange("p (c t) -> p c t", c=B), float(NA_D) ** -0.5)
                    else:
                        ins = act.copy(kT[:, :, key_at(m):key_at(m) + P],
                                       pt[:, n % 2, :].rearrange("p (c t) -> p c t", c=B))
                    ins.then_inc(s_tc, 1)

                def copy_scores(u):
                    act.wait_ge(s_s, u + 1)
                    if u >= 2:
                        act.wait_ge(s_p, u - 1)
                    act.copy(s[:, u % 2, 512:640], ps[:, u % 2, 1, 0:P]).then_inc(s_ctx, 1)

                def exponent(u):
                    part = slice(0, 640) if units[u][0] else slice(512, 640)
                    act.wait_ge(s_max, u + 1)
                    act.activation(s[:, u % 2, part], s[:, u % 2, part], ACT.Exp, bias=nmax[:, u:u + 1],
                                   accum_out=tot[:, 0, u:u + 1]).then_inc(s_exp, 1)

                def copy_probs(u):
                    m, h = units[u]
                    act.wait_ge(s_p, u + 1)
                    if u >= 2:
                        act.wait_ge(s_pv, u - 1)
                    part = slice(0, 640) if m else slice(512, 640)
                    act.copy(pT[:, u % 2, part], pt[:].rearrange("p a b -> p (a b)")[:, part]).then_inc(s_pc, 1)

                copy_scores(0)
                for u in range(len(units)):
                    exponent(u)
                    if u + 1 < len(units):
                        copy_scores(u + 1)
                    copy_probs(u)

            @block.vector
            def _(dve):
                dve.memset(rpb[:], 1.0).then_inc(s_one, 1)
                keep_bias(dve, dve.tensor_copy, 1, s_bhi)
                dve.wait_ge(s_bhi, NT)
                dve.wait_ge(s_blo, NT)

                def out_rows(u):
                    m, h = units[u]
                    dve.wait_ge(s_rec, u + 1)
                    dve.wait_ge(s_pv, u + 1)
                    dve.tensor_scalar(y[:, m, h * NA_D:(h + 1) * NA_D], po[:, u % 2, 0:NA_D], tot[:, 1, u:u + 1],
                                      None, ALU.mult).then_inc(s_y, 1)

                for u, (m, h) in enumerate(units):
                    dve.wait_ge(s_s, u + 1)
                    if u >= 2:
                        dve.wait_ge(s_p, u - 1)
                    if m:
                        d0 = 7 - 2 * (m - 1)
                        dve.tensor_tensor(s[:, u % 2, 0:512], ps[:, u % 2, 0, :],
                                          bias[:, h, d0:d0 + 8, :].rearrange("p r c -> p (r c)"), ALU.add)\
                           .then_inc(s_add, 1)
                    else:
                        dve.sem_inc(s_add, 1)
                    dve.wait_ge(s_add, u + 1)
                    dve.wait_ge(s_ctx, u + 1)
                    part = slice(0, 640) if m else slice(512, 640)
                    dve.tensor_reduce(nmax[:, u:u + 1], s[:, u % 2, part], AX.X, ALU.max, negate=True)\
                       .then_inc(s_max, 1)
                    dve.wait_ge(s_exp, u + 1)
                    dve.reciprocal(tot[:, 1, u:u + 1], tot[:, 0, u:u + 1]).then_inc(s_rec, 1)
                    if u:
                        out_rows(u - 1)
                out_rows(len(units) - 1)


def wide(ap):
    return ap.unsqueeze(2).to_broadcast([P, 8, P])


def heads(ap):
    return ap.rearrange("p b (h t) -> p (b h) t", h=4)


def per_dir(ap):
    return ap.unsqueeze(2).to_broadcast([P, 2, 4, P])


def four(ap):
    return ap.rearrange("p (d h) t -> p d h t", d=2)


def gdn_prepare(nc, e, l, row, tile):
    W, QK = 1536, 1024
    with Stage(nc, "gprep") as st:
        xs, cw = st.sb("xs", [P, 3, W]), st.sb("cw", [P, 3, W])
        ab, rate, dtb = st.sb("ab", [P, 16]), st.sb("rate", [P, 8]), st.sb("dtb", [P, 8])
        rope = st.sb("rope", [P, 2, 64])
        sig, sq, ss = st.sb("sig", [P, W]), st.sb("sq", [P, QK]), st.sb("ss", [P, 4, 8])
        rot, tmp = st.sb("rot", [P, 16, 2, 32]), st.sb("tmp", [P, 16, 32])
        res, sm = st.sb("res", [P, W + 16]), st.sb("sm", [P, 4, 8])
        s_in, s_out, s_dve = st.sem("in"), st.sem("out"), st.sem("dve")
        s_c2, s_conv, s_sig, s_ss, s_root, s_t, s_e, s_ln, s_done = (
            st.sem(n) for n in ("c2", "conv", "sig", "ss", "root", "t", "e", "ln", "done"))
        with nc.Block() as block:
            @block.sync
            def _(sp):
                ld = Loads(sp, s_in)
                for j in range(3):
                    ld(xs[:, j, :], e.PR[bass.ds(row - 1 + j, P), 0:W])
                ld(cw[:].rearrange("p j w -> p (j w)"),
                   e.gdn_conv[l].rearrange("j w -> (j w)").partition_broadcast(P))
                ld(ab[:], e.PR[bass.ds(row, P), COL['gdn_a']:COL['gdn_a'] + 16])
                ld(rate[:], e.gdn_A_log[l].partition_broadcast(P))
                ld(dtb[:], e.gdn_dt_bias[l].partition_broadcast(P))
                ld(rope[:].rearrange("p a b -> p (a b)"), rows(e.rope, tile * P))
                sp.wait_ge(s_done, 1)
                sp.dma_start(rows(e.GQ, tile * P), res[:]).then_inc(s_out, 16)
                sp.wait_ge(s_out, 16)

            @block.gpsimd
            def _(pool):
                pool.wait_ge(s_in, 128)
                pool.tensor_tensor(xs[:, 2, :], xs[:, 2, :], cw[:, 2, :], ALU.mult).then_inc(s_c2, 1)

            @block.scalar
            def _(act):
                act.wait_ge(s_in, 128)
                act.activation(rate[:], rate[:], ACT.Exp).then_inc(s_e, 1)
                act.wait_ge(s_t, 1)
                act.activation(sm[:, 2, :], sm[:, 2, :], ACT.Exp).then_inc(s_e, 1)
                act.wait_ge(s_e, 2)
                act.activation(sm[:, 3, :], sm[:, 2, :], ACT.Ln, bias=1.0).then_inc(s_ln, 1)
                act.activation(res[:, W + 8:W + 16], ab[:, 8:16], ACT.Sigmoid).then_inc(s_e, 1)
                act.wait_ge(s_conv, 1)
                act.activation(sig[:], xs[:, 0, :], ACT.Sigmoid).then_inc(s_sig, 1)
                act.wait_ge(s_ss, 1)
                act.activation(ss[:, 2, :], ss[:, 1, :], ACT.Sqrt).then_inc(s_root, 1)

            @block.vector
            def _(dve):
                step = Chain(dve, s_dve)
                dve.wait_ge(s_in, 128)
                step(dve.tensor_tensor(sm[:, 0, :], ab[:, 0:8], dtb[:], ALU.add))
                step(dve.tensor_scalar(sm[:, 1, :], sm[:, 0, :], 0.0, None, ALU.max))
                dve.scalar_tensor_tensor(out=sm[:, 2, :], in0=sm[:, 1, :], scalar=-2.0, in1=sm[:, 0, :],
                                         op0=ALU.mult, op1=ALU.add).then_inc(s_t, 1)
                step(dve.tensor_tensor(xs[:, 0, :], xs[:, 0, :], cw[:, 0, :], ALU.mult))
                step(dve.tensor_tensor(xs[:, 1, :], xs[:, 1, :], cw[:, 1, :], ALU.mult))
                step(dve.tensor_tensor(xs[:, 0, :], xs[:, 0, :], xs[:, 1, :], ALU.add))
                dve.wait_ge(s_c2, 1)
                dve.tensor_tensor(xs[:, 0, :], xs[:, 0, :], xs[:, 2, :], ALU.add).then_inc(s_conv, 1)
                dve.wait_ge(s_ln, 1)
                step(dve.tensor_tensor(sm[:, 1, :], sm[:, 1, :], sm[:, 3, :], ALU.add))
                dve.wait_ge(s_e, 3)
                step(dve.scalar_tensor_tensor(out=res[:, W:W + 8], in0=sm[:, 1, :], scalar=-1.0, in1=rate[:],
                                              op0=ALU.mult, op1=ALU.mult))
                dve.wait_ge(s_sig, 1)
                step(dve.tensor_tensor(xs[:, 0, 0:QK], xs[:, 0, 0:QK], sig[:, 0:QK], ALU.mult))
                step(dve.tensor_tensor(res[:, QK:W], xs[:, 0, QK:W], sig[:, QK:W], ALU.mult))
                step(dve.tensor_tensor(sq[:], xs[:, 0, 0:QK], xs[:, 0, 0:QK], ALU.mult))
                step(dve.tensor_reduce(ss[:, 0, :], sq[:].rearrange("p (h d) -> p h d", h=8), AX.X, ALU.add))
                dve.tensor_scalar(ss[:, 1, :], ss[:, 0, :], NORM_EPS, None, ALU.add).then_inc(s_ss, 1)
                xv = xs[:, 0, 0:QK].rearrange("p (g s c) -> p g s c", g=16, s=2)
                x1, x2 = xv[:, :, 0, :], xv[:, :, 1, :]

                def table(k):
                    t = rope[:, k, :].rearrange("p (a c) -> p a c", a=2).unsqueeze(1)
                    return t.to_broadcast([P, 8, 2, 32])
                ax = lambda t: t.rearrange("p (h a) c -> p h a c", a=2)
                cos, sin = table(0), table(1)
                step(dve.tensor_tensor(ax(rot[:, :, 0, :]), ax(x1), cos, ALU.mult))
                step(dve.tensor_tensor(ax(tmp[:]), ax(x2), sin, ALU.mult))
                step(dve.tensor_tensor(rot[:, :, 0, :], rot[:, :, 0, :], tmp[:], ALU.subtract))
                step(dve.tensor_tensor(ax(rot[:, :, 1, :]), ax(x1), sin, ALU.mult))
                step(dve.tensor_tensor(ax(tmp[:]), ax(x2), cos, ALU.mult))
                step(dve.tensor_tensor(rot[:, :, 1, :], rot[:, :, 1, :], tmp[:], ALU.add))
                dve.wait_ge(s_root, 1)
                step(dve.reciprocal(ss[:, 3, :], ss[:, 2, :]))
                step(dve.tensor_scalar(ss[:, 3, 0:4], ss[:, 3, 0:4], float(P) ** -0.5, None, ALU.mult))
                dve.tensor_tensor(res[:, 0:QK].rearrange("p (h d) -> p h d", h=8),
                                  rot[:].rearrange("p g s c -> p (g s c)").rearrange("p (h d) -> p h d", h=8),
                                  wide(ss[:, 3, :]), ALU.mult).then_inc(s_done, 1)


def gated_norm_stage(nc, e, l, row, tile, src, gate_col, weight, dst_col):
    with Stage(nc, "gnorm") as st:
        o, z, w = st.sb("o", [P, 2, 512]), st.sb("z", [P, 512]), st.sb("w", [P, P])
        sig, sq, ss = st.sb("sig", [P, 512]), st.sb("sq", [P, 512]), st.sb("ss", [P, 4, 4])
        s_in, s_out, s_dve, s_sig, s_ss, s_root, s_done = (
            st.sem(n) for n in ("in", "out", "dve", "sig", "ss", "root", "done"))
        with nc.Block() as block:
            @block.sync
            def _(sp):
                ld = Loads(sp, s_in)
                for d in range(2):
                    ld(o[:, d, :], src[d, bass.ds(tile * P, P), :])
                ld(z[:], e.PR[bass.ds(row, P), gate_col:gate_col + 512])
                ld(w[:], weight.partition_broadcast(P))
                sp.wait_ge(s_done, 1)
                sp.dma_start(e.Y[bass.ds(tile * P, P), dst_col:dst_col + 512], sq[:]).then_inc(s_out, 16)
                sp.wait_ge(s_out, 16)

            @block.scalar
            def _(act):
                act.wait_ge(s_in, 64)
                act.activation(sig[:], z[:], ACT.Sigmoid).then_inc(s_sig, 1)
                act.wait_ge(s_ss, 1)
                act.activation(ss[:, 2, :], ss[:, 1, :], ACT.Sqrt).then_inc(s_root, 1)

            @block.vector
            def _(dve):
                step = Chain(dve, s_dve)
                dve.wait_ge(s_in, 64)
                step(dve.tensor_tensor(o[:, 0, :], o[:, 0, :], o[:, 1, :], ALU.add))
                step(dve.tensor_tensor(sq[:], o[:, 0, :], o[:, 0, :], ALU.mult))
                hv = lambda t: t.rearrange("p (h d) -> p h d", h=4)
                step(dve.tensor_reduce(ss[:, 0, :], hv(sq[:]), AX.X, ALU.add))
                dve.tensor_scalar(ss[:, 1, :], ss[:, 0, :], 1.0 / P, NORM_EPS, ALU.mult, ALU.add).then_inc(s_ss, 1)
                dve.wait_ge(s_sig, 1)
                step(dve.tensor_tensor(sig[:], sig[:], z[:], ALU.mult))
                step(dve.tensor_tensor(hv(sig[:]), hv(sig[:]), w[:].unsqueeze(1).to_broadcast([P, 4, P]), ALU.mult))
                dve.wait_ge(s_root, 1)
                step(dve.reciprocal(ss[:, 3, :], ss[:, 2, :]))
                step(dve.tensor_tensor(hv(o[:, 0, :]), hv(o[:, 0, :]),
                                       ss[:, 3, :].unsqueeze(2).to_broadcast([P, 4, P]), ALU.mult))
                dve.tensor_tensor(sq[:], o[:, 0, :], sig[:], ALU.mult).then_inc(s_done, 1)


def copy_stage(nc, pairs):
    with Stage(nc, "copy") as st:
        s_dma = st.sem("dma")
        with nc.Block() as block:
            @block.sync
            def _(sp):
                ld = Loads(sp, s_dma)
                for dst, src in pairs:
                    ld(dst, src)
                ld.wait()


def gdn_unit(nc, e, r, tiles):
    with Stage(nc, "gdn") as st:
        x = st.sb("x", [P, 2, 1552])
        la, be, g = st.sb("la", [P, 8]), st.sb("be", [P, 8]), st.sb("g", [P, 8])
        qT, kT = st.sb("qT", [P, 8, P]), st.sb("kT", [P, 8, P])
        big = lambda n: st.sb(n, [P, 8, P])
        ula, ediff, dec, decT, erow, a, attn = (big(n) for n in ("ula", "ediff", "dec", "decT", "erow", "a", "attn"))
        lev, inv, invT, w = st.sb("lev", [P, 2, 8, P]), big("inv"), big("invT"), big("w")
        res, vnew, kdec, o = big("res"), big("vnew"), big("kdec"), big("o")
        gl = st.sb("gl", [P, 4, 8])
        ps = st.ps("ps", [P, 8, CHUNK])
        names = ("load out dve t tc gsum ula G kk E2 E1 er D DT gl egl A lev lvu W wc dx inv res ks vn vnc o st oc "
                 "kdec fin pool").split()
        s = named(**{n: st.sem(n) for n in names})
        S = r.state
        with nc.Block() as block:
            @block.sync
            def _(sp):
                ld = Loads(sp, s.load)
                for d in range(2):
                    ld(x[:, d, :], rows(e.GQ, tiles[d] * P))
                sp.wait_ge(s.oc, 1)
                out = Loads(sp, s.out)
                for d in range(2):
                    out(e.OG[d, bass.ds(tiles[d] * P, P), :], o[:, 4 * d:4 * d + 4, :].rearrange("p h t -> p (h t)"))
                out.wait()


            @block.tensor
            def _(pe):
                pe.wait_ge(s.load, 32)
                for d in range(2):
                    for kind in range(2):
                        for h in range(4):
                            t = pe.transpose(ps[:, 2 * kind + d, h * P:(h + 1) * P],
                                             x[:, d, (4 * kind + h) * P:(4 * kind + h + 1) * P], r.ident[:])
                        t.then_inc(s.t, 1)
                for d in range(2):
                    t = pe.matmul(ps[:, 4, 4 * d:4 * d + 4], r.cum[:, d, :],
                                  x[:, d, 1536 + 4 * d:1540 + 4 * d], start=True, stop=True)
                t.then_inc(s.gsum, 1)
                pe.wait_ge(s.ula, 1)
                for d in range(2):
                    t = pe.matmul(ps[:, 5 + d, :], r.ones[:],
                                  ula[:, 4 * d:4 * d + 4, :].rearrange("p h t -> p (h t)"), start=True, stop=True)
                t.then_inc(s.G, 1)
                pe.wait_ge(s.tc, 4)
                for n in range(8):
                    t = pe.matmul(ps[:, n // 4, (n % 4) * P:(n % 4 + 1) * P], kT[:, n, :], kT[:, n, :],
                                  start=True, stop=True)
                t.then_inc(s.kk, 1)
                for n in range(8):
                    t = pe.matmul(ps[:, 2 + n // 4, (n % 4) * P:(n % 4 + 1) * P], kT[:, n, :], qT[:, n, :],
                                  start=True, stop=True)
                t.then_inc(s.kk, 1)
                blk = lambda b, n: ps[:, b + n // 4, (n % 4) * P:(n % 4 + 1) * P]
                for v in range(LEVELS):
                    pe.wait_ge(s.lev, v + 1)
                    if v == 0:
                        pe.wait_ge(s.A, 2)
                        pe.wait_ge(s.er, 1)
                        pe.wait_ge(s.gl, 1)
                        for n in range(8):
                            t = pe.transpose(blk(0, n), lev[:, 0, n, :], r.ident[:])
                        t.then_inc(s.W, 1)
                        continue
                    pe.wait_ge(s.inv, 2 * v)
                    for n in range(8):
                        t = pe.matmul(blk(0, n), lev[:, v % 2, n, :], invT[:, n, :], start=True, stop=True)
                    t.then_inc(s.W, 1)
                    pe.wait_ge(s.wc, v)
                    for n in range(8):
                        t = pe.matmul(blk(2, n), w[:, n, :], inv[:, n, :], start=True, stop=True)
                    t.then_inc(s.dx, 1)
                    for n in range(8):
                        t = pe.matmul(blk(4, n), inv[:, n, :], w[:, n, :], start=True, stop=True)
                    t.then_inc(s.dx, 1)
                pe.wait_ge(s.DT, 3)
                for n in range(8):
                    t = pe.matmul(blk(6, n), kT[:, n, :], S[:, n, :], start=True, stop=True)
                t.then_inc(s.ks, 1)
                pe.wait_ge(s.res, 1)
                pe.wait_ge(s.inv, 2 * LEVELS)
                for n in range(8):
                    t = pe.matmul(blk(0, n), invT[:, n, :], res[:, n, :], start=True, stop=True)
                t.then_inc(s.vn, 1)
                pe.wait_ge(s.vnc, 1)
                for n in range(8):
                    pe.matmul(blk(2, n), qT[:, n, :], S[:, n, :], start=True, stop=False)
                    t = pe.matmul(blk(2, n), attn[:, n, :], vnew[:, n, :], start=False, stop=True)
                t.then_inc(s.o, 1)
                pe.wait_ge(s.kdec, 1)
                for n in range(8):
                    t = pe.matmul(blk(4, n), kdec[:, n, :], vnew[:, n, :], start=True, stop=True)
                t.then_inc(s.st, 1)

            @block.scalar
            def _(act):
                for n in range(4):
                    d, kind = n // 2, n % 2
                    act.wait_ge(s.t, n + 1)
                    act.copy((qT, kT)[kind][:, 4 * d:4 * d + 4, :].rearrange("p h t -> p (h t)"),
                             ps[:, 2 * kind + d, :]).then_inc(s.tc, 1)
                act.wait_ge(s.G, 1)
                act.activation(erow[:], heads(ps[:, 5:7, :]), ACT.Exp).then_inc(s.er, 1)
                act.wait_ge(s.E1, 1)
                act.activation(dec[:], dec[:], ACT.Exp, scale=-1.0).then_inc(s.D, 1)
                act.wait_ge(s.E2, 1)
                act.activation(decT[:], decT[:], ACT.Exp).then_inc(s.D, 1)
                act.wait_ge(s.gl, 1)
                act.activation(gl[:, 2:4, :], gl[:, 0:2, :], ACT.Exp).then_inc(s.egl, 1)
                for v in range(1, LEVELS):
                    act.wait_ge(s.W, v + 1)
                    act.copy(w[:], heads(ps[:, 0:2, :])).then_inc(s.wc, 1)
                act.wait_ge(s.vn, 1)
                act.copy(vnew[:], heads(ps[:, 0:2, :])).then_inc(s.vnc, 1)
                act.wait_ge(s.o, 1)
                act.copy(o[:], heads(ps[:, 2:4, :])).then_inc(s.oc, 1)

            @block.gpsimd
            def _(pool):
                pool.wait_ge(s.A, 1)
                for v in range(LEVELS):
                    if v >= 2:
                        pool.wait_ge(s.W, v - 1)
                    if v == 2:
                        pool.wait_ge(s.inv, 1)
                    pool.tensor_tensor(four(lev[:, v % 2]), four(a[:]), per_dir(r.levels[:, v]), ALU.mult)\
                        .then_inc(s.lev, 1)
                    if v == 1:
                        pool.wait_ge(s.egl, 1)
                        for d in range(2):
                            t = pool.tensor_tensor(kdec[:, 4 * d:4 * d + 4, :],
                                                   x[:, d, 512:1024].rearrange("p (h t) -> p h t", h=4),
                                                   gl[:, 3, 4 * d:4 * d + 4].unsqueeze(2).to_broadcast([P, 4, P]),
                                                   ALU.mult)
                        t.then_inc(s.kdec, 1)

            @block.vector
            def _(dve):
                step = Chain(dve, s.dve)
                dve.wait_ge(s.load, 32)
                for d in range(2):
                    h = slice(4 * d, 4 * d + 4)
                    step(dve.tensor_copy(la[:, h], x[:, d, 1536 + 4 * d:1540 + 4 * d]))
                    step(dve.tensor_copy(be[:, h], x[:, d, 1544 + 4 * d:1548 + 4 * d]))
                dve.tensor_tensor(four(ula[:]), per_dir(r.cum[:]), four(wide(la[:])), ALU.mult).then_inc(s.ula, 1)
                dve.wait_ge(s.gsum, 1)
                step(dve.tensor_copy(g[:], ps[:, 4, 0:8]))
                dve.wait_ge(s.er, 1)
                step(dve.tensor_tensor(ediff[:], heads(ps[:, 5:7, :]), wide(g[:]), ALU.subtract))
                dve.tensor_scalar(dec[:], ediff[:], 0.0, None, ALU.max).then_inc(s.E1, 1)
                dve.tensor_scalar(decT[:], ediff[:], 0.0, None, ALU.min).then_inc(s.E2, 1)
                step(dve.tensor_copy(gl[:, 0, 0:4], ps[:, 5, P - 1:CHUNK:P]))
                step(dve.tensor_copy(gl[:, 0, 4:8], ps[:, 6, 0:CHUNK:P]))
                dve.tensor_tensor(gl[:, 1, :], gl[:, 0, :], g[:], ALU.subtract).then_inc(s.gl, 1)
                dve.wait_ge(s.kk, 2)
                dve.wait_ge(s.D, 1)
                step(dve.tensor_tensor(a[:], heads(ps[:, 0:2, :]), dec[:], ALU.mult))
                dve.tensor_tensor(a[:], a[:], wide(be[:]), ALU.mult).then_inc(s.A, 1)
                dve.wait_ge(s.D, 2)
                dve.tensor_tensor(attn[:], heads(ps[:, 2:4, :]), decT[:], ALU.mult).then_inc(s.A, 1)
                dve.wait_ge(s.A, 2)
                dve.tensor_tensor(four(attn[:]), four(attn[:]), per_dir(r.cum[:]), ALU.mult).then_inc(s.DT, 1)
                dve.wait_ge(s.er, 1)
                dve.tensor_tensor(qT[:], qT[:], erow[:], ALU.mult).then_inc(s.DT, 1)
                dve.tensor_tensor(kT[:], kT[:], erow[:], ALU.mult).then_inc(s.DT, 1)
                ident8 = r.ident[:].unsqueeze(1).to_broadcast([P, 8, P])
                dve.wait_ge(s.lev, 1)
                dve.tensor_tensor(inv[:], ident8, lev[:, 0], ALU.subtract).then_inc(s.inv, 1)
                dve.wait_ge(s.W, 1)
                dve.tensor_tensor(invT[:], ident8, heads(ps[:, 0:2, :]), ALU.subtract).then_inc(s.inv, 1)
                dve.wait_ge(s.inv, 2)
                for v in range(1, LEVELS):
                    dve.wait_ge(s.dx, 2 * v)
                    dve.tensor_tensor(inv[:], inv[:], heads(ps[:, 2:4, :]), ALU.subtract).then_inc(s.inv, 1)
                    dve.tensor_tensor(invT[:], invT[:], heads(ps[:, 4:6, :]), ALU.subtract).then_inc(s.inv, 1)
                    dve.wait_ge(s.inv, 2 * v + 2)
                dve.wait_ge(s.ks, 1)
                for d in range(2):
                    step(dve.tensor_tensor(res[:, 4 * d:4 * d + 4, :],
                                           x[:, d, 1024:1536].rearrange("p (h t) -> p h t", h=4),
                                           ps[:, 6 + d, :].rearrange("p (h t) -> p h t", h=4), ALU.subtract))
                dve.tensor_tensor(res[:], res[:], wide(be[:]), ALU.mult).then_inc(s.res, 1)
                dve.wait_ge(s.o, 1)
                dve.wait_ge(s.egl, 1)
                step(dve.tensor_tensor(S[:], S[:], wide(gl[:, 2, :]), ALU.mult))
                dve.wait_ge(s.st, 1)
                dve.tensor_tensor(S[:], S[:], heads(ps[:, 4:6, :]), ALU.add).then_inc(s.fin, 1)


def gdn_pass(nc, e, l):
    gdn_prepare(nc, e, l, ROW_CTX, 0)
    with nc.Fori(0, LAT_TILES) as i:
        gdn_prepare(nc, e, l, i * P + ROW_LAT, i + 1)
    with Stage(nc, "gres") as st:
        r = named(ident=st.sb("ident", [P, P]), ones=st.sb("ones", [P, P]), cum=st.sb("cum", [P, 2, P]),
                            levels=st.sb("levels", [P, LEVELS, 2, P]), state=st.sb("state", [P, 8, P]))
        by_head = lambda t: t.rearrange("d h k v -> k (d h) v")
        copy_stage(nc, [(r.ident[:], e.ident), (r.ones[:], e.ones), (r.cum[:], e.cum), (r.levels[:], e.levels),
                        (r.state[:], e.zero_state)])
        gdn_unit(nc, e, r, (0, 0))
        copy_stage(nc, [(by_head(e.new_gdn[l]), r.state[:])])
        copy_stage(nc, [(r.state[:], by_head(e.state_gdn[l]))])
        with nc.Fori(0, LAT_TILES) as i:
            gdn_unit(nc, e, r, (i + 1, LAT_TILES - i))
    gated_norm_stage(nc, e, l, ROW_CTX, 0, e.OG, COL['gdn_g'], e.gdn_norm[l], 0)
    with nc.Fori(0, LAT_TILES) as i:
        gated_norm_stage(nc, e, l, i * P + ROW_LAT, i + 1, e.OG, COL['gdn_g'], e.gdn_norm[l], 0)


def hgrn_unit(nc, e, l, r, row, tiles):
    X = 512
    with Stage(nc, "hg") as st:
        x, kf, lb = st.sb("x", [P, 2, 3 * X]), st.sb("kf", [P, 2, X]), st.sb("lb", [P, 2, X])
        ea, eb, t1, lf = (st.sb(n, [P, 2, X]) for n in ("ea", "eb", "t1", "lf"))
        big = lambda n: st.sb(n, [P, 8, P])
        qT, kT, attn, qb, kdec, o = (big(n) for n in ("qT", "kT", "attn", "qb", "kdec", "o"))
        ex, ql, kl, part = (st.sb(n, [P, 2, 8, P]) for n in ("ex", "ql", "kl", "part"))
        blast = st.sb("blast", [P, 8])
        ps = st.ps("ps", [P, 8, CHUNK])
        names = ("load out dve pool abs e kf f ln lf t tc bt kd eb ekd qb diag dm kdec span exp ql kl prod m acc o oc "
                 "st fin").split()
        s = named(**{n: st.sem(n) for n in names})
        S = r.state
        blk = lambda b, n: ps[:, b + n // 4, (n % 4) * P:(n % 4 + 1) * P]
        head = lambda n: slice((n % 4) * P, (n % 4 + 1) * P)
        hv = lambda ap: ap.rearrange("p d (h t) -> p (d h) t", h=4)
        span_bank = lambda v: 4 if v % 2 == 0 else 0
        prod_bank = lambda v: 6 if v % 2 == 0 else 2
        with nc.Block() as block:
            @block.sync
            def _(sp):
                ld = Loads(sp, s.load)
                for d in range(2):
                    here = bass.ds(row[d], P)
                    ld(x[:, d, 0:X], e.PR[here, COL['hg_q']:COL['hg_q'] + X])
                    ld(x[:, d, X:2 * X], e.PR[here, COL['hg_f'] + d * X:COL['hg_f'] + (d + 1) * X])
                    ld(x[:, d, 2 * X:3 * X], e.PR[here, COL['hg_i']:COL['hg_i'] + X])
                ld(lb[:, 0, :], e.LB[l].partition_broadcast(P))
                sp.wait_ge(s.oc, 1)
                out = Loads(sp, s.out)
                for d in range(2):
                    out(e.OH[d, bass.ds(tiles[d] * P, P), :], o[:, 4 * d:4 * d + 4, :].rearrange("p h t -> p (h t)"))
                out.wait()

            @block.vector
            def _(dve):
                step = Chain(dve, s.dve)
                dve.wait_ge(s.load, 112)
                z = x[:, :, X:2 * X]
                step(dve.tensor_scalar(lb[:, 1, :], lb[:, 0, :], -1.0, 1.0, ALU.mult, ALU.add))
                lbb = lb[:, 0, :].unsqueeze(1).to_broadcast([P, 2, X])
                lbc = lb[:, 1, :].unsqueeze(1).to_broadcast([P, 2, X])
                dve.tensor_scalar(ea[:], z, 0.0, None, ALU.min).then_inc(s.abs, 1)
                dve.tensor_scalar(eb[:], z, 0.0, None, ALU.max).then_inc(s.abs, 1)
                dve.wait_ge(s.e, 2)
                step(dve.tensor_tensor(t1[:], ea[:], eb[:], ALU.add))
                step(dve.reciprocal(t1[:], t1[:]))
                step(dve.tensor_tensor(kf[:], eb[:], t1[:], ALU.mult))
                dve.tensor_tensor(kf[:], kf[:], lbc, ALU.mult).then_inc(s.kf, 1)
                step(dve.tensor_tensor(eb[:], eb[:], lbb, ALU.mult))
                step(dve.tensor_tensor(ea[:], ea[:], eb[:], ALU.add))
                step(dve.tensor_tensor(t1[:], ea[:], t1[:], ALU.mult))
                dve.tensor_scalar(ea[:], t1[:], 2.0 ** -62, None, ALU.max).then_inc(s.f, 1)
                step(dve.tensor_scalar(eb[:], t1[:], 2.0 ** -62, 2.0 ** 60, ALU.min, ALU.mult))
                dve.tensor_scalar(eb[:], eb[:], 2.0 ** -62, None, ALU.max).then_inc(s.f, 1)
                dve.wait_ge(s.ln, 2)
                dve.scalar_tensor_tensor(out=lf[:], in0=eb[:], scalar=float(2 * np.log(2.0)), in1=ea[:],
                                         op0=ALU.add, op1=ALU.add).then_inc(s.lf, 1)
                dve.wait_ge(s.diag, 1)
                dve.tensor_tensor(attn[:], heads(ps[:, 2:4, :]), r.ident[:].unsqueeze(1).to_broadcast([P, 8, P]),
                                  ALU.mult).then_inc(s.dm, 1)
                dve.wait_ge(s.eb, 1)
                dve.tensor_tensor(qb[:], qT[:], qb[:], ALU.mult).then_inc(s.qb, 1)
                dve.wait_ge(s.ekd, 1)
                dve.tensor_tensor(kdec[:], hv(kf[:]), kdec[:], ALU.mult).then_inc(s.kdec, 1)
                for v in range(LEVELS + 1):
                    if v < LEVELS:
                        dve.wait_ge(s.exp, v + 1)
                        if v >= 2:
                            dve.wait_ge(s.prod, v - 1)
                        dve.tensor_tensor(ql[:, v % 2], qT[:], ex[:, v % 2], ALU.mult).then_inc(s.ql, 1)
                    if v:
                        u = v - 1
                        dve.wait_ge(s.prod, u + 1)
                        if u >= 2:
                            dve.wait_ge(s.acc, u - 1)
                        b = prod_bank(u)
                        dve.tensor_tensor(four(part[:, u % 2]), four(heads(ps[:, b:b + 2, :])),
                                          per_dir(r.levels_t[:, u]), ALU.mult).then_inc(s.m, 1)
                dve.wait_ge(s.o, 1)
                step(dve.tensor_tensor(S[:], S[:], wide(blast[:]), ALU.mult))
                dve.wait_ge(s.st, 1)
                dve.tensor_tensor(S[:], S[:], heads(ps[:, 0:2, :]), ALU.add).then_inc(s.fin, 1)

            @block.gpsimd
            def _(pool):
                pool.wait_ge(s.tc, 4)
                for v in range(LEVELS + 1):
                    if v < LEVELS:
                        pool.wait_ge(s.exp, v + 1)
                        if v >= 2:
                            pool.wait_ge(s.prod, v - 1)
                        pool.tensor_tensor(kl[:, v % 2], kT[:], ex[:, v % 2], ALU.mult).then_inc(s.kl, 1)
                    if v:
                        pool.wait_ge(s.dm, 1)
                        pool.wait_ge(s.m, v)
                        if v >= 2:
                            pool.wait_ge(s.acc, v - 1)
                        pool.tensor_tensor(attn[:], attn[:], part[:, (v - 1) % 2], ALU.add).then_inc(s.acc, 1)

            @block.scalar
            def _(act):
                act.wait_ge(s.abs, 1)
                act.activation(ea[:], ea[:], ACT.Exp).then_inc(s.e, 1)
                act.wait_ge(s.abs, 2)
                act.activation(eb[:], eb[:], ACT.Exp, scale=-1.0).then_inc(s.e, 1)
                act.wait_ge(s.f, 1)
                act.activation(ea[:], ea[:], ACT.Ln).then_inc(s.ln, 1)
                act.wait_ge(s.f, 2)
                act.activation(eb[:], eb[:], ACT.Ln).then_inc(s.ln, 1)
                for n in range(4):
                    kind, d = n // 2, n % 2
                    act.wait_ge(s.t, n + 1)
                    act.copy((qT, kT)[kind][:, 4 * d:4 * d + 4, :].rearrange("p h t -> p (h t)"), ps[:, n, :])\
                       .then_inc(s.tc, 1)
                act.wait_ge(s.bt, 1)
                act.activation(qb[:], heads(ps[:, 4:6, :]), ACT.Exp).then_inc(s.eb, 1)
                act.wait_ge(s.eb, 1)
                act.activation(blast[:, 0:4], ps[:, 4, P - 1:CHUNK:P], ACT.Exp).then_inc(s.pool, 1)
                act.activation(blast[:, 4:8], ps[:, 5, 0:CHUNK:P], ACT.Exp).then_inc(s.pool, 1)
                act.wait_ge(s.kd, 1)
                act.activation(kdec[:], heads(ps[:, 6:8, :]), ACT.Exp).then_inc(s.ekd, 1)
                for v in range(LEVELS):
                    act.wait_ge(s.span, v + 1)
                    if v >= 2:
                        act.wait_ge(s.ql, v - 1)
                        act.wait_ge(s.kl, v - 1)
                    b = span_bank(v)
                    act.activation(ex[:, v % 2], heads(ps[:, b:b + 2, :]), ACT.Exp).then_inc(s.exp, 1)
                act.wait_ge(s.o, 1)
                act.copy(o[:], heads(ps[:, 4:6, :])).then_inc(s.oc, 1)

            @block.tensor
            def _(pe):
                pe.wait_ge(s.load, 112)
                for n in range(4):
                    kind, d = n // 2, n % 2
                    if n == 2:
                        pe.wait_ge(s.kf, 1)
                    for h in range(4):
                        src = x[:, d, h * P:(h + 1) * P] if kind == 0 else kf[:, d, h * P:(h + 1) * P]
                        t = pe.transpose(ps[:, n, h * P:(h + 1) * P], src, r.ident[:])
                    t.then_inc(s.t, 1)
                pe.wait_ge(s.lf, 1)
                for n in range(8):
                    t = pe.matmul(blk(4, n), lf[:, n // 4, head(n)], r.cum[:, n // 4, :], start=True, stop=True)
                t.then_inc(s.bt, 1)
                for d in range(2):
                    t = pe.matmul(ps[:, 6 + d, :], r.after[:, d, :], lf[:, d, :], start=True, stop=True)
                t.then_inc(s.kd, 1)
                pe.wait_ge(s.tc, 4)
                for n in range(8):
                    t = pe.matmul(blk(2, n), kT[:, n, :], qT[:, n, :], start=True, stop=True)
                t.then_inc(s.diag, 1)

                def spans(v):
                    if v == 0:
                        pe.wait_ge(s.pool, 2)
                    if v >= 2:
                        pe.wait_ge(s.exp, v - 1)
                    for n in range(8):
                        t = pe.matmul(blk(span_bank(v), n), lf[:, n // 4, head(n)], r.spans[:, v, n // 4, :],
                                      start=True, stop=True)
                    t.then_inc(s.span, 1)

                spans(0)
                for v in range(LEVELS):
                    if v + 1 < LEVELS:
                        spans(v + 1)
                    pe.wait_ge(s.ql, v + 1)
                    pe.wait_ge(s.kl, v + 1)
                    if v == 0:
                        pe.wait_ge(s.ekd, 1)
                    if v == 1:
                        pe.wait_ge(s.dm, 1)
                    if v >= 2:
                        pe.wait_ge(s.m, v - 1)
                    for n in range(8):
                        t = pe.matmul(blk(prod_bank(v), n), kl[:, v % 2, n, :], ql[:, v % 2, n, :],
                                      start=True, stop=True)
                    t.then_inc(s.prod, 1)
                pe.wait_ge(s.acc, LEVELS)
                pe.wait_ge(s.qb, 1)
                pe.wait_ge(s.exp, LEVELS)
                for n in range(8):
                    pe.matmul(blk(4, n), qb[:, n, :], S[:, n, :], start=True, stop=False)
                    t = pe.matmul(blk(4, n), attn[:, n, :], x[:, n // 4, 2 * X:][:, head(n)],
                                  start=False, stop=True)
                t.then_inc(s.o, 1)
                pe.wait_ge(s.kdec, 1)
                for n in range(8):
                    t = pe.matmul(blk(0, n), kdec[:, n, :], x[:, n // 4, 2 * X:][:, head(n)], start=True, stop=True)
                t.then_inc(s.st, 1)


def hgrn_pass(nc, e, l):
    with Stage(nc, "hres") as st:
        r = named(ident=st.sb("ident", [P, P]), cum=st.sb("cum", [P, 2, P]), after=st.sb("after", [P, 2, P]),
                            levels_t=st.sb("levels", [P, LEVELS, 2, P]), spans=st.sb("spans", [P, LEVELS, 2, P]),
                            state=st.sb("state", [P, 8, P]))
        by_head = lambda t: t.rearrange("d h k v -> k (d h) v")
        copy_stage(nc, [(r.ident[:], e.ident), (r.cum[:], e.cum), (r.after[:], e.after), (r.levels_t[:], e.levels_t),
                        (r.spans[:], e.spans), (r.state[:], e.zero_state)])
        hgrn_unit(nc, e, l, r, (ROW_CTX, ROW_CTX), (0, 0))
        copy_stage(nc, [(by_head(e.new_hgrn[l]), r.state[:])])
        copy_stage(nc, [(r.state[:], by_head(e.state_hgrn[l]))])
        with nc.Fori(0, LAT_TILES) as i:
            hgrn_unit(nc, e, l, r, (i * P + ROW_LAT, (LAT_TILES - 1 - i) * P + ROW_LAT), (i + 1, LAT_TILES - i))
    gated_norm_stage(nc, e, l, ROW_CTX, 0, e.OH, COL['hg_g'], e.hg_norm[l], 1024)
    with nc.Fori(0, LAT_TILES) as i:
        gated_norm_stage(nc, e, l, i * P + ROW_LAT, i + 1, e.OH, COL['hg_g'], e.hg_norm[l], 1024)


RQ_PARTS = ('r', 'k', 'v', 'nkk', 'b', 'lw0', 'lw1', 'gate', 'bonus')
RQ = {name: 512 * n for n, name in enumerate(RQ_PARTS)}


def rwkv_prepare(nc, e, l, row, tile):
    with Stage(nc, "rprep") as st:
        xs, mu = st.sb("xs", [P, 3, RW_W]), st.sb("mu", [P, 2, RW_W])
        vec = st.sb("vec", [P, 6, RW])
        w2, a2, g2, ident = st.sb("w2", [P, RW]), st.sb("a2", [64, RW]), st.sb("g2", [P, RW]), st.sb("ident", [P, P])
        lora, loraT = st.sb("lora", [P, 2, P]), st.sb("loraT", [P, 3, P])
        res, a, t1, t2 = st.sb("res", [P, 9, RW]), st.sb("a", [P, RW]), st.sb("t1", [P, RW]), st.sb("t2", [P, RW])
        ss = st.sb("ss", [P, 5, RW_H])
        ps, pt = st.ps("ps", [P, 4, CHUNK]), st.ps("pt", [P, CHUNK])
        names = "load out dve shift lora t tc mm w sig root ss done gate".split()
        s = named(**{n: st.sem(n) for n in names})
        n_loads = 3 + 2 + 6 + 4
        hv = lambda ap: ap.rearrange("p (h d) -> p h d", h=RW_H)
        hb = lambda ap: ap.unsqueeze(2).to_broadcast([P, RW_H, RW_D])
        o0 = 3 * RW
        with nc.Block() as block:
            @block.sync
            def _(sp):
                ld = Loads(sp, s.load)
                for j in range(3):
                    ld(xs[:, j, :], e.PR[bass.ds(row - 1 + j, P), COL['rw']:COL['rw'] + RW_W])
                for j in range(2):
                    ld(mu[:, j, :], e.rw_mu[l, j, :].partition_broadcast(P))
                for j, v in enumerate((e.rw_w0[l, 0, :], e.rw_w0[l, 1, :], e.rw_a0[l], e.rw_kk[l], e.rw_ka[l],
                                       e.rw_rk[l])):
                    ld(vec[:, j, :], v.partition_broadcast(P))
                ld(w2[:], e.rw_w2[l])
                ld(a2[:], e.rw_a2[l])
                ld(g2[:], e.rw_g2[l])
                ld(ident[:], e.ident)
                sp.wait_ge(s.done, 1)
                sp.wait_ge(s.gate, 1)
                sp.dma_start(rows(e.RQ, tile * P), res[:].rearrange("p a b -> p (a b)")).then_inc(s.out, 16)
                sp.wait_ge(s.out, 16)

            @block.scalar
            def _(act):
                act.wait_ge(s.shift, 1)
                act.activation(lora[:, 0, :], xs[:, 1, o0:o0 + P], ACT.Tanh).then_inc(s.lora, 1)
                act.activation(lora[:, 1, :], xs[:, 1, o0 + 192:o0 + 192 + P], ACT.Sigmoid).then_inc(s.lora, 1)
                act.wait_ge(s.t, 1)
                act.copy(loraT[:].rearrange("p a b -> p (a b)")[:, 0:2 * P], pt[:, 0:2 * P]).then_inc(s.tc, 1)
                act.copy(loraT[0:64, 2, :], pt[0:64, 2 * P:3 * P]).then_inc(s.tc, 1)
                for n, dst in enumerate((res[:, 5, :], res[:, 6, :], a[:])):
                    act.wait_ge(s.w, n + 1)
                    act.activation(dst, dst, ACT.Sigmoid).then_inc(s.sig, 1)
                act.wait_ge(s.mm, 4)
                act.copy(res[:, 7, :], ps[:, 3, :]).then_inc(s.gate, 1)
                act.wait_ge(s.ss, 1)
                act.activation(ss[:, 2, :], ss[:, 1, :], ACT.Sqrt).then_inc(s.root, 1)

            @block.tensor
            def _(pe):
                pe.wait_ge(s.lora, 2)
                pe.transpose(pt[:, 0:P], lora[:, 0, :], ident[:])
                pe.transpose(pt[:, P:2 * P], lora[:, 1, :], ident[:])
                pe.transpose(pt[0:64, 2 * P:3 * P], xs[:, 1, o0 + P:o0 + 192], ident[:]).then_inc(s.t, 1)
                pe.wait_ge(s.tc, 2)
                for d in range(2):
                    r = slice(64 * d, 64 * d + 64)
                    pe.matmul(ps[:, d, :], loraT[r, 0, :], w2[r, :], start=True, stop=True).then_inc(s.mm, 1)
                pe.matmul(ps[:, 2, :], loraT[0:64, 2, :], a2[:], start=True, stop=True).then_inc(s.mm, 1)
                pe.matmul(ps[:, 3, :], loraT[:, 1, :], g2[:], start=True, stop=True).then_inc(s.mm, 1)

            @block.vector
            def _(dve):
                step = Chain(dve, s.dve)
                dve.wait_ge(s.load, 16 * n_loads)
                for j in (0, 2):
                    step(dve.tensor_tensor(xs[:, j, :], xs[:, j, :], xs[:, 1, :], ALU.subtract))
                    step(dve.tensor_tensor(xs[:, j, :], xs[:, j, :], mu[:, j // 2, :], ALU.mult))
                step(dve.tensor_tensor(xs[:, 0, :], xs[:, 0, :], xs[:, 2, :], ALU.add))
                dve.tensor_tensor(xs[:, 1, :], xs[:, 1, :], xs[:, 0, :], ALU.add).then_inc(s.shift, 1)
                dve.wait_ge(s.shift, 1)
                r, kr, v = (xs[:, 1, n * RW:(n + 1) * RW] for n in range(3))
                step(dve.tensor_copy(res[:, 0, :], r))
                step(dve.tensor_copy(res[:, 2, :], v))
                step(dve.tensor_tensor(t1[:], kr, vec[:, 3, :], ALU.mult))
                step(dve.tensor_tensor(t2[:], t1[:], t1[:], ALU.mult))
                step(dve.tensor_reduce(ss[:, 0, :], hv(t2[:]), AX.X, ALU.add))
                dve.tensor_scalar(ss[:, 1, :], ss[:, 0, :], NORM_EPS, None, ALU.add).then_inc(s.ss, 1)
                for n, dst in enumerate((res[:, 5, :], res[:, 6, :], a[:])):
                    dve.wait_ge(s.mm, n + 1)
                    dve.tensor_tensor(dst, ps[:, n, :], vec[:, n, :], ALU.add).then_inc(s.w, 1)
                for n in (5, 6):
                    dve.wait_ge(s.sig, n - 4)
                    step(dve.tensor_scalar(res[:, n, :], res[:, n, :], -float(np.exp(-0.5)), None, ALU.mult))
                dve.wait_ge(s.root, 1)
                step(dve.reciprocal(ss[:, 3, :], ss[:, 2, :]))
                step(dve.tensor_scalar(ss[:, 4, :], ss[:, 3, :], -1.0, None, ALU.mult))
                step(dve.tensor_tensor(hv(res[:, 3, :]), hv(t1[:]), hb(ss[:, 4, :]), ALU.mult))
                step(dve.tensor_tensor(hv(t1[:]), hv(t1[:]), hb(ss[:, 3, :]), ALU.mult))
                dve.wait_ge(s.sig, 3)
                step(dve.tensor_tensor(res[:, 4, :], t1[:], a[:], ALU.mult))
                step(dve.scalar_tensor_tensor(out=a[:], in0=a[:], scalar=-1.0, in1=vec[:, 4, :], op0=ALU.add,
                                              op1=ALU.mult))
                step(dve.scalar_tensor_tensor(out=res[:, 1, :], in0=a[:], scalar=1.0, in1=kr, op0=ALU.add,
                                              op1=ALU.mult))
                step(dve.tensor_tensor(t2[:], r, res[:, 1, :], ALU.mult))
                step(dve.tensor_tensor(t2[:], t2[:], vec[:, 5, :], ALU.mult))
                step(dve.tensor_reduce(ss[:, 0, :], hv(t2[:]), AX.X, ALU.add))
                dve.tensor_tensor(hv(res[:, 8, :]), hv(v), hb(ss[:, 0, :]), ALU.mult).then_inc(s.done, 1)


def rwkv_unit(nc, e, r, tiles):
    H2 = 2 * RW_H
    with Stage(nc, "rw") as st:
        x = st.sb("x", [P, 2, 6, RW])
        big = lambda n: st.sb(n, [P, 8, P])
        ep, em, epx, dec, rt, kt, at, bt = (big(n) for n in ("ep", "em", "epx", "dec", "rt", "kt", "at", "bt"))
        kd, bd, sm, o, rhs, u = (big(n) for n in ("kd", "bd", "sm", "o", "rhs", "u"))
        emid, efin = st.sb("emid", [P, 8]), st.sb("efin", [P, 8])
        nm, inv, invT, w = (st.sb(n, [P, H2, P]) for n in ("nm", "inv", "invT", "w"))
        lev = st.sb("lev", [P, 2, H2, P])
        ps = st.ps("ps", [P, 8, CHUNK])
        names = ("load out dve exp em epx ex t til N nc A ac B bc C cc lev W wc dx dxT inv sm R rc U uc Y oc dec st fin "
                 "mid").split()
        s = named(**{n: st.sem(n) for n in names})
        S = r.state
        blk = lambda b, n: ps[:, b + n // 4, (n % 4) * P:(n % 4 + 1) * P]
        order = [8 * q + p for p in range(8) for q in range(2)]
        hd = lambda ap, n: ap[64 * (n // 8):64 * (n // 8) + 64, n % 8, :]
        lane = lambda n: slice((n // 8) * RW_D, (n // 8 + 1) * RW_D)
        vals = lambda n: x[:, (n % 8) // 4, 2, :].rearrange("p (a c) -> p a c", a=4)[:, n % 4, lane(n)]
        all4 = lambda b: ps[:, b:b + 4, :].rearrange("p b (h t) -> p (b h) t", h=4)
        half_of = lambda ap, q: four(ap[:, 8 * q:8 * q + 8, :])
        with nc.Block() as block:
            @block.sync
            def _(sp):
                ld = Loads(sp, s.load)
                for d in range(2):
                    ld(x[:, d, 0:5, :].rearrange("p a b -> p (a b)"), e.RQ[bass.ds(tiles[d] * P, P), 0:5 * RW])
                    ld(x[:, d, 5, :], e.RQ[bass.ds(tiles[d] * P, P), (5 + d) * RW:(6 + d) * RW])
                sp.wait_ge(s.oc, 1)
                out = Loads(sp, s.out)
                for d in range(2):
                    out(e.OR[d, bass.ds(tiles[d] * P, P), :], o[:, 4 * d:4 * d + 4, :].rearrange("p h t -> p (h t)"))
                out.wait()

            @block.tensor
            def _(pe):
                pe.wait_ge(s.load, 64)
                lw = lambda n: x[:, n // 4, 5, (n % 4) * P:(n % 4 + 1) * P]
                for n in range(8):
                    pe.matmul(blk(0, n), lw(n), r.mid[:, n // 4, :], start=True, stop=True)
                    pe.matmul(blk(2, n), lw(n), r.midx[:, n // 4, :], start=True, stop=True)
                for d in range(2):
                    pe.matmul(ps[:, 4 + d, :], r.after[:, d, :], x[:, d, 5, :], start=True, stop=True)
                for n in range(8):
                    m = P // 2 - 1 if n < 4 else P // 2
                    t = pe.matmul(ps[:, 6, n:n + 1], lw(n), r.cum[:, n // 4, m:m + 1], start=True, stop=True)
                t.then_inc(s.exp, 1)
                pe.wait_ge(s.ex, 5)
                for b, part in enumerate((0, 1, 3, 4)):
                    for n in range(8):
                        t = pe.transpose(blk(2 * b, n), x[:, n // 4, part, (n % 4) * P:(n % 4 + 1) * P], r.ident[:])
                    t.then_inc(s.t, 1)
                pe.wait_ge(s.til, 4)
                for n in order:
                    t = pe.matmul(blk(0, n), hd(at, n), hd(bt, n), start=True, stop=True)
                t.then_inc(s.N, 1)
                for n in order:
                    t = pe.matmul(blk(4, n), hd(kt, n), hd(at, n), start=True, stop=True)
                t.then_inc(s.A, 1)
                pe.wait_ge(s.nc, 1)
                for n in order:
                    t = pe.matmul(blk(0, n), hd(bt, n), hd(rt, n), start=True, stop=True)
                t.then_inc(s.B, 1)
                pe.wait_ge(s.ac, 2)
                for n in order:
                    t = pe.matmul(blk(4, n), hd(kt, n), hd(rt, n), start=True, stop=True)
                t.then_inc(s.C, 1)
                for v in range(LEVELS):
                    pe.wait_ge(s.lev, 2 * v + 2)
                    if v == 0:
                        pe.wait_ge(s.bc, 2)
                        for n in range(H2):
                            t = pe.transpose(blk(0, n), lev[:, 0, n, :], r.ident[:])
                        t.then_inc(s.W, 1)
                        continue
                    pe.wait_ge(s.inv, 2 * v)
                    for n in range(H2):
                        t = pe.matmul(blk(0, n), lev[:, v % 2, n, :], invT[:, n, :], start=True, stop=True)
                    t.then_inc(s.W, 1)
                    pe.wait_ge(s.wc, v)
                    pe.wait_ge(s.cc, 2)
                    for n in range(H2):
                        t = pe.matmul(blk(4, n), w[:, n, :], inv[:, n, :], start=True, stop=True)
                    t.then_inc(s.dx, 1)
                    for n in range(H2):
                        t = pe.matmul(blk(0, n), inv[:, n, :], w[:, n, :], start=True, stop=True)
                    t.then_inc(s.dx, 1)
                pe.wait_ge(s.inv, 2 * LEVELS)
                pe.wait_ge(s.sm, 1)
                half = lambda b, n: ps[:, b + (n % 8) // 4, :].rearrange("p (a c) -> p a c", a=4)[:, n % 4, lane(n)]
                for p in range(8):
                    pe.matmul(blk(0, p), at[:, p, :], sm[:, p, :], start=True, stop=True)
                    for n in (p, 8 + p):
                        t = pe.matmul(half(0, n), r.aak[:, n, :], vals(n), start=False, stop=True,
                                      skip_group_check=True)
                t.then_inc(s.R, 1)
                pe.wait_ge(s.rc, 1)
                flat = lambda ap, n: ap[:, n % 8, lane(n)]
                for n in range(H2):
                    t = pe.matmul(half(2, n), invT[:, n, :], flat(rhs, n), start=True, stop=True)
                t.then_inc(s.U, 1)
                pe.wait_ge(s.uc, 1)
                for p in range(8):
                    pe.matmul(blk(4, p), rt[:, p, :], sm[:, p, :], start=True, stop=True)
                    for n in (p, 8 + p):
                        pe.matmul(half(4, n), r.arb[:, n, :], flat(u, n), start=False, stop=True,
                                  skip_group_check=True)
                        t = pe.matmul(half(4, n), r.ark[:, n, :], vals(n), start=False, stop=True,
                                      skip_group_check=True)
                t.then_inc(s.Y, 1)
                pe.wait_ge(s.dec, 2)
                for p in range(8):
                    pe.matmul(blk(6, p), kd[:, p, :], x[:, p // 4, 2, (p % 4) * P:(p % 4 + 1) * P],
                              start=True, stop=False)
                    t = pe.matmul(blk(6, p), bd[:, p, :], u[:, p, :], start=False, stop=True)
                t.then_inc(s.st, 1)

            @block.scalar
            def _(act):
                act.wait_ge(s.exp, 1)
                act.activation(ep[:], heads(ps[:, 0:2, :]), ACT.Exp).then_inc(s.ex, 1)
                act.activation(em[:], heads(ps[:, 0:2, :]), ACT.Exp, scale=-1.0).then_inc(s.ex, 1)
                act.activation(epx[:], heads(ps[:, 2:4, :]), ACT.Exp).then_inc(s.ex, 1)
                act.activation(dec[:], heads(ps[:, 4:6, :]), ACT.Exp).then_inc(s.ex, 1)
                act.activation(emid[:], ps[:, 6, 0:8], ACT.Exp).then_inc(s.ex, 1)
                act.wait_ge(s.N, 1)
                act.copy(nm[:], all4(0)).then_inc(s.nc, 1)
                for v in range(1, LEVELS):
                    act.wait_ge(s.W, v + 1)
                    act.copy(w[:], all4(0)).then_inc(s.wc, 1)
                act.wait_ge(s.R, 1)
                act.copy(rhs[:], heads(ps[:, 0:2, :])).then_inc(s.rc, 1)
                act.wait_ge(s.U, 1)
                act.copy(u[:], heads(ps[:, 2:4, :])).then_inc(s.uc, 1)
                act.wait_ge(s.Y, 1)
                act.copy(o[:], heads(ps[:, 4:6, :])).then_inc(s.oc, 1)

            @block.gpsimd
            def _(pool):
                pool.wait_ge(s.nc, 1)
                for v in range(LEVELS):
                    if v >= 2:
                        pool.wait_ge(s.W, v - 1)
                    if v == 2:
                        pool.wait_ge(s.inv, 1)
                    for q in range(2):
                        pool.tensor_tensor(half_of(lev[:, v % 2], q), half_of(nm[:], q), per_dir(r.levels[:, v]),
                                           ALU.mult).then_inc(s.lev, 1)
                    if v == 2:
                        pool.wait_ge(s.ex, 4)
                        for dst, part in ((kd, 1), (bd, 4)):
                            pool.tensor_tensor(four(dst[:]), x[:, :, part, :].rearrange("p d (h t) -> p d h t", h=4),
                                               four(dec[:]), ALU.mult).then_inc(s.dec, 1)

            @block.vector
            def _(dve):
                step = Chain(dve, s.dve)
                dve.wait_ge(s.ex, 5)
                for b, (dst, ex) in enumerate(((rt, ep), (kt, em), (at, epx), (bt, em))):
                    dve.wait_ge(s.t, b + 1)
                    dve.tensor_tensor(dst[:], heads(ps[:, 2 * b:2 * b + 2, :]), ex[:], ALU.mult).then_inc(s.til, 1)
                dve.tensor_tensor(sm[:], S[:], wide(emid[:]), ALU.mult).then_inc(s.sm, 1)
                step(dve.tensor_tensor(efin[:, 0:4], ep[:, 0:4, P - 1], emid[:, 0:4], ALU.mult))
                step(dve.tensor_tensor(efin[:, 4:8], ep[:, 4:8, 0], emid[:, 4:8], ALU.mult))
                for done, mask, dst, b, out in ((s.A, r.before_u, r.aak, 4, s.ac), (s.B, r.cum_u, r.arb, 0, s.bc),
                                                (s.C, r.cum_u, r.ark, 4, s.cc)):
                    dve.wait_ge(done, 1)
                    for q in range(2):
                        dve.copy_predicated(half_of(dst, q), per_dir(mask[:]), half_of(all4(b), q)).then_inc(out, 1)
                id16 = r.ident[:].unsqueeze(1).to_broadcast([P, H2, P])
                dve.wait_ge(s.lev, 2)
                dve.tensor_tensor(inv[:], id16, lev[:, 0], ALU.add).then_inc(s.inv, 1)
                dve.wait_ge(s.W, 1)
                dve.tensor_tensor(invT[:], id16, all4(0), ALU.add).then_inc(s.inv, 1)
                dve.wait_ge(s.inv, 2)
                for v in range(1, LEVELS):
                    dve.wait_ge(s.dx, 2 * v)
                    dve.tensor_tensor(inv[:], inv[:], all4(4), ALU.add).then_inc(s.inv, 1)
                    dve.tensor_tensor(invT[:], invT[:], all4(0), ALU.add).then_inc(s.inv, 1)
                    dve.wait_ge(s.inv, 2 * v + 2)
                step(dve.tensor_tensor(S[:], S[:], wide(efin[:]), ALU.mult))
                dve.wait_ge(s.st, 1)
                for q in range(2):
                    h = slice(64 * q, 64 * q + 64)
                    dve.tensor_tensor(S[h, :, h], S[h, :, h], heads(ps[:, 6:8, :])[h, :, h], ALU.add)\
                       .then_inc(s.fin, 1)


def rwkv_finish(nc, e, l, tile):
    with Stage(nc, "rfin") as st:
        o, gb, gn = st.sb("o", [P, 2, RW]), st.sb("gb", [P, 2, RW]), st.sb("gn", [P, 2, RW])
        sq, ss = st.sb("sq", [P, RW]), st.sb("ss", [P, 6, RW_H])
        names = "load out dve ss root done".split()
        s = named(**{n: st.sem(n) for n in names})
        hv = lambda ap: ap.rearrange("p (h d) -> p h d", h=RW_H)
        hb = lambda ap: ap.unsqueeze(2).to_broadcast([P, RW_H, RW_D])
        with nc.Block() as block:
            @block.sync
            def _(sp):
                ld = Loads(sp, s.load)
                for d in range(2):
                    ld(o[:, d, :], e.OR[d, bass.ds(tile * P, P), :])
                ld(gb[:].rearrange("p a b -> p (a b)"), e.RQ[bass.ds(tile * P, P), RQ['gate']:RQ['gate'] + 2 * RW])
                ld(gn[:, 0, :], e.rw_gn_w[l].partition_broadcast(P))
                ld(gn[:, 1, :], e.rw_gn_b[l].partition_broadcast(P))
                sp.wait_ge(s.done, 1)
                sp.dma_start(e.Y[bass.ds(tile * P, P), 1536:2048], sq[:]).then_inc(s.out, 16)
                sp.wait_ge(s.out, 16)

            @block.scalar
            def _(act):
                act.wait_ge(s.ss, 1)
                act.activation(ss[:, 3, :], ss[:, 2, :], ACT.Sqrt).then_inc(s.root, 1)

            @block.vector
            def _(dve):
                step = Chain(dve, s.dve)
                dve.wait_ge(s.load, 80)
                y = o[:, 0, :]
                step(dve.tensor_tensor(y, y, o[:, 1, :], ALU.add))
                step(dve.tensor_reduce(ss[:, 0, :], hv(y), AX.X, ALU.add))
                step(dve.tensor_scalar(ss[:, 1, :], ss[:, 0, :], 1.0 / RW_D, None, ALU.mult))
                step(dve.tensor_tensor(hv(y), hv(y), hb(ss[:, 1, :]), ALU.subtract))
                step(dve.tensor_tensor(sq[:], y, y, ALU.mult))
                step(dve.tensor_reduce(ss[:, 0, :], hv(sq[:]), AX.X, ALU.add))
                dve.tensor_scalar(ss[:, 2, :], ss[:, 0, :], 1.0 / RW_D, RW_GN_EPS, ALU.mult, ALU.add)\
                   .then_inc(s.ss, 1)
                dve.wait_ge(s.root, 1)
                step(dve.reciprocal(ss[:, 4, :], ss[:, 3, :]))
                step(dve.tensor_tensor(hv(y), hv(y), hb(ss[:, 4, :]), ALU.mult))
                step(dve.tensor_tensor(y, y, gn[:, 0, :], ALU.mult))
                step(dve.tensor_tensor(y, y, gn[:, 1, :], ALU.add))
                step(dve.tensor_tensor(y, y, gb[:, 1, :], ALU.add))
                dve.tensor_tensor(sq[:], y, gb[:, 0, :], ALU.mult).then_inc(s.done, 1)


def rwkv_pass(nc, e, l):
    rwkv_prepare(nc, e, l, ROW_CTX, 0)
    with nc.Fori(0, LAT_TILES) as i:
        rwkv_prepare(nc, e, l, i * P + ROW_LAT, i + 1)
    with Stage(nc, "rres") as st:
        m = lambda n, dt=F32: st.sb(n, [P, 2, P], dt)
        r = named(ident=st.sb("ident", [P, P]), cum=m("cum"), after=m("after"), mid=m("mid"),
                            midx=m("midx"), cum_u=m("cumu", I32), before_u=m("beforeu", I32),
                            levels=st.sb("levels", [P, LEVELS, 2, P]), state=st.sb("state", [P, 8, P]),
                            aak=st.sb("aak", [P, 16, P]), arb=st.sb("arb", [P, 16, P]), ark=st.sb("ark", [P, 16, P]))
        s_zero = st.sem("zero")
        with nc.Block() as block:
            @block.vector
            def _(dve):
                for t in (r.aak, r.arb, r.ark):
                    dve.memset(t[:], 0.0).then_inc(s_zero, 1)
        half = lambda q: slice(64 * q, 64 * q + 64)
        copy_stage(nc, [
            (r.ident[:], e.ident), (r.cum[:], e.cum), (r.after[:], e.after), (r.mid[:], e.mid), (r.midx[:], e.midx),
            (r.cum_u[:], e.cum_u), (r.before_u[:], e.before_u), (r.levels[:], e.levels),
            (r.state[:], e.zero_state)])
        rwkv_unit(nc, e, r, (0, 0))
        copy_stage(nc, [(e.new_rwkv[l, q], r.state[half(q), :, half(q)]) for q in range(2)])
        copy_stage(nc, [(r.state[half(q), :, half(q)], e.state_rwkv[l, q]) for q in range(2)])
        with nc.Fori(0, LAT_TILES) as i:
            rwkv_unit(nc, e, r, (i + 1, LAT_TILES - i))
    rwkv_finish(nc, e, l, 0)
    with nc.Fori(0, LAT_TILES) as i:
        rwkv_finish(nc, e, l, i + 1)


def constants():
    j, t = np.arange(P)[:, None], np.arange(P)[None]
    mirror = lambda m: np.stack([m, m[::-1, ::-1]], 1).astype(np.float32)
    cum = mirror(j <= t)
    levels, spans = [], []
    for v in range(LEVELS):
        s = 1 << v
        levels.append(mirror((j // (2 * s) == t // (2 * s)) & ((j // s) % 2 == 1) & ((t // s) % 2 == 0)))
        mid = (t // (2 * s)) * 2 * s + s - 1
        spans.append(mirror(((t > mid) & (j > mid) & (j <= t)) | ((t <= mid) & (j > t) & (j <= mid))))
    levels, spans = np.stack(levels, 1), np.stack(spans, 1)
    mid = [mirror(((j >= P // 2) & (j <= t - k)).astype(np.float32) - ((j < P // 2) & (j > t - k))) for k in (0, 1)]
    inv = 10000.0 ** (-np.arange(32, dtype=np.float32) / 32)
    rope = np.zeros((CTX + LAT, 2, 2, 32), np.float32)
    rope[:, 0] = 1.0
    pos = np.arange(LAT)
    for a, grid in enumerate((pos // GRID_W, pos % GRID_W)):
        angle = grid.astype(np.float32)[:, None] * inv[None]
        rope[CTX:, 0, a], rope[CTX:, 1, a] = np.cos(angle), np.sin(angle)
    key_shift = np.zeros((32, GRID_W, P), np.float32)
    for ck in range(GRID_W):
        for p in range(P):
            cq = p % GRID_W
            first = min(max(cq - NA_WC // 2, 0), GRID_W - NA_WC)
            key_shift[0, ck, p] = 0.0 if first <= ck < first + NA_WC else -1e30
            if 0 <= ck - cq + NA_WC - 1 < 2 * NA_WC - 1:
                key_shift[ck - cq + NA_WC, ck, p] = 1.0
    return {
        "ident": np.eye(P, dtype=np.float32), "ones": np.ones((P, P), np.float32), "cum": cum, "after": 1 - cum,
        "levels": levels, "levels_t": np.ascontiguousarray(levels[:, :, ::-1]), "spans": spans,
        "mid": mid[0], "midx": mid[1], "cum_u": cum.astype(np.int32),
        "before_u": (cum * (1 - np.eye(P, dtype=np.float32)[:, None])).astype(np.int32),
        "zero_state": np.zeros((P, 8, P), np.float32), "rope": rope.reshape(CTX + LAT, P),
        "key_shift": key_shift.reshape(32, GRID_W * P),
        "layer_base": np.arange(DEPTH, dtype=np.float32).reshape(DEPTH, 1, 1).repeat(P, 1) * N_EXPERTS,
        "iota16": np.tile(np.arange(TOPK, dtype=np.float32), (P, 1)),
    }


def end_stage(nc, e):
    copy_stage(nc, [(e.y_prompt, e.X[0:CTX, :]), (e.y_sample, e.X[CTX:, :])])


def build(nc, e):
    with ExitStack() as ctx:
        s_rows = [ctx.enter_context(nc.semaphore(f"rows{n}")) for n in range(SLOTS)]
        start_stage(nc, e)
        with nc.Fori(0, DEPTH) as l:
            mod_stage(nc, e, l)
            project_stage(nc, e, l, 0, e.w_in[l], IN_W, e.PR[ROW_LAT:ROW_LAT + LAT, :], e.PR[ROW_CTX:ROW_CTX + CTX, :])
            attention_stage(nc, e, l)
            gdn_pass(nc, e, l)
            hgrn_pass(nc, e, l)
            rwkv_pass(nc, e, l)
            merge_stage(nc, e, l)
            project_stage(nc, e, l, 3, e.peer_wq[l], 2 * HEADS * HALF, e.QH[CTX:, :], e.QH[0:CTX, :])
            with nc.Fori(0, TILES) as i:
                route_stage(nc, e, l, i)
            with nc.Fori(0, TILES) as i:
                expert_stage(nc, e, l, i, s_rows)
        end_stage(nc, e)


SCRATCH = {
    "X": (CTX + LAT, D), "PR": (P_ROWS, IN_W), "MOD": (TILES, 6 * D), "LB": (DEPTH, 512), "Y": (CTX + LAT, 2048),
    "GQ": (CTX + LAT, 1552), "OG": (2, CTX + LAT, 512), "OH": (2, CTX + LAT, 512), "OR": (2, CTX + LAT, 512),
    "RQ": (CTX + LAT, 9 * RW), "QH": (CTX + LAT, 2048), "G": (CTX + LAT, PICKS),
}
OUTPUTS = {
    "y_prompt": (CTX, D), "y_sample": (LAT, D), "new_gdn": (DEPTH, 2, GD_H, P, P), "new_hgrn": (DEPTH, 2, HG_H, P, P),
    "new_rwkv": (DEPTH, 2, RW_D, 8, RW_D), "new_k": (DEPTH, NA_H, CTX, NA_D), "new_v": (DEPTH, NA_H, CTX, NA_D),
}


def kernel(**inputs):
    import concourse.bacc as _bacc
    from concourse.bass_utils import run_bass_kernel_spmd as _run

    a = {k: np.ascontiguousarray(v) for k, v in inputs.items()}
    arrays = constants()
    for k in ("w_mod", "b_mod", "w_in", "gdn_conv", "gdn_norm", "hg_lb_logits", "hg_norm", "rw_mu", "rw_w0", "rw_a0",
              "rw_a2", "rw_g2", "rw_kk", "rw_ka", "rw_gn_w", "rw_gn_b", "w_branch", "w_out", "ln1_g", "ln1_b",
              "ln2_g", "ln2_b", "peer_wq"):
        arrays[k] = a[k]
    arrays.update(
        x_prompt=a["x_prompt"][0], x_sample=a["x_sample"][0],
        c_cols=np.stack([a["c_ctx"], a["c"][0]], -1).reshape(KD, P, 2).transpose(1, 0, 2),
        gdn_A_log=a["gdn_A_log"].reshape(DEPTH, 8), gdn_dt_bias=a["gdn_dt_bias"].reshape(DEPTH, 8),
        rw_rk=a["rw_rk"].reshape(DEPTH, RW), rw_w2=a["rw_w2"].reshape(DEPTH, P, RW),
        rpb_t=a["na_rpb"].transpose(0, 3, 1, 2).reshape(DEPTH, 2 * NA_WC - 1, -1),
        cache_k=a["cache_k_na"][0], cache_v=a["cache_v_na"][0],
        state_gdn=a["state_gdn"][0], state_hgrn=a["state_hgrn"][0],
        state_rwkv=a["state_rwkv"][0].reshape(DEPTH, 2, 4, 2, RW_D, RW_D).transpose(0, 3, 5, 1, 2, 4)
        .reshape(DEPTH, 2, RW_D, 8, RW_D),
        keys_t=a["peer_keys"].reshape(DEPTH, 2 * HEADS, NKEYS, HALF).transpose(0, 3, 1, 2),
        peer_u=a["peer_u"].reshape(DEPTH * N_EXPERTS, D), peer_v=a["peer_v"].reshape(DEPTH * N_EXPERTS, D))
    arrays = {f"in_{k}": np.ascontiguousarray(v) for k, v in arrays.items()}

    Stage.count = 0
    nc = _bacc.Bacc("TRN2", target_bir_lowering=False, num_devices=1)
    e = {k[3:]: nc.dram_tensor(k, v.shape, mybir.dt.from_np(v.dtype), kind="ExternalInput").ap()
         for k, v in arrays.items()}
    e.update({k: nc.dram_tensor(f"scratch_{k}", v, F32).ap() for k, v in SCRATCH.items()})
    e["EIDX"] = nc.dram_tensor("scratch_EIDX", (CTX + LAT, PICKS), I32).ap()
    e.update({k: nc.dram_tensor(f"out_{k}", v, F32, kind="ExternalOutput").ap() for k, v in OUTPUTS.items()})
    build(nc, named(**e))
    got = _run(nc, [arrays], core_ids=[0]).results[0]
    out = {k: got[f"out_{k}"] for k in OUTPUTS}
    rwkv = out["new_rwkv"].reshape(DEPTH, 2, RW_D, 2, 4, RW_D).transpose(0, 3, 4, 1, 5, 2)
    return (out["y_prompt"][None], out["y_sample"][None], out["new_gdn"][None], out["new_hgrn"][None],
            np.ascontiguousarray(rwkv.reshape(1, DEPTH, 2, RW_H, RW_D, RW_D)), out["new_k"][None],
            out["new_v"][None])
```

```python
from collections import namedtuple
from contextlib import ExitStack

import numpy as np
import concourse.bass as bass
from concourse import mybir

F32 = mybir.dt.float32
I32 = mybir.dt.int32
F32R = mybir.dt.float32r
U32 = mybir.dt.uint32
ALU = mybir.AluOpType
ACT = mybir.ActivationFunctionType
AX = mybir.AxisListType

P = 128
D = 1024
KD = D // P
DEPTH = 2
CTX, LAT = 128, 512
TILES = (CTX + LAT) // P
LAT_TILES = LAT // P
GRID_W = 64
CHUNK = 512
GD_H = HG_H = 4
NA_H, NA_D = 8, 64
NA_WC = 16
RW_H, RW_D = 8, 64
RW = RW_H * RW_D
N_BRANCH, BRANCH_W = 4, 512
HEADS, NKEYS, TOPK = 8, 128, 16
HALF = 128
PICKS = HEADS * TOPK
N_EXPERTS = NKEYS * NKEYS
LN_EPS, NORM_EPS, RW_GN_EPS = 1e-5, 1e-6, 64e-5
ALPHA = float((2.0 * DEPTH) ** 0.25)

WIDTHS = (('gdn_qkv', 1536), ('gdn_g', 512), ('gdn_a', 8), ('gdn_b', 8), ('na_q', 512), ('na_k', 512),
          ('na_v', 512), ('hg_q', 512), ('hg_f', 1024), ('hg_i', 512), ('hg_g', 512), ('rw', 1856),
          ('merge', 4096))
COL, IN_W = {}, 0
for _name, _w in WIDTHS:
    COL[_name] = IN_W
    IN_W += _w
RW_W = 1856

ROW_CTX, ROW_LAT = 1, 2 + CTX
P_ROWS = 3 + CTX + LAT
LEVELS = 7


class Stage:

    count = 0

    def __init__(self, nc, name):
        self.nc, self.name, self.ctx, self.sems = nc, f"{name}{Stage.count}", ExitStack(), []
        Stage.count += 1

    def __enter__(self):
        return self

    def sb(self, name, shape, dt=F32):
        return self.ctx.enter_context(self.nc.sbuf_tensor(f"{self.name}_{name}", shape, dt))

    def ps(self, name, shape, dt=F32):
        return self.ctx.enter_context(self.nc.psum_tensor(f"{self.name}_{name}", shape, dt))

    def sem(self, name):
        self.sems.append(self.ctx.enter_context(self.nc.semaphore(f"{self.name}_{name}")))
        return self.sems[-1]

    def __exit__(self, *exc):
        if exc[0] is None:
            for s in self.sems:
                self.nc.gpsimd.sem_clear(s)
            self.nc.all_engine_barrier()
            self.ctx.close()


class Chain:

    def __init__(self, eng, sem):
        self.eng, self.sem, self.n = eng, sem, 0

    def __call__(self, ins):
        self.n += 1
        ins.then_inc(self.sem, 1)
        self.eng.wait_ge(self.sem, self.n)


class Loads:

    def __init__(self, eng, sem):
        self.eng, self.sem, self.n = eng, sem, 0

    def __call__(self, dst, src):
        self.n += 1
        self.eng.dma_start(dst, src).then_inc(self.sem, 16)

    def wait(self):
        self.eng.wait_ge(self.sem, 16 * self.n)


def named(**items):
    return namedtuple("Named", items)(**items)


def rows(ap, start, size=P):
    return ap[bass.ds(start, size), :]


def start_stage(nc, e):
    with Stage(nc, "start") as st:
        zeros = st.sb("zeros", [1, IN_W])
        s_zero, s_dma = st.sem("zero"), st.sem("dma")
        with nc.Block() as block:
            @block.vector
            def _(dve):
                dve.memset(zeros[:], 0.0).then_inc(s_zero, 1)

            @block.sync
            def _(sp):
                ld = Loads(sp, s_dma)
                ld(e.X[0:CTX, :], e.x_prompt)
                ld(e.X[CTX:, :], e.x_sample)
                sp.wait_ge(s_zero, 1)
                for r in (0, ROW_LAT - 1, P_ROWS - 1):
                    ld(e.PR[r:r + 1, :], zeros[:])
                ld.wait()


def mod_stage(nc, e, l):
    n_chunks = 6 * D // CHUNK
    with Stage(nc, "mod") as st:
        c_in, c_sig = st.sb("c_in", [P, KD, 2]), st.sb("c_sig", [P, KD, 2])
        w = st.sb("w", [P, 2, KD, CHUNK])
        bias, mod = st.sb("bias", [2, 6 * D]), st.sb("mod", [2, 6 * D])
        lg, lb = st.sb("lg", [1, 2, 512]), st.sb("lb", [1, 4, 512])
        ps = st.ps("ps", [P, 2, CHUNK])
        s_in, s_w, s_out = st.sem("in"), [st.sem("w0"), st.sem("w1")], st.sem("out")
        s_sig, s_silu, s_mm, s_add = st.sem("sig"), st.sem("silu"), st.sem("mm"), st.sem("add")
        s_diff, s_lb, s_dve, s_scaled = st.sem("diff"), st.sem("lbsig"), st.sem("dve"), st.sem("scaled")
        with nc.Block() as block:
            @block.sync
            def _(sp):
                ld = Loads(sp, s_in)
                ld(c_in[:], e.c_cols)
                for g in range(2):
                    ld(bias[g:g + 1, :], e.b_mod[l, :].unsqueeze(0))
                ld(lg[:], e.hg_lb_logits.unsqueeze(0))
                for j in range(n_chunks):
                    if j >= 2:
                        sp.wait_ge(s_mm, j - 1)
                    sp.dma_start(w[:, j % 2], e.w_mod[l, :, j * CHUNK:(j + 1) * CHUNK]
                                 .rearrange("(k p) n -> p k n", p=P)).then_inc(s_w[j % 2], 16)
                sp.wait_ge(s_scaled, 1)
                out = Loads(sp, s_out)
                for m in range(TILES):
                    g = 0 if m == 0 else 1
                    out(e.MOD[m:m + 1, :], mod[g:g + 1, :])
                out(e.LB.unsqueeze(0), lb[:, 2:4, :])
                out.wait()

            @block.scalar
            def _(act):
                act.wait_ge(s_in, 64)
                act.activation(c_sig[:], c_in[:], ACT.Sigmoid).then_inc(s_sig, 1)
                act.wait_ge(s_diff, 1)
                act.activation(lb[:, 1, :], lb[:, 0, :], ACT.Sigmoid).then_inc(s_lb, 1)

            @block.tensor
            def _(pe):
                pe.wait_ge(s_silu, 1)
                for j in range(n_chunks):
                    pe.wait_ge(s_w[j % 2], 16 * (j // 2 + 1))
                    if j >= 2:
                        pe.wait_ge(s_add, j - 1)
                    for k in range(KD):
                        mm = pe.matmul(ps[0:2, j % 2, :], c_in[:, k, :], w[:, j % 2, k, :],
                                       start=(k == 0), stop=(k == KD - 1))
                    mm.then_inc(s_mm, 1)

            @block.vector
            def _(dve):
                step = Chain(dve, s_dve)
                dve.wait_ge(s_in, 64)
                dve.tensor_tensor(lb[:, 0, :], lg[:, 1, :], lg[:, 0, :], ALU.subtract).then_inc(s_diff, 1)
                dve.wait_ge(s_sig, 1)
                dve.tensor_tensor(c_in[:], c_in[:], c_sig[:], ALU.mult).then_inc(s_silu, 1)
                dve.wait_ge(s_lb, 1)
                step(dve.memset(lb[:, 2, :], 0.0))
                step(dve.tensor_copy(lb[:, 3, :], lb[:, 1, :]))
                for j in range(n_chunks):
                    cols = slice(j * CHUNK, (j + 1) * CHUNK)
                    dve.wait_ge(s_mm, j + 1)
                    dve.tensor_tensor(mod[:, cols], ps[0:2, j % 2, :], bias[:, cols], ALU.add).then_inc(s_add, 1)
                dve.wait_ge(s_add, n_chunks)
                for part in (1, 4):
                    ins = dve.tensor_scalar(mod[:, part * D:(part + 1) * D], mod[:, part * D:(part + 1) * D],
                                            1.0, None, ALU.add)
                    if part == 1:
                        step(ins)
                ins.then_inc(s_scaled, 1)


def project_stage(nc, e, l, part, w_src, n_cols, dst_lat, dst_ctx):
    sizes = [CHUNK] * (n_cols // CHUNK) + ([n_cols % CHUNK] if n_cols % CHUNK else [])
    n = len(sizes)
    n_pairs = n // 2
    assert n % 2 == 0 and n_pairs >= 2
    size = lambda last, b: sizes[-2 + b] if last else CHUNK

    def in_pairs(eng, body):
        body(0, True, False)
        if n_pairs > 2:
            body(1, False, False)
        if n_pairs > 3:
            with eng.Fori(2, n_pairs - 1) as g:
                body(g, False, False)
        body(n_pairs - 1, False, True)

    with Stage(nc, "proj") as st:
        x = st.sb("x", [P, TILES, D])
        h = st.sb("h", [P, 2, CHUNK])
        hT, hT_low = st.sb("hT", [P, KD, TILES * P], F32R), st.sb("hTl", [P, KD, TILES * P], F32R)
        mrows, mcols = st.sb("mrows", [4 * KD, P]), st.sb("mcols", [P, 2, 2, KD])
        ident = st.sb("ident", [P, P])
        w, dist = st.sb("w", [P, 2, KD, CHUNK]), st.sb("dist", [P, KD // 2, CHUNK])
        w_high, w_low = st.sb("wh", [P, 2, KD, CHUNK], F32R), st.sb("wl", [P, 2, KD, CHUNK], F32R)
        o = st.sb("o", [P, 2, TILES, CHUNK])
        ps = st.ps("ps", [P, TILES, CHUNK])
        pt = st.ps("pt", [P, 2, CHUNK])
        s_in, s_w, s_out = st.sem("in"), [st.sem("w0"), st.sem("w1")], [st.sem("o0"), st.sem("o1")]
        s_mt, s_mc = st.sem("mt"), st.sem("mc")
        s_t, s_h, s_mm, s_a, s_v = st.sem("t"), st.sem("h"), st.sem("mm"), st.sem("a"), st.sem("v")
        s_high, s_low, s_dve, s_dist = st.sem("high"), st.sem("low"), st.sem("dve"), st.sem("dist")
        groups = [(0, 0), (1, 0), (1, 1)]
        ev = [[m for m in range(TILES) if m % 2 == k] for k in range(2)]
        with nc.Block() as block:
            @block.sync
            def _(sp):
                ld = Loads(sp, s_in)
                ld(ident[:], e.ident)
                ld(x[:], e.X.rearrange("(m p) d -> p m d", p=P))
                for g in range(2):
                    ld(mrows[2 * KD * g:2 * KD * (g + 1), :],
                       e.MOD[g, part * D:(part + 2) * D].rearrange("(k p) -> k p", p=P))

                def store(j):
                    sp.wait_ge(s_a, len(ev[0]) * (j + 1))
                    sp.wait_ge(s_v, len(ev[1]) * (j + 1))
                    cols = slice(j * CHUNK, j * CHUNK + sizes[j])
                    sp.dma_start(dst_ctx[:, cols], o[:, j % 2, 0, 0:sizes[j]]).then_inc(s_out[j % 2], 16)
                    sp.dma_start(dst_lat[:, cols].rearrange("(m p) n -> p m n", p=P),
                                 o[:, j % 2, 1:TILES, 0:sizes[j]]).then_inc(s_out[j % 2], 16)

                for j in range(n):
                    if j >= 2:
                        sp.wait_ge(s_low, j - 1)
                    sp.dma_start(w[:, j % 2, :, 0:sizes[j]], w_src[:, j * CHUNK:j * CHUNK + sizes[j]]
                                 .rearrange("(k p) n -> p k n", p=P)).then_inc(s_w[j % 2], 16)
                    if j >= 2:
                        store(j - 2)
                for j in range(n - 2, n):
                    store(j)
                for b in range(2):
                    sp.wait_ge(s_out[b], 32 * n_pairs)

            @block.tensor
            def _(pe):
                pe.wait_ge(s_in, 16 * 4)
                pe.transpose(ps[:, 0, 0:4 * KD], mrows[:], ident[0:4 * KD, 0:4 * KD]).then_inc(s_mt, 1)
                for i in range(2 * TILES):
                    m, half = i // 2, i % 2
                    if i >= 2:
                        pe.wait_ge(s_h, i - 1)
                    for q in range(4):
                        t = pe.transpose(pt[:, i % 2, q * P:(q + 1) * P],
                                         x[:, m, (4 * half + q) * P:(4 * half + q + 1) * P], ident[:])
                    t.then_inc(s_t, 1)
                pe.wait_ge(s_h, 2 * TILES)

                def multiply(g, first, last):
                    for b in range(2):
                        width = size(last, b)
                        pe.wait_ge(s_high, 4 * g + (2 * b + 2))
                        pe.wait_ge(s_low, 2 * g + (b + 1))
                        for m in range(TILES):
                            if not first or b:
                                mine = len(ev[m % 2])
                                pe.wait_ge((s_a, s_v)[m % 2], 2 * mine * g + (mine * (b - 1) + m // 2 + 1))
                            for k in range(KD):
                                products = ((hT, w_low), (hT, w_high), (hT_low, w_high))
                                for n_product, (ours, theirs) in enumerate(products):
                                    mm = pe.matmul(ps[:, m, 0:width], ours[:, k, m * P:(m + 1) * P],
                                                   theirs[:, b, k, 0:width], start=(k == 0 and n_product == 0),
                                                   stop=(k == KD - 1 and n_product == 2))
                            mm.then_inc(s_mm, 1)

                in_pairs(pe, multiply)

            def read_out(eng, copy, which, s, g, b, width, first):
                if not first:
                    eng.wait_ge(s_out[b], 32 * g)
                for m in ev[which]:
                    eng.wait_ge(s_mm, 2 * TILES * g + (TILES * b + m + 1))
                    copy(o[:, b, m, 0:width], ps[:, m, 0:width]).then_inc(s, 1)

            @block.gpsimd
            def _(pool):
                def split_low(g, first, last):
                    for b in range(2):
                        cols = slice(0, size(last, b))
                        pool.wait_ge(s_high, 4 * g + (2 * b + 2))
                        if not first:
                            pool.wait_ge(s_mm, 2 * TILES * g + TILES * (b - 1))
                        pool.tensor_tensor(w_low[:, b, :, cols], w[:, b, :, cols], w_high[:, b, :, cols],
                                           ALU.subtract).then_inc(s_low, 1)

                in_pairs(pool, split_low)

            @block.vector
            def _(dve):
                step = Chain(dve, s_dve)

                def high(dst, src, scratch):
                    step(dve.scalar_tensor_tensor(out=scratch, in0=src, scalar=4097.0, in1=src, op0=ALU.mult,
                                                  op1=ALU.subtract))
                    return dve.scalar_tensor_tensor(out=dst, in0=src, scalar=4097.0, in1=scratch, op0=ALU.mult,
                                                    op1=ALU.subtract)

                dve.wait_ge(s_mt, 1)
                dve.tensor_copy(mcols[:].rearrange("p g w k -> p (g w k)"), ps[:, 0, 0:4 * KD]).then_inc(s_mc, 1)
                dve.wait_ge(s_mc, 1)
                four_blocks = lambda ap: ap.rearrange("p (q t) -> p q t", q=4)
                for i in range(2 * TILES):
                    m, half = i // 2, i % 2
                    g = 0 if m == 0 else 1
                    dve.wait_ge(s_t, i + 1)
                    for q in range(4):
                        k = 4 * half + q
                        ins = dve.tensor_scalar(h[:, 0, q * P:(q + 1) * P], pt[:, i % 2, q * P:(q + 1) * P],
                                                mcols[:, g, 1, k:k + 1], mcols[:, g, 0, k:k + 1], ALU.mult, ALU.add)
                    step(ins)
                    here = slice(4 * half, 4 * half + 4), slice(m * P, (m + 1) * P)
                    step(high(hT[:, here[0], here[1]], four_blocks(h[:, 0, :]), four_blocks(h[:, 1, :])))
                    dve.tensor_tensor(hT_low[:, here[0], here[1]], four_blocks(h[:, 0, :]),
                                      hT[:, here[0], here[1]], ALU.subtract).then_inc(s_h, 1)
                    dve.wait_ge(s_h, i + 1)

                def split_high(g, first, last):
                    for b in range(2):
                        dve.wait_ge(s_w[b], 16 * g + 16)
                        if not first:
                            dve.wait_ge(s_mm, 2 * TILES * g + TILES * (b - 1))
                        for half in range(2):
                            blocks, cols = slice(half * KD // 2, (half + 1) * KD // 2), slice(0, size(last, b))
                            if not (first and b == half == 0):
                                dve.wait_ge(s_high, 4 * g + (2 * b + half))
                            dve.scalar_tensor_tensor(out=dist[:, :, cols], in0=w[:, b, blocks, cols], scalar=4097.0,
                                                     in1=w[:, b, blocks, cols], op0=ALU.mult, op1=ALU.subtract)\
                               .then_inc(s_dist, 1)
                            dve.wait_ge(s_dist, 4 * g + (2 * b + half + 1))
                            dve.scalar_tensor_tensor(out=w_high[:, b, blocks, cols], in0=w[:, b, blocks, cols],
                                                     scalar=4097.0, in1=dist[:, :, cols], op0=ALU.mult,
                                                     op1=ALU.subtract).then_inc(s_high, 1)
                        if b:
                            read_out(dve, dve.tensor_copy, 1, s_v, g, 0, size(last, 0), first)
                        elif not first:
                            read_out(dve, dve.tensor_copy, 1, s_v, g - 1, 1, CHUNK, isinstance(g, int) and g == 1)

                in_pairs(dve, split_high)
                read_out(dve, dve.tensor_copy, 1, s_v, n_pairs - 1, 1, sizes[-1], False)

            @block.scalar
            def _(act):
                def read_both(g, first, last):
                    for b in range(2):
                        read_out(act, act.copy, 0, s_a, g, b, size(last, b), first)

                in_pairs(act, read_both)


class Route:
    HP = 2 * HEADS
    LOADS = 5

    def __init__(self, st, e, l, tile):
        HP = self.HP
        self.e, self.l, self.tile = e, l, tile
        self.q, self.qT, self.keys = (st.sb(n, [P, HP, P]) for n in ("q", "qT", "keys"))
        self.ident, self.base, self.iota = st.sb("ident", [P, P]), st.sb("base", [P, 1]), st.sb("iota", [P, TOPK])
        self.sc, self.left = st.sb("sc", [P, HP, NKEYS]), st.sb("left", [P, NKEYS])
        self.sv, self.si = st.sb("sv", [P, HP, TOPK]), st.sb("si", [P, HP, TOPK], U32)
        self.cand, self.cleft = st.sb("cand", [P, HEADS, TOPK, TOPK]), st.sb("cleft", [P, TOPK * TOPK])
        self.best, self.pos = st.sb("best", [P, HEADS, TOPK]), st.sb("pos", [P, HEADS, TOPK], U32)
        self.part, self.partf = st.sb("part", [P, 2, PICKS], U32), st.sb("partf", [P, 2, PICKS])
        self.sif, self.ids = st.sb("sif", [P, HP, TOPK]), st.sb("ids", [P, 3, PICKS])
        self.hot, self.idx = st.sb("hot", [P, PICKS, TOPK]), st.sb("ridx", [P, PICKS], I32)
        self.ex, self.tot = st.sb("ex", [P, HEADS, TOPK]), st.sb("tot", [P, 2, HEADS])
        self.pt, self.ps = st.ps("pt", [P, 4, CHUNK]), st.ps("ps", [P, 4, CHUNK])
        self.s = named(**{n: st.sem("r" + n) for n in "load t q mm sc dve best exp idx g out".split()})

    def load(self, sp):
        ld, e, l = Loads(sp, self.s.load), self.e, self.l
        ld(self.ident[:], e.ident)
        ld(self.q[:].rearrange("p a b -> p (a b)"), rows(e.QH, self.tile * P))
        ld(self.keys[:], e.keys_t[l])
        ld(self.base[:], e.layer_base[l])
        ld(self.iota[:], e.iota16)

    def store(self, sp):
        sp.wait_ge(self.s.idx, 1)
        out = Loads(sp, self.s.out)
        out(rows(self.e.EIDX, self.tile * P), self.idx[:])
        sp.wait_ge(self.s.g, 1)
        out(rows(self.e.G, self.tile * P), self.ex[:].rearrange("p h k -> p (h k)"))
        out.wait()

    def tensor(self, pe):
        s = self.s
        pe.wait_ge(s.load, 16 * self.LOADS)
        for b in range(self.HP):
            t = pe.transpose(self.pt[:, b // 4, (b % 4) * P:(b % 4 + 1) * P], self.q[:, b, :], self.ident[:])
            if b % 4 == 3:
                t.then_inc(s.t, 1)
        for b in range(self.HP):
            if b % 4 == 0:
                pe.wait_ge(s.q, b // 4 + 1)
            mm = pe.matmul(self.ps[:, b // 4, (b % 4) * P:(b % 4 + 1) * P], self.qT[:, b, :], self.keys[:, b, :],
                           start=True, stop=True)
            if b % 4 == 3:
                mm.then_inc(s.mm, 1)

    def read_scores(self, act):
        s = self.s
        for b in range(4):
            act.wait_ge(s.t, b + 1)
            act.copy(self.qT[:, 4 * b:4 * b + 4, :].rearrange("p a b -> p (a b)"), self.pt[:, b, :]).then_inc(s.q, 1)
        for b in range(4):
            act.wait_ge(s.mm, b + 1)
            act.copy(self.sc[:, 4 * b:4 * b + 4, :].rearrange("p a b -> p (a b)"), self.ps[:, b, :]).then_inc(s.sc, 1)

    def exponentials(self, act):
        s = self.s
        act.wait_ge(s.best, 1)
        act.activation(self.ex[:], self.best[:], ACT.Exp).then_inc(s.exp, 1)

    def vector(self, dve):
        s, HP, LOW = self.s, self.HP, -3.0e38
        step = Chain(dve, s.dve)
        wide16 = [P, HEADS, TOPK, TOPK]

        def top16(vals, left, v16, i16):
            step(dve.max(v16[:, 0:8], vals))
            step(dve.max_index(i16[:, 0:8], v16[:, 0:8], vals))
            step(dve.match_replace(left, v16[:, 0:8], vals, LOW))
            step(dve.max(v16[:, 8:16], left))
            step(dve.max_index(i16[:, 8:16], v16[:, 8:16], left))

        for b in range(HP):
            dve.wait_ge(s.sc, b // 4 + 1)
            top16(self.sc[:, b, :], self.left[:], self.sv[:, b, :], self.si[:, b, :])
            yield
        cand, best, pos, hot, ids, ex, tot = self.cand, self.best, self.pos, self.hot, self.ids, self.ex, self.tot
        svh = self.sv[:].rearrange("p (h s) k -> p h s k", s=2)
        step(dve.tensor_tensor(cand[:], svh[:, :, 0, :].unsqueeze(3).to_broadcast(wide16),
                               svh[:, :, 1, :].unsqueeze(2).to_broadcast(wide16), ALU.add))
        yield
        for h in range(HEADS):
            top16(cand[:, h].rearrange("p a b -> p (a b)"), self.cleft[:], best[:, h, :], pos[:, h, :])
            yield
        step(dve.tensor_copy(tot[:, 0, :], best[:, :, 0]))
        dve.tensor_tensor(best[:], best[:], tot[:, 0, :].unsqueeze(2).to_broadcast([P, HEADS, TOPK]),
                          ALU.subtract).then_inc(s.best, 1)
        posf, part = pos[:].rearrange("p h k -> p (h k)"), self.part
        step(dve.tensor_single_scalar(part[:, 0, :], posf, 4, ALU.logical_shift_right))
        step(dve.tensor_single_scalar(part[:, 1, :], posf, 15, ALU.bitwise_and))
        step(dve.tensor_copy(self.partf[:], part[:]))
        step(dve.tensor_copy(self.sif[:], self.si[:]))
        yield
        sih = self.sif[:].rearrange("p (h s) k -> p h s k", s=2)
        hv = hot[:].rearrange("p (h k) c -> p h k c", h=HEADS)
        for k in range(2):
            step(dve.tensor_tensor(hot[:], self.partf[:, k, :].unsqueeze(2).to_broadcast([P, PICKS, TOPK]),
                                   self.iota[:].unsqueeze(1).to_broadcast([P, PICKS, TOPK]), ALU.is_equal))
            yield
            step(dve.tensor_tensor(hv, hv, sih[:, :, k, :].unsqueeze(2).to_broadcast(wide16), ALU.mult))
            yield
            step(dve.tensor_reduce(ids[:, k, :], hot[:], AX.X, ALU.add))
            yield
        step(dve.tensor_scalar(ids[:, 2, :], ids[:, 0, :], float(NKEYS), self.base[:, 0:1], ALU.mult, ALU.add))
        dve.tensor_tensor(self.idx[:], ids[:, 2, :], ids[:, 1, :], ALU.add).then_inc(s.idx, 1)
        dve.wait_ge(s.exp, 1)
        step(dve.tensor_reduce(tot[:, 0, :], ex[:], AX.X, ALU.add))
        step(dve.reciprocal(tot[:, 1, :], tot[:, 0, :]))
        dve.tensor_tensor(ex[:], ex[:], tot[:, 1, :].unsqueeze(2).to_broadcast([P, HEADS, TOPK]),
                          ALU.mult).then_inc(s.g, 1)
        yield


def route_stage(nc, e, l, tile):
    with Stage(nc, "route") as st:
        route = Route(st, e, l, tile)
        with nc.Block() as block:
            @block.sync
            def _(sp):
                route.load(sp)
                route.store(sp)

            @block.tensor
            def _(pe):
                route.tensor(pe)

            @block.scalar
            def _(act):
                route.read_scores(act)
                route.exponentials(act)

            @block.vector
            def _(dve):
                for _ in route.vector(dve):
                    pass


def norm_steps(dve, step, s_var, s_std, t, stats, mv, gamma, beta, base=0):
    for c in range(2):
        step(dve.bn_stats(stats[:, c, :], t[:, c * CHUNK:(c + 1) * CHUNK]))
    step(dve.bn_aggr(mv[:, 0:2], stats[:].rearrange("p c s -> p (c s)")))
    dve.tensor_scalar(mv[:, 2:3], mv[:, 1:2], LN_EPS, None, ALU.add).then_inc(s_var, 1)
    dve.wait_ge(s_std, base + 1)
    step(dve.reciprocal(mv[:, 4:5], mv[:, 3:4]))
    step(dve.tensor_scalar(t[:], t[:], mv[:, 0:1], mv[:, 4:5], ALU.subtract, ALU.mult))
    step(dve.tensor_tensor(t[:], t[:], gamma[:], ALU.mult))
    return dve.tensor_tensor(t[:], t[:], beta[:], ALU.add)


SLOTS = 16


def expert_stage(nc, e, l, i, row, s_rows, first, last):
    route_next = not last
    per_tile = 2 * PICKS // SLOTS
    turn = l * TILES + i
    with Stage(nc, "expert") as st:
        x, h = st.sb("x", [P, D]), st.sb("h", [P, D])
        junk, sums = st.sb("junk", [P, 2, D]), st.sb("sums", [P, 2, D])
        shift, scale, gate, gamma, beta = (st.sb(n, [P, D]) for n in ("shift", "scale", "gate", "gamma", "beta"))
        idx, g = st.sb("idx", [P, PICKS], I32), st.sb("g", [P, PICKS])
        hid, cub, th, wt = (st.sb(n, [P, PICKS]) for n in ("hid", "cub", "th", "wt"))
        stats, mv = st.sb("stats", [P, 2, 6]), st.sb("mv", [P, 5])
        s_idx, s_in, s_used, s_dve, s_cub, s_tanh, s_var, s_std, s_x, s_out = (
            st.sem(n) for n in ("idx", "in", "used", "dve", "cub", "tanh", "var", "std", "x", "out"))
        route = Route(st, e, l, i + 1) if route_next else None
        with nc.Block() as block:
            @block.sync
            def _(sp):
                sp.dma_start(idx[:], rows(e.EIDX, i * P)).then_inc(s_idx, 16)
                ld = Loads(sp, s_in)
                ld(x[:], rows(e.X, i * P))
                for buf, part in ((shift, 3), (scale, 4), (gate, 5)):
                    ld(buf[:], e.MOD[i, part * D:(part + 1) * D].partition_broadcast(P))
                ld(gamma[:], e.ln2_g[l].partition_broadcast(P))
                ld(beta[:], e.ln2_b[l].partition_broadcast(P))
                ld(g[:], rows(e.G, i * P))
                if route_next:
                    route.load(sp)
                    route.store(sp)
                sp.wait_ge(s_x, 1)
                sp.dma_start(rows(e.X, i * P), sums[:, 0, :]).then_inc(s_out, 16)
                sp.wait_ge(s_out, 16)

            @block.gpsimd
            def _(pool):
                def gather(n, idx):
                    k = n % PICKS
                    pool.indirect_dma_start(
                        out=row[:, n % SLOTS, :], out_offset=None, in_=e.peer_u if n < PICKS else e.peer_v,
                        in_offset=bass.IndirectOffsetOnAxis(ap=idx[:, k:k + 1], axis=0),
                    ).then_inc(s_rows[n % SLOTS], 16)

                pool.wait_ge(s_idx, 16)
                for n in range(0 if first else SLOTS, 2 * PICKS):
                    if n >= SLOTS:
                        pool.wait_ge(s_used, n - SLOTS + 1)
                    gather(n, idx)
                if route_next:
                    pool.wait_ge(route.s.idx, 1)
                    for n in range(SLOTS):
                        pool.wait_ge(s_used, 2 * PICKS - SLOTS + n + 1)
                        gather(n, route.idx)

            if route_next:
                @block.tensor
                def _(pe):
                    route.tensor(pe)

            @block.scalar
            def _(act):
                if route_next:
                    route.read_scores(act)
                act.wait_ge(s_cub, 1)
                act.activation(th[:], cub[:], ACT.Tanh, scale=0.7978845608028654).then_inc(s_tanh, 1)
                if route_next:
                    route.exponentials(act)
                act.wait_ge(s_var, 1)
                act.activation(mv[:, 3:4], mv[:, 2:3], ACT.Sqrt).then_inc(s_std, 1)

            @block.vector
            def _(dve):
                step = Chain(dve, s_dve)
                dve.wait_ge(s_in, 16 * 7)
                step(dve.tensor_tensor(h[:], x[:], scale[:], ALU.mult))
                step(dve.tensor_tensor(h[:], h[:], shift[:], ALU.add))

                def arrived(n):
                    dve.wait_ge(s_rows[n % SLOTS], turn * (16 * per_tile) + 16 * (n // SLOTS + 1))

                portions = route.vector(dve) if route_next else iter(())
                for n in range(PICKS):
                    if n >= SLOTS and n % 6 == 2:
                        next(portions, None)
                    arrived(n)
                    if n >= 2:
                        dve.wait_ge(s_used, n - 1)
                    dve.tensor_tensor_reduce(junk[:, n % 2], row[:, n % SLOTS, :], h[:], 1.0, 0.0, ALU.mult, ALU.add,
                                             hid[:, n:n + 1]).then_inc(s_used, 1)
                dve.wait_ge(s_used, PICKS)
                step(dve.tensor_tensor(cub[:], hid[:], hid[:], ALU.mult))
                step(dve.tensor_scalar(cub[:], cub[:], 0.044715, 1.0, ALU.mult, ALU.add))
                dve.tensor_tensor(cub[:], cub[:], hid[:], ALU.mult).then_inc(s_cub, 1)
                step(dve.tensor_tensor(wt[:], hid[:], g[:], ALU.mult))
                dve.wait_ge(s_tanh, 1)
                step(dve.tensor_scalar(th[:], th[:], 0.5, 0.5, ALU.mult, ALU.add))
                step(dve.tensor_tensor(wt[:], wt[:], th[:], ALU.mult))
                for n in range(PICKS, 2 * PICKS):
                    if n % 6 == 2:
                        next(portions, None)
                    arrived(n)
                    k = n - PICKS
                    acc = sums[:, n % 2, :]
                    if k < 2:
                        ins = dve.tensor_scalar(acc, row[:, n % SLOTS, :], wt[:, k:k + 1], None, ALU.mult)
                    else:
                        dve.wait_ge(s_used, n - 1)
                        ins = dve.scalar_tensor_tensor(out=acc, in0=row[:, n % SLOTS, :], scalar=wt[:, k:k + 1],
                                                       in1=acc, op0=ALU.mult, op1=ALU.add)
                    ins.then_inc(s_used, 1)
                assert next(portions, None) is None
                dve.wait_ge(s_used, 2 * PICKS)
                acc = sums[:, 0, :]
                step(dve.tensor_tensor(acc, acc, sums[:, 1, :], ALU.add))
                step(dve.tensor_tensor(acc, acc, gate[:], ALU.mult))
                step(dve.scalar_tensor_tensor(out=acc, in0=x[:], scalar=ALPHA, in1=acc, op0=ALU.mult, op1=ALU.add))
                norm_steps(dve, step, s_var, s_std, acc, stats, mv, gamma, beta).then_inc(s_x, 1)


def merge_stage(nc, e, l):
    CB = BRANCH_W // P
    turns = [("A", 0)]
    for m in range(TILES):
        turns += ([("A", m + 1)] if m + 1 < TILES else []) + [("B", m)]
    with Stage(nc, "merge") as st:
        ident = st.sb("ident", [P, P])
        wb, wo = st.sb("wb", [P, N_BRANCH * CB, D]), st.sb("wo", [P, KD, D])
        y, yT = st.sb("y", [P, 2, N_BRANCH * BRANCH_W]), st.sb("yT", [P, N_BRANCH * CB, P])
        gates, mix, mixT = st.sb("gates", [P, N_BRANCH * D]), st.sb("mix", [P, 2, D]), st.sb("mixT", [P, KD, P])
        tmp, t, x = st.sb("tmp", [P, CHUNK]), st.sb("t", [P, D]), st.sb("x", [P, D])
        gate, gamma, beta = st.sb("gate", [P, D]), st.sb("gamma", [P, D]), st.sb("beta", [P, D])
        stats, mv = st.sb("stats", [P, 2, 6]), st.sb("mv", [P, 5])
        pt, ps = st.ps("pt", [P, 2, CHUNK]), st.ps("ps", [P, 4, CHUNK])
        s_id, s_y = st.sem("id"), [st.sem("y0"), st.sem("y1")]
        s_w = [st.sem(f"w{b}") for b in range(N_BRANCH)]
        s_wo, s_g, s_x, s_out = (st.sem(n) for n in ("wo", "g", "x", "out"))
        s_t, s_tc, s_mm, s_used, s_sig, s_mix = (st.sem(n) for n in ("t", "tc", "mm", "used", "sig", "mix"))
        s_dve, s_var, s_std, s_new, s_a, s_bm = (st.sem(n) for n in ("dve", "var", "std", "new", "a", "bm"))
        with nc.Block() as block:
            @block.sync
            def _(sp):
                sp.dma_start(ident[:], e.ident).then_inc(s_id, 16)

                def load_tile(m):
                    if m >= 2:
                        sp.wait_ge(s_a, m - 1)
                    sp.dma_start(y[:, m % 2], e.Y[m * P:(m + 1) * P, :]).then_inc(s_y[m % 2], 16)
                    if m >= 1:
                        sp.wait_ge(s_mix, m)
                    r = ROW_CTX if m == 0 else ROW_LAT + (m - 1) * P
                    sp.dma_start(gates[:], e.PR[r:r + P, COL['merge']:COL['merge'] + N_BRANCH * D]).then_inc(s_g, 16)

                load_tile(0)
                for b in range(N_BRANCH):
                    sp.dma_start(wb[:, b * CB:(b + 1) * CB, :],
                                 e.w_branch[l, b].rearrange("(c p) d -> p c d", p=P)).then_inc(s_w[b], 16)
                sp.dma_start(wo[:], e.w_out[l].rearrange("(k p) d -> p k d", p=P)).then_inc(s_wo, 16)
                sp.dma_start(gamma[:], e.ln1_g[l].partition_broadcast(P)).then_inc(s_wo, 16)
                sp.dma_start(beta[:], e.ln1_b[l].partition_broadcast(P)).then_inc(s_wo, 16)
                for kind, m in turns:
                    if kind == "A":
                        if m:
                            load_tile(m)
                        continue
                    if m:
                        sp.wait_ge(s_new, m)
                    sp.dma_start(x[:], e.X[m * P:(m + 1) * P, :]).then_inc(s_x, 16)
                    sp.dma_start(gate[:], e.MOD[m, 2 * D:3 * D].partition_broadcast(P)).then_inc(s_x, 16)
                    if m:
                        sp.dma_start(e.X[(m - 1) * P:m * P, :], t[:]).then_inc(s_out, 16)
                sp.wait_ge(s_new, TILES)
                sp.dma_start(e.X[(TILES - 1) * P:, :], t[:]).then_inc(s_out, 16)
                sp.wait_ge(s_out, 16 * TILES)

            @block.tensor
            def _(pe):
                n_t, n_mm = 0, 0
                for kind, m in turns:
                    n_groups = N_BRANCH * CB // 4 if kind == "A" else KD // 4
                    if kind == "A":
                        pe.wait_ge(s_id, 16)
                        pe.wait_ge(s_y[m % 2], 16 * (m // 2 + 1))
                    else:
                        pe.wait_ge(s_mix, m + 1)
                    for q in range(n_groups):
                        if n_t >= 2:
                            pe.wait_ge(s_tc, n_t - 1)
                        src = y[:, m % 2] if kind == "A" else mix[:, m % 2]
                        for c in range(4):
                            tr = pe.transpose(pt[:, n_t % 2, c * P:(c + 1) * P],
                                              src[:, (4 * q + c) * P:(4 * q + c + 1) * P], ident[:])
                        n_t += 1
                        tr.then_inc(s_t, 1)
                    if kind == "A":
                        pe.wait_ge(s_t, n_t)
                        pe.sem_inc(s_a, 1)
                    pe.wait_ge(s_tc, n_t)
                    if kind == "B":
                        pe.wait_ge(s_wo, 48)
                    for b in range(N_BRANCH if kind == "A" else 1):
                        if kind == "A" and m == 0:
                            pe.wait_ge(s_w[b], 16)
                        for half in range(2):
                            if n_mm >= 4:
                                pe.wait_ge(s_used, n_mm - 3)
                            cols = slice(half * CHUNK, (half + 1) * CHUNK)
                            depth = CB if kind == "A" else KD
                            for c in range(depth):
                                lhs = yT[:, b * CB + c, :] if kind == "A" else mixT[:, c, :]
                                rhs = wb[:, b * CB + c, cols] if kind == "A" else wo[:, c, cols]
                                mm = pe.matmul(ps[:, n_mm % 4, :], lhs, rhs, start=(c == 0), stop=(c == depth - 1))
                            n_mm += 1
                            mm.then_inc(s_mm, 1)

            @block.scalar
            def _(act):
                n_t, n_mm = 0, 0
                for kind, m in turns:
                    n_groups = N_BRANCH * CB // 4 if kind == "A" else KD // 4
                    act.wait_ge(s_mm, n_mm)
                    for q in range(n_groups):
                        act.wait_ge(s_t, n_t + 1)
                        dst = yT if kind == "A" else mixT
                        act.copy(dst[:, 4 * q:4 * q + 4, :].rearrange("p a b -> p (a b)"),
                                 pt[:, n_t % 2, :]).then_inc(s_tc, 1)
                        n_t += 1
                    if kind == "A":
                        act.wait_ge(s_g, 16 * (m + 1))
                        act.activation(gates[:], gates[:], ACT.Sigmoid).then_inc(s_sig, 1)
                    n_mm += 2 * N_BRANCH if kind == "A" else 2
                    if kind == "B":
                        act.wait_ge(s_var, m + 1)
                        act.activation(mv[:, 3:4], mv[:, 2:3], ACT.Sqrt).then_inc(s_std, 1)

            @block.vector
            def _(dve):
                step = Chain(dve, s_dve)
                n_mm = 0
                for kind, m in turns:
                    if kind == "A":
                        dve.wait_ge(s_sig, m + 1)
                        for b in range(N_BRANCH):
                            for half in range(2):
                                cols = slice(half * CHUNK, (half + 1) * CHUNK)
                                gcols = slice(b * D + half * CHUNK, b * D + (half + 1) * CHUNK)
                                dve.wait_ge(s_mm, n_mm + 1)
                                dst = mix[:, m % 2, cols] if b == 0 else tmp[:]
                                dve.tensor_tensor(dst, ps[:, n_mm % 4, :], gates[:, gcols], ALU.mult)\
                                   .then_inc(s_used, 1)
                                n_mm += 1
                                dve.wait_ge(s_used, n_mm)
                                if b:
                                    step(dve.tensor_tensor(mix[:, m % 2, cols], mix[:, m % 2, cols], tmp[:],
                                                           ALU.add))
                        dve.sem_inc(s_mix, 1)
                        continue
                    dve.wait_ge(s_x, 32 * (m + 1))
                    dve.wait_ge(s_wo, 48)
                    if m:
                        dve.wait_ge(s_out, 16 * m)
                    for half in range(2):
                        cols = slice(half * CHUNK, (half + 1) * CHUNK)
                        dve.wait_ge(s_mm, n_mm + 1)
                        dve.tensor_tensor(t[:, cols], ps[:, n_mm % 4, :], gate[:, cols], ALU.mult).then_inc(s_used, 1)
                        n_mm += 1
                    dve.wait_ge(s_used, n_mm)
                    step(dve.scalar_tensor_tensor(out=t[:], in0=x[:], scalar=ALPHA, in1=t[:], op0=ALU.mult,
                                                  op1=ALU.add))
                    norm_steps(dve, step, s_var, s_std, t, stats, mv, gamma, beta, base=m).then_inc(s_new, 1)


def attention_stage(nc, e, l):
    B, RB = 4, 15
    units = [(m, h) for m in range(1, TILES) for h in range(NA_H)] + [(0, h) for h in range(NA_H)]
    groups = [(kind, m) for m in range(TILES) for kind in "qk"] + [("k", TILES)]
    KEYS = LAT + P + CTX
    NT = GRID_W // 4
    key_at = lambda m: (m - 1) * P if 1 <= m <= LAT_TILES else (LAT + P if m == 0 else LAT)
    q_at = lambda m: m * P
    with Stage(nc, "na") as st:
        ident = st.sb("ident", [P, P])
        x, kc = st.sb("x", [P, TILES, 3 * 512]), st.sb("kc", [P, 512])
        vc = st.sb("vc", [P, 512])
        qT, kT = st.sb("qT", [P, B, TILES * P]), st.sb("kT", [P, B, KEYS])
        rpb, shift = st.sb("rpb", [32, NA_H * RB]), st.sb("shift", [32, GRID_W * P])
        bias = st.sb("bias", [P, NA_H, RB + 1, GRID_W])
        s, pT = st.sb("s", [P, 2, 640]), st.sb("pT", [P, 2, 640])
        nmax, tot = st.sb("nmax", [P, 40]), st.sb("tot", [P, 2, 40])
        y = st.sb("y", [P, TILES, 512])
        ps, pt, po = st.ps("ps", [P, 2, 2, CHUNK]), st.ps("pt", [P, 2, CHUNK]), st.ps("po", [P, 2, CHUNK])
        s_one, s_b, s_x, s_kc, s_out = (st.sem(n) for n in ("one", "b", "x", "kc", "out"))
        s_bias, s_blo, s_bhi, s_t, s_tc = (st.sem(n) for n in ("bias", "blo", "bhi", "t", "tc"))
        s_s, s_add, s_ctx, s_max, s_exp, s_rec, s_p, s_pc, s_pv, s_y = (
            st.sem(n) for n in ("s", "add", "ctx", "max", "exp", "rec", "p", "pc", "pv", "y"))
        with nc.Block() as block:
            @block.sync
            def _(sp):
                sp.wait_ge(s_one, 1)
                b = Loads(sp, s_b)
                b(ident[:], e.ident)
                b(rpb[1:32, :], e.rpb_t[l])
                b(shift[:], e.key_shift)
                ld = Loads(sp, s_x)
                cols = slice(COL['na_q'], COL['na_q'] + 1536)
                ld(x[:, 0, :], e.PR[ROW_CTX:ROW_CTX + CTX, cols])
                ld(x[:, 1:, :], e.PR[ROW_LAT:ROW_LAT + LAT, cols].rearrange("(m p) n -> p m n", p=P))
                kc_ld = Loads(sp, s_kc)
                kc_ld(kc[:].rearrange("p (h d) -> p h d", h=NA_H), e.cache_k[l].rearrange("h j d -> j h d"))
                kc_ld(vc[:].rearrange("p (h d) -> p h d", h=NA_H), e.cache_v[l].rearrange("h j d -> j h d"))
                out = Loads(sp, s_out)
                for k, dst in ((1, e.new_k), (2, e.new_v)):
                    c0 = COL['na_q'] + 512 * k
                    out(dst[l].rearrange("h j d -> j h d"),
                        e.PR[ROW_CTX:ROW_CTX + CTX, c0:c0 + 512].rearrange("j (h d) -> j h d", h=NA_H))
                for n, m in enumerate(list(range(1, TILES)) + [0]):
                    sp.wait_ge(s_y, NA_H * (n + 1))
                    out(e.Y[m * P:(m + 1) * P, 512:1024], y[:, m, :])
                out.wait()

            @block.tensor
            def _(pe):
                pe.wait_ge(s_b, 48)
                for n in range(NT):
                    if n >= 2:
                        pe.wait_ge(s_blo, n - 1)
                        pe.wait_ge(s_bhi, n - 1)
                    for c in range(4):
                        ck = 4 * n + c
                        mm = pe.matmul(po[:, n % 2, c * 120:(c + 1) * 120], shift[:, ck * P:(ck + 1) * P], rpb[:],
                                       start=True, stop=True)
                    mm.then_inc(s_bias, 1)
                pe.wait_ge(s_x, 32)
                pe.wait_ge(s_kc, 32)
                for n, (kind, m) in enumerate(groups):
                    if n >= 2:
                        pe.wait_ge(s_tc, n - 1)
                    for c in range(B):
                        src = kc[:, c * P:(c + 1) * P] if m == TILES else \
                            x[:, m, (0 if kind == "q" else 512) + c * P:][:, 0:P]
                        tr = pe.transpose(pt[:, n % 2, c * P:(c + 1) * P], src, ident[:])
                    tr.then_inc(s_t, 1)
                pe.wait_ge(s_tc, len(groups))

                def scores(u):
                    m, h = units[u]
                    r = slice(64 * (h % 2), 64 * (h % 2) + 64)
                    if u >= 2:
                        pe.wait_ge(s_add, u - 1)
                        pe.wait_ge(s_ctx, u - 1)
                    q = qT[r, h // 2, q_at(m):q_at(m) + P]
                    if m:
                        pe.matmul(ps[:, u % 2, 0, :], q, kT[r, h // 2, 0:LAT], start=True, stop=True)
                    k0 = LAT if m else LAT + P
                    pe.matmul(ps[:, u % 2, 1, 0:P], q, kT[r, h // 2, k0:k0 + P], start=True, stop=True)\
                      .then_inc(s_s, 1)

                def values(u):
                    m, h = units[u]
                    blocks = range(5) if m else [4]
                    pe.wait_ge(s_exp, u + 1)
                    if u >= 1:
                        pe.wait_ge(s_pc, u)
                    for b in blocks:
                        tr = pe.transpose(pt[:, b // 4, (b % 4) * P:(b % 4 + 1) * P], s[:, u % 2, b * P:(b + 1) * P],
                                          ident[:])
                    tr.then_inc(s_p, 1)
                    pe.wait_ge(s_pc, u + 1)
                    if u >= 2:
                        pe.wait_ge(s_y, u - 1)
                    for b in blocks:
                        v = x[:, b + 1, 1024 + h * NA_D:1024 + (h + 1) * NA_D] if b < 4 else \
                            (vc[:, h * NA_D:(h + 1) * NA_D] if m else x[:, 0, 1024 + h * NA_D:1024 + (h + 1) * NA_D])
                        mm = pe.matmul(po[:, u % 2, 0:NA_D], pT[:, u % 2, b * P:(b + 1) * P], v,
                                       start=(b == blocks[0]), stop=(b == 4))
                    mm.then_inc(s_pv, 1)

                for u in range(len(units) + 1):
                    if u < len(units):
                        scores(u)
                    if u:
                        values(u - 1)

            def keep_bias(eng, copy, half, s_done):
                r = slice(64 * half, 64 * half + 64)
                for n in range(NT):
                    eng.wait_ge(s_bias, n + 1)
                    copy(bias[r, :, half:half + RB, 4 * n:4 * n + 4],
                         po[r, n % 2, 0:480].rearrange("p (c h r) -> p h r c", c=4, h=NA_H)).then_inc(s_done, 1)

            @block.scalar
            def _(act):
                keep_bias(act, act.copy, 0, s_blo)
                for n, (kind, m) in enumerate(groups):
                    act.wait_ge(s_t, n + 1)
                    if kind == "q":
                        ins = act.mul(qT[:, :, q_at(m):q_at(m) + P],
                                      pt[:, n % 2, :].rearrange("p (c t) -> p c t", c=B), float(NA_D) ** -0.5)
                    else:
                        ins = act.copy(kT[:, :, key_at(m):key_at(m) + P],
                                       pt[:, n % 2, :].rearrange("p (c t) -> p c t", c=B))
                    ins.then_inc(s_tc, 1)

                def copy_scores(u):
                    act.wait_ge(s_s, u + 1)
                    if u >= 2:
                        act.wait_ge(s_p, u - 1)
                    act.copy(s[:, u % 2, 512:640], ps[:, u % 2, 1, 0:P]).then_inc(s_ctx, 1)

                def exponent(u):
                    part = slice(0, 640) if units[u][0] else slice(512, 640)
                    act.wait_ge(s_max, u + 1)
                    act.activation(s[:, u % 2, part], s[:, u % 2, part], ACT.Exp, bias=nmax[:, u:u + 1],
                                   accum_out=tot[:, 0, u:u + 1]).then_inc(s_exp, 1)

                def copy_probs(u):
                    m, h = units[u]
                    act.wait_ge(s_p, u + 1)
                    if u >= 2:
                        act.wait_ge(s_pv, u - 1)
                    part = slice(0, 640) if m else slice(512, 640)
                    act.copy(pT[:, u % 2, part], pt[:].rearrange("p a b -> p (a b)")[:, part]).then_inc(s_pc, 1)

                copy_scores(0)
                for u in range(len(units)):
                    exponent(u)
                    if u + 1 < len(units):
                        copy_scores(u + 1)
                    copy_probs(u)

            @block.vector
            def _(dve):
                dve.memset(rpb[:], 1.0).then_inc(s_one, 1)
                keep_bias(dve, dve.tensor_copy, 1, s_bhi)
                dve.wait_ge(s_bhi, NT)
                dve.wait_ge(s_blo, NT)

                def out_rows(u):
                    m, h = units[u]
                    dve.wait_ge(s_rec, u + 1)
                    dve.wait_ge(s_pv, u + 1)
                    dve.tensor_scalar(y[:, m, h * NA_D:(h + 1) * NA_D], po[:, u % 2, 0:NA_D], tot[:, 1, u:u + 1],
                                      None, ALU.mult).then_inc(s_y, 1)

                for u, (m, h) in enumerate(units):
                    dve.wait_ge(s_s, u + 1)
                    if u >= 2:
                        dve.wait_ge(s_p, u - 1)
                    if m:
                        d0 = 7 - 2 * (m - 1)
                        dve.tensor_tensor(s[:, u % 2, 0:512], ps[:, u % 2, 0, :],
                                          bias[:, h, d0:d0 + 8, :].rearrange("p r c -> p (r c)"), ALU.add)\
                           .then_inc(s_add, 1)
                    else:
                        dve.sem_inc(s_add, 1)
                    dve.wait_ge(s_add, u + 1)
                    dve.wait_ge(s_ctx, u + 1)
                    part = slice(0, 640) if m else slice(512, 640)
                    dve.tensor_reduce(nmax[:, u:u + 1], s[:, u % 2, part], AX.X, ALU.max, negate=True)\
                       .then_inc(s_max, 1)
                    dve.wait_ge(s_exp, u + 1)
                    dve.reciprocal(tot[:, 1, u:u + 1], tot[:, 0, u:u + 1]).then_inc(s_rec, 1)
                    if u:
                        out_rows(u - 1)
                out_rows(len(units) - 1)


def wide(ap):
    return ap.unsqueeze(2).to_broadcast([P, 8, P])


def heads(ap):
    return ap.rearrange("p b (h t) -> p (b h) t", h=4)


def per_dir(ap):
    return ap.unsqueeze(2).to_broadcast([P, 2, 4, P])


def four(ap):
    return ap.rearrange("p (d h) t -> p d h t", d=2)


def first_row(m):
    return ROW_CTX if m == 0 else ROW_LAT + (m - 1) * P


def gdn_prepare(nc, e, l):
    W, QK = 1536, 1024
    with Stage(nc, "gprep") as st:
        xs3, cw = st.sb("xs", [P, 3, 3, W]), st.sb("cw", [P, 3, W])
        ab, rate, dtb = st.sb("ab", [P, TILES, 16]), st.sb("rate", [P, 8]), st.sb("dtb", [P, 8])
        rope = st.sb("rope", [P, TILES, 2, 64])
        sig, sq, ss2 = st.sb("sig", [P, W]), st.sb("sq", [P, QK]), st.sb("ss", [P, 2, 4, 8])
        rot, tmp = st.sb("rot", [P, 16, 2, 32]), st.sb("tmp", [P, 2, 16, 32])
        res2, sm = st.sb("res", [P, 2, W]), st.sb("sm", [P, 4, TILES, 8])
        gates = st.sb("gates", [P, TILES, 16])
        names = "weights taps conv sig q ss root t e ln rot turned done out_g dve pool".split()
        s = named(**{n: st.sem(n) for n in names})
        s_load, s_out = [st.sem(f"load{b}") for b in range(3)], [st.sem(f"out{b}") for b in range(2)]
        by_tile = lambda ap: ap.rearrange("(m p) c -> p m c", p=P)

        def table(m, k):
            t = rope[:, m, k, :].rearrange("p (a c) -> p a c", a=2).unsqueeze(1)
            return t.to_broadcast([P, 8, 2, 32])

        ax = lambda t: t.rearrange("p (h a) c -> p h a c", a=2)
        halves = lambda m: xs3[:, m % 3, 0, 0:QK].rearrange("p (g s c) -> p g s c", g=16, s=2)
        with nc.Block() as block:
            @block.sync
            def _(sp):
                def load(m):
                    for j in range(3):
                        sp.dma_start(xs3[:, m % 3, j, :], e.PR[first_row(m) - 1 + j:first_row(m) - 1 + j + P, 0:W])\
                            .then_inc(s_load[m % 3], 16)

                load(0)
                ld = Loads(sp, s.weights)
                ld(cw[:].rearrange("p j w -> p (j w)"),
                   e.gdn_conv[l].rearrange("j w -> (j w)").partition_broadcast(P))
                ab_cols = slice(COL['gdn_a'], COL['gdn_a'] + 16)
                ld(ab[:, 0, :], e.PR[ROW_CTX:ROW_CTX + P, ab_cols])
                ld(ab[:, 1:TILES, :], by_tile(e.PR[ROW_LAT:ROW_LAT + LAT, ab_cols]))
                ld(rate[:], e.gdn_A_log[l].partition_broadcast(P))
                ld(dtb[:], e.gdn_dt_bias[l].partition_broadcast(P))
                ld(rope[:].rearrange("p m a b -> p m (a b)"), by_tile(e.rope))
                load(1)
                load(2)
                for m in range(TILES):
                    sp.wait_ge(s.done, m + 1)
                    sp.dma_start(e.GQ[m * P:(m + 1) * P, 0:W], res2[:, m % 2, :]).then_inc(s_out[m % 2], 16)
                    if m + 3 < TILES:
                        load(m + 3)
                sp.wait_ge(s.q, 2)
                sp.dma_start(by_tile(e.GQ[:, W:W + 16]), gates[:]).then_inc(s.out_g, 16)
                sp.wait_ge(s.out_g, 16)
                for b in range(2):
                    sp.wait_ge(s_out[b], 16 * ((TILES + 1 - b) // 2))

            @block.gpsimd
            def _(pool):
                step = Chain(pool, s.pool)
                pool.wait_ge(s.weights, 96)

                def taps(m):
                    xs = xs3[:, m % 3]
                    pool.wait_ge(s_load[m % 3], 48 * (m // 3 + 1))
                    step(pool.tensor_tensor(xs[:, 1, :], xs[:, 1, :], cw[:, 1, :], ALU.mult))
                    step(pool.tensor_tensor(xs[:, 2, :], xs[:, 2, :], cw[:, 2, :], ALU.mult))
                    pool.tensor_tensor(xs[:, 1, :], xs[:, 1, :], xs[:, 2, :], ALU.add).then_inc(s.taps, 1)

                taps(0)
                for m in range(TILES):
                    if m + 1 < TILES:
                        taps(m + 1)
                    pool.wait_ge(s.rot, m + 1)
                    if m:
                        pool.wait_ge(s.done, m)
                    x1, x2 = halves(m)[:, :, 0, :], halves(m)[:, :, 1, :]
                    step(pool.tensor_tensor(ax(rot[:, :, 1, :]), ax(x1), table(m, 1), ALU.mult))
                    step(pool.tensor_tensor(ax(tmp[:, 1]), ax(x2), table(m, 0), ALU.mult))
                    pool.tensor_tensor(rot[:, :, 1, :], rot[:, :, 1, :], tmp[:, 1], ALU.add).then_inc(s.turned, 1)

            @block.scalar
            def _(act):
                act.wait_ge(s.weights, 96)
                act.activation(rate[:], rate[:], ACT.Exp).then_inc(s.e, 1)
                act.wait_ge(s.t, 1)
                act.activation(sm[:, 2], sm[:, 2], ACT.Exp).then_inc(s.e, 1)
                act.wait_ge(s.e, 2)
                act.activation(sm[:, 3], sm[:, 2], ACT.Ln, bias=1.0).then_inc(s.ln, 1)
                act.activation(gates[:, :, 8:16], ab[:, :, 8:16], ACT.Sigmoid).then_inc(s.q, 1)
                for m in range(TILES):
                    act.wait_ge(s.conv, m + 1)
                    if m:
                        act.wait_ge(s.rot, m)
                    act.activation(sig[:], xs3[:, m % 3, 0, :], ACT.Sigmoid).then_inc(s.sig, 1)
                    act.wait_ge(s.ss, m + 1)
                    act.activation(ss2[:, m % 2, 2, :], ss2[:, m % 2, 1, :], ACT.Sqrt).then_inc(s.root, 1)

            @block.vector
            def _(dve):
                step = Chain(dve, s.dve)
                dve.wait_ge(s.weights, 96)
                all_tiles = lambda ap: ap.unsqueeze(1).to_broadcast([P, TILES, 8])
                step(dve.tensor_tensor(sm[:, 0], ab[:, :, 0:8], all_tiles(dtb[:]), ALU.add))
                step(dve.tensor_scalar(sm[:, 1], sm[:, 0], 0.0, None, ALU.max))
                dve.scalar_tensor_tensor(out=sm[:, 2], in0=sm[:, 1], scalar=-2.0, in1=sm[:, 0],
                                         op0=ALU.mult, op1=ALU.add).then_inc(s.t, 1)

                def convolve(m):
                    xs = xs3[:, m % 3]
                    dve.wait_ge(s_load[m % 3], 48 * (m // 3 + 1))
                    step(dve.tensor_tensor(xs[:, 0, :], xs[:, 0, :], cw[:, 0, :], ALU.mult))
                    dve.wait_ge(s.taps, m + 1)
                    dve.tensor_tensor(xs[:, 0, :], xs[:, 0, :], xs[:, 1, :], ALU.add).then_inc(s.conv, 1)
                    dve.wait_ge(s.conv, m + 1)

                convolve(0)
                dve.wait_ge(s.ln, 1)
                step(dve.tensor_tensor(sm[:, 1], sm[:, 1], sm[:, 3], ALU.add))
                step(dve.tensor_scalar(sm[:, 1], sm[:, 1], -1.0, None, ALU.mult))
                dve.tensor_tensor(gates[:, :, 0:8], sm[:, 1], all_tiles(rate[:]), ALU.mult).then_inc(s.q, 1)
                for m in range(TILES):
                    qkv, res, ss = xs3[:, m % 3, 0, :], res2[:, m % 2], ss2[:, m % 2]
                    dve.wait_ge(s.sig, m + 1)
                    if m >= 2:
                        dve.wait_ge(s_out[m % 2], 16 * (m // 2))
                    step(dve.tensor_tensor(res[:, QK:W], qkv[:, QK:W], sig[:, QK:W], ALU.mult))
                    dve.tensor_tensor(qkv[:, 0:QK], qkv[:, 0:QK], sig[:, 0:QK], ALU.mult).then_inc(s.rot, 1)
                    dve.wait_ge(s.rot, m + 1)
                    step(dve.tensor_tensor(sq[:], qkv[:, 0:QK], qkv[:, 0:QK], ALU.mult))
                    step(dve.tensor_reduce(ss[:, 0, :], sq[:].rearrange("p (h d) -> p h d", h=8), AX.X, ALU.add))
                    dve.tensor_scalar(ss[:, 1, :], ss[:, 0, :], NORM_EPS, None, ALU.add).then_inc(s.ss, 1)
                    x1, x2 = halves(m)[:, :, 0, :], halves(m)[:, :, 1, :]
                    step(dve.tensor_tensor(ax(rot[:, :, 0, :]), ax(x1), table(m, 0), ALU.mult))
                    step(dve.tensor_tensor(ax(tmp[:, 0]), ax(x2), table(m, 1), ALU.mult))
                    step(dve.tensor_tensor(rot[:, :, 0, :], rot[:, :, 0, :], tmp[:, 0], ALU.subtract))
                    if m + 1 < TILES:
                        convolve(m + 1)
                    dve.wait_ge(s.root, m + 1)
                    step(dve.reciprocal(ss[:, 3, :], ss[:, 2, :]))
                    step(dve.tensor_scalar(ss[:, 3, 0:4], ss[:, 3, 0:4], float(P) ** -0.5, None, ALU.mult))
                    dve.wait_ge(s.turned, m + 1)
                    dve.tensor_tensor(res[:, 0:QK].rearrange("p (h d) -> p h d", h=8),
                                      rot[:].rearrange("p g s c -> p (g s c)").rearrange("p (h d) -> p h d", h=8),
                                      wide(ss[:, 3, :]), ALU.mult).then_inc(s.done, 1)
                    dve.wait_ge(s.done, m + 1)


def gated_norm_stage(nc, e, l, src, gate_col, weight, dst_col):
    G = 4 * TILES
    with Stage(nc, "gnorm") as st:
        o, z, w = st.sb("o", [P, 2, TILES, 512]), st.sb("z", [P, TILES, 512]), st.sb("w", [P, P])
        sig, sq, ss = st.sb("sig", [P, TILES, 512]), st.sb("sq", [P, TILES, 512]), st.sb("ss", [P, 4, G])
        s_in, s_z, s_out, s_dve, s_sig, s_gate, s_ss, s_root, s_done = (
            st.sem(n) for n in ("in", "z", "out", "dve", "sig", "gate", "ss", "root", "done"))
        hv = lambda t: t.rearrange("p m (h d) -> p (m h) d", h=4)
        gate_cols = slice(gate_col, gate_col + 512)
        with nc.Block() as block:
            @block.sync
            def _(sp):
                ldz = Loads(sp, s_z)
                ldz(z[:, 0, :], e.PR[ROW_CTX:ROW_CTX + P, gate_cols])
                ldz(z[:, 1:TILES, :], e.PR[ROW_LAT:ROW_LAT + LAT, gate_cols].rearrange("(m p) c -> p m c", p=P))
                ldz(w[:], weight.partition_broadcast(P))
                ld = Loads(sp, s_in)
                for d in range(2):
                    ld(o[:, d], src[d].rearrange("(m p) c -> p m c", p=P))
                sp.wait_ge(s_done, 1)
                sp.dma_start(e.Y[:, dst_col:dst_col + 512].rearrange("(m p) c -> p m c", p=P), sq[:])\
                    .then_inc(s_out, 16)
                sp.wait_ge(s_out, 16)

            @block.scalar
            def _(act):
                act.wait_ge(s_z, 48)
                act.activation(sig[:], z[:], ACT.Sigmoid).then_inc(s_sig, 1)
                act.wait_ge(s_ss, 1)
                act.activation(ss[:, 2, :], ss[:, 1, :], ACT.Sqrt).then_inc(s_root, 1)

            @block.gpsimd
            def _(pool):
                pool.wait_ge(s_sig, 1)
                pool.tensor_tensor(sig[:], sig[:], z[:], ALU.mult).then_inc(s_gate, 1)
                pool.wait_ge(s_gate, 1)
                pool.tensor_tensor(hv(sig[:]), hv(sig[:]), w[:].unsqueeze(1).to_broadcast([P, G, P]), ALU.mult)\
                    .then_inc(s_gate, 1)

            @block.vector
            def _(dve):
                step = Chain(dve, s_dve)
                dve.wait_ge(s_in, 32)
                step(dve.tensor_tensor(o[:, 0], o[:, 0], o[:, 1], ALU.add))
                step(dve.tensor_tensor(sq[:], o[:, 0], o[:, 0], ALU.mult))
                step(dve.tensor_reduce(ss[:, 0, :], hv(sq[:]), AX.X, ALU.add))
                dve.tensor_scalar(ss[:, 1, :], ss[:, 0, :], 1.0 / P, NORM_EPS, ALU.mult, ALU.add).then_inc(s_ss, 1)
                dve.wait_ge(s_root, 1)
                step(dve.reciprocal(ss[:, 3, :], ss[:, 2, :]))
                step(dve.tensor_tensor(hv(o[:, 0]), hv(o[:, 0]), ss[:, 3, :].unsqueeze(2).to_broadcast([P, G, P]),
                                       ALU.mult))
                dve.wait_ge(s_gate, 2)
                dve.tensor_tensor(sq[:], o[:, 0], sig[:], ALU.mult).then_inc(s_done, 1)


def copy_stage(nc, pairs, then=()):
    with Stage(nc, "copy") as st:
        s_dma = st.sem("dma")
        with nc.Block() as block:
            @block.sync
            def _(sp):
                ld = Loads(sp, s_dma)
                for part in (pairs, then):
                    for dst, src in part:
                        ld(dst, src)
                    ld.wait()


def second(ap, v, d):
    head = " ".join("pn"[:len(ap.shape) - 1])
    return ap.rearrange(f"{head} (a two b) -> {head} a two b", two=2, b=1 << v)[..., 1 - d, :]


def gdn_unit(nc, e, r, tiles):
    with Stage(nc, "gdn") as st:
        x = st.sb("x", [P, 2, 1552])
        la, be, g = st.sb("la", [P, 8]), st.sb("be", [P, 8]), st.sb("g", [P, 8])
        qT, kT = st.sb("qT", [P, 8, P]), st.sb("kT", [P, 8, P])
        big = lambda n: st.sb(n, [P, 8, P])
        ula, ediff, dec, decT, erow, a, attn = (big(n) for n in ("ula", "ediff", "dec", "decT", "erow", "a", "attn"))
        lev, inv, invT, w = st.sb("lev", [P, 2, 8, P]), big("inv"), big("invT"), st.sb("w", [P, 2, 4, 64])
        res, vnew, kdec, o = big("res"), big("vnew"), big("kdec"), big("o")
        gl = st.sb("gl", [P, 4, 8])
        ps = st.ps("ps", [P, 8, CHUNK])
        names = "load out dve t tc gsum ula G kk E2 E1 er D DT gl egl A res ks vn vnc o st oc kdec fin".split()
        s = named(**{n: st.sem(n) for n in names})
        sd = [named(**{n: st.sem(f"{n}{d}") for n in "lev x xt T W wc D".split()}) for d in range(2)]
        of_dir = lambda ap, d: ap[:, 4 * d:4 * d + 4, :]
        over4 = lambda ap: ap.unsqueeze(1).to_broadcast([P, 4, P])
        bank = lambda b: ps[:, b, :].rearrange("p (h t) -> p h t", h=4)
        spread = lambda b, n: ps[:, b + 4 * (n // 4), (n % 4) * P:(n % 4 + 1) * P]
        S = r.state
        with nc.Block() as block:
            @block.sync
            def _(sp):
                ld = Loads(sp, s.load)
                for d in range(2):
                    ld(x[:, d, :], rows(e.GQ, tiles[d] * P))
                sp.wait_ge(s.oc, 2)
                out = Loads(sp, s.out)
                for d in range(2):
                    out(e.OG[d, bass.ds(tiles[d] * P, P), :], o[:, 4 * d:4 * d + 4, :].rearrange("p h t -> p (h t)"))
                out.wait()


            @block.tensor
            def _(pe):
                pe.wait_ge(s.load, 32)
                for d in range(2):
                    for kind in range(2):
                        for h in range(4):
                            t = pe.transpose(ps[:, 2 * kind + d, h * P:(h + 1) * P],
                                             x[:, d, (4 * kind + h) * P:(4 * kind + h + 1) * P], r.ident[:])
                        t.then_inc(s.t, 1)
                for d in range(2):
                    t = pe.matmul(ps[:, 4, 4 * d:4 * d + 4], r.cum[:, d, :],
                                  x[:, d, 1536 + 4 * d:1540 + 4 * d], start=True, stop=True)
                t.then_inc(s.gsum, 1)
                pe.wait_ge(s.ula, 1)
                for d in range(2):
                    t = pe.matmul(ps[:, 5 + d, :], r.ones[:],
                                  ula[:, 4 * d:4 * d + 4, :].rearrange("p h t -> p (h t)"), start=True, stop=True)
                t.then_inc(s.G, 1)
                pe.wait_ge(s.tc, 4)
                for n in range(8):
                    t = pe.matmul(ps[:, n // 4, (n % 4) * P:(n % 4 + 1) * P], kT[:, n, :], kT[:, n, :],
                                  start=True, stop=True)
                t.then_inc(s.kk, 1)
                for n in range(8):
                    t = pe.matmul(ps[:, 2 + n // 4, (n % 4) * P:(n % 4 + 1) * P], kT[:, n, :], qT[:, n, :],
                                  start=True, stop=True)
                t.then_inc(s.kk, 1)

                def turn_round(d, src):
                    for n in range(4):
                        t = pe.transpose(ps[:, 4 * d + 2, n * P:(n + 1) * P], src[:, 4 * d + n, :], r.ident[:])
                    t.then_inc(sd[d].T, 1)

                pe.wait_ge(s.A, 2)
                pe.wait_ge(s.er, 1)
                pe.wait_ge(s.gl, 1)
                for d in range(2):
                    pe.wait_ge(sd[d].x, 1)
                    turn_round(d, inv)
                pe.wait_ge(s.DT, 3)
                for n in range(8):
                    t = pe.matmul(spread(3, n), kT[:, n, :], S[:, n, :], start=True, stop=True)
                t.then_inc(s.ks, 1)
                for v in range(1, LEVELS):
                    for d in range(2):
                        pe.wait_ge(sd[d].lev, v + 1)
                        pe.wait_ge(sd[d].xt, v)
                        for n in range(4):
                            t = pe.matmul(ps[:, 4 * d, 64 * n:64 * n + 64], lev[:, v % 2, 4 * d + n, :],
                                          second(invT[:, 4 * d + n, :], v, d), start=True, stop=True)
                        t.then_inc(sd[d].W, 1)
                        if v > 1:
                            turn_round(d, invT)
                    for d in range(2):
                        pe.wait_ge(sd[d].wc, v)
                        pe.wait_ge(sd[d].x, v)
                        for n in range(4):
                            t = pe.matmul(ps[:, 4 * d + 1, 64 * n:64 * n + 64], inv[:, 4 * d + n, :], w[:, d, n, :],
                                          start=True, stop=True)
                        t.then_inc(sd[d].D, 1)
                pe.wait_ge(s.res, 1)
                for d in range(2):
                    pe.wait_ge(sd[d].xt, LEVELS)
                    for n in range(4 * d, 4 * d + 4):
                        t = pe.matmul(spread(0, n), invT[:, n, :], res[:, n, :], start=True, stop=True)
                    t.then_inc(s.vn, 1)
                for d in range(2):
                    pe.wait_ge(s.vnc, d + 1)
                    for n in range(4 * d, 4 * d + 4):
                        pe.matmul(spread(1, n), qT[:, n, :], S[:, n, :], start=True, stop=False)
                        t = pe.matmul(spread(1, n), attn[:, n, :], vnew[:, n, :], start=False, stop=True)
                t.then_inc(s.o, 1)
                pe.wait_ge(s.kdec, 1)
                for n in range(8):
                    t = pe.matmul(spread(2, n), kdec[:, n, :], vnew[:, n, :], start=True, stop=True)
                t.then_inc(s.st, 1)

            @block.scalar
            def _(act):
                for n in range(4):
                    d, kind = n // 2, n % 2
                    act.wait_ge(s.t, n + 1)
                    act.copy((qT, kT)[kind][:, 4 * d:4 * d + 4, :].rearrange("p h t -> p (h t)"),
                             ps[:, 2 * kind + d, :]).then_inc(s.tc, 1)
                act.wait_ge(s.G, 1)
                act.activation(erow[:], heads(ps[:, 5:7, :]), ACT.Exp).then_inc(s.er, 1)
                act.wait_ge(s.E1, 1)
                act.activation(dec[:], dec[:], ACT.Exp, scale=-1.0).then_inc(s.D, 1)
                act.wait_ge(s.E2, 1)
                act.activation(decT[:], decT[:], ACT.Exp).then_inc(s.D, 1)
                act.wait_ge(s.gl, 1)
                act.activation(gl[:, 2:4, :], gl[:, 0:2, :], ACT.Exp).then_inc(s.egl, 1)
                for d in range(2):
                    act.wait_ge(sd[d].T, 1)
                    act.copy(of_dir(invT, d), bank(4 * d + 2)).then_inc(sd[d].xt, 1)
                for v in range(1, LEVELS):
                    for d in range(2):
                        act.wait_ge(sd[d].W, v)
                        act.copy(w[:, d].rearrange("p n c -> p (n c)"), ps[:, 4 * d, 0:256]).then_inc(sd[d].wc, 1)
                        if v > 1:
                            act.wait_ge(sd[d].T, v)
                            act.copy(of_dir(inv, d), bank(4 * d + 2)).then_inc(sd[d].x, 1)
                for d in range(2):
                    act.wait_ge(s.vn, d + 1)
                    act.copy(of_dir(vnew, d), bank(4 * d)).then_inc(s.vnc, 1)
                act.wait_ge(s.o, 1)
                for d in range(2):
                    act.copy(of_dir(o, d), bank(4 * d + 1)).then_inc(s.oc, 1)

            @block.gpsimd
            def _(pool):
                pool.wait_ge(s.A, 1)
                for v in range(LEVELS):
                    for d in range(2):
                        if v == 2:
                            pool.wait_ge(sd[d].x, 1)
                        elif v > 2:
                            pool.wait_ge(sd[d].W, v - 2)
                        pool.tensor_tensor(of_dir(lev[:, v % 2], d), of_dir(a, d), over4(r.levels[:, v, d, :]),
                                           ALU.mult).then_inc(sd[d].lev, 1)
                    if v == 1:
                        pool.wait_ge(s.egl, 1)
                        for d in range(2):
                            t = pool.tensor_tensor(kdec[:, 4 * d:4 * d + 4, :],
                                                   x[:, d, 512:1024].rearrange("p (h t) -> p h t", h=4),
                                                   gl[:, 3, 4 * d:4 * d + 4].unsqueeze(2).to_broadcast([P, 4, P]),
                                                   ALU.mult)
                        t.then_inc(s.kdec, 1)

            @block.vector
            def _(dve):
                step = Chain(dve, s.dve)
                dve.wait_ge(s.load, 32)
                for d in range(2):
                    h = slice(4 * d, 4 * d + 4)
                    step(dve.tensor_copy(la[:, h], x[:, d, 1536 + 4 * d:1540 + 4 * d]))
                    step(dve.tensor_copy(be[:, h], x[:, d, 1544 + 4 * d:1548 + 4 * d]))
                dve.tensor_tensor(four(ula[:]), per_dir(r.cum[:]), four(wide(la[:])), ALU.mult).then_inc(s.ula, 1)
                dve.wait_ge(s.gsum, 1)
                step(dve.tensor_copy(g[:], ps[:, 4, 0:8]))
                dve.wait_ge(s.er, 1)
                step(dve.tensor_tensor(ediff[:], heads(ps[:, 5:7, :]), wide(g[:]), ALU.subtract))
                dve.tensor_scalar(dec[:], ediff[:], 0.0, None, ALU.max).then_inc(s.E1, 1)
                dve.tensor_scalar(decT[:], ediff[:], 0.0, None, ALU.min).then_inc(s.E2, 1)
                step(dve.tensor_copy(gl[:, 0, 0:4], ps[:, 5, P - 1:CHUNK:P]))
                step(dve.tensor_copy(gl[:, 0, 4:8], ps[:, 6, 0:CHUNK:P]))
                dve.tensor_tensor(gl[:, 1, :], gl[:, 0, :], g[:], ALU.subtract).then_inc(s.gl, 1)
                dve.wait_ge(s.kk, 2)
                dve.wait_ge(s.D, 1)
                step(dve.tensor_tensor(a[:], heads(ps[:, 0:2, :]), dec[:], ALU.mult))
                dve.tensor_tensor(a[:], a[:], wide(be[:]), ALU.mult).then_inc(s.A, 1)
                dve.wait_ge(s.D, 2)
                dve.tensor_tensor(attn[:], heads(ps[:, 2:4, :]), decT[:], ALU.mult).then_inc(s.A, 1)
                dve.wait_ge(s.A, 2)
                dve.tensor_tensor(four(attn[:]), four(attn[:]), per_dir(r.cum[:]), ALU.mult).then_inc(s.DT, 1)
                dve.wait_ge(s.er, 1)
                dve.tensor_tensor(qT[:], qT[:], erow[:], ALU.mult).then_inc(s.DT, 1)
                dve.tensor_tensor(kT[:], kT[:], erow[:], ALU.mult).then_inc(s.DT, 1)
                for d in range(2):
                    dve.wait_ge(sd[d].lev, 1)
                    dve.tensor_tensor(of_dir(inv, d), over4(r.ident[:]), of_dir(lev[:, 0], d), ALU.subtract)\
                       .then_inc(sd[d].x, 1)
                dve.wait_ge(s.ks, 1)
                for d in range(2):
                    step(dve.tensor_tensor(of_dir(res, d), x[:, d, 1024:1536].rearrange("p (h t) -> p h t", h=4),
                                           bank(4 * d + 3), ALU.subtract))
                dve.tensor_tensor(res[:], res[:], wide(be[:]), ALU.mult).then_inc(s.res, 1)
                for v in range(1, LEVELS):
                    for d in range(2):
                        dve.wait_ge(sd[d].D, v)
                        dve.wait_ge(sd[d].xt, v)
                        part = second(of_dir(invT, d), v, d)
                        change = ps[:, 4 * d + 1, 0:256].rearrange("p (n a b) -> p n a b", n=4, b=1 << v)
                        dve.tensor_tensor(part, part, change, ALU.subtract).then_inc(sd[d].xt, 1)
                dve.wait_ge(s.o, 1)
                dve.wait_ge(s.egl, 1)
                step(dve.tensor_tensor(S[:], S[:], wide(gl[:, 2, :]), ALU.mult))
                dve.wait_ge(s.st, 1)
                for d in range(2):
                    dve.tensor_tensor(of_dir(S, d), of_dir(S, d), bank(4 * d + 2), ALU.add).then_inc(s.fin, 1)


def gdn_pass(nc, e, l):
    gdn_prepare(nc, e, l)
    with Stage(nc, "gres") as st:
        r = named(ident=st.sb("ident", [P, P]), ones=st.sb("ones", [P, P]), cum=st.sb("cum", [P, 2, P]),
                            levels=st.sb("levels", [P, LEVELS, 2, P]), state=st.sb("state", [P, 8, P]))
        by_head = lambda t: t.rearrange("d h k v -> k (d h) v")
        copy_stage(nc, [(r.ident[:], e.ident), (r.ones[:], e.ones), (r.cum[:], e.cum), (r.levels[:], e.levels),
                        (r.state[:], e.zero_state)])
        gdn_unit(nc, e, r, (0, 0))
        copy_stage(nc, [(by_head(e.new_gdn[l]), r.state[:])], then=[(r.state[:], by_head(e.state_gdn[l]))])
        with nc.Fori(0, LAT_TILES) as i:
            gdn_unit(nc, e, r, (i + 1, LAT_TILES - i))
    gated_norm_stage(nc, e, l, e.OG, COL['gdn_g'], e.gdn_norm[l], 0)


def hgrn_unit(nc, e, l, r, row, tiles):
    X = 512
    with Stage(nc, "hg") as st:
        x, kf, lb = st.sb("x", [P, 2, 3 * X]), st.sb("kf", [P, 2, X]), st.sb("lb", [P, 2, X])
        ea, eb, t1, lf, over = (st.sb(n, [P, 2, X]) for n in ("ea", "eb", "t1", "lf", "over"))
        big = lambda n: st.sb(n, [P, 8, P])
        qT, kT, attn, qb, kdec, o = (big(n) for n in ("qT", "kT", "attn", "qb", "kdec", "o"))
        ex, ql, kl, part = (st.sb(n, [P, 2, 8, P]) for n in ("ex", "ql", "kl", "part"))
        blast = st.sb("blast", [P, 8])
        ps = st.ps("ps", [P, 8, CHUNK])
        names = ("gates load out dve pool abs e kf f ln lf t tc bt kd eb ekd qb diag dm kdec span exp ql kl prod m acc o oc "
                 "st fin").split()
        s = named(**{n: st.sem(n) for n in names})
        S = r.state
        blk = lambda b, n: ps[:, b + n // 4, (n % 4) * P:(n % 4 + 1) * P]
        head = lambda n: slice((n % 4) * P, (n % 4 + 1) * P)
        hv = lambda ap: ap.rearrange("p d (h t) -> p (d h) t", h=4)
        span_bank = lambda v: 4 if v % 2 == 0 else 0
        prod_bank = lambda v: 6 if v % 2 == 0 else 2
        with nc.Block() as block:
            @block.sync
            def _(sp):
                first, ld = Loads(sp, s.gates), Loads(sp, s.load)
                for d in range(2):
                    first(x[:, d, X:2 * X], e.PR[bass.ds(row[d], P), COL['hg_f'] + d * X:COL['hg_f'] + (d + 1) * X])
                first(lb[:, 0, :], e.LB[l].partition_broadcast(P))
                for d in range(2):
                    ld(x[:, d, 0:X], e.PR[bass.ds(row[d], P), COL['hg_q']:COL['hg_q'] + X])
                    ld(x[:, d, 2 * X:3 * X], e.PR[bass.ds(row[d], P), COL['hg_i']:COL['hg_i'] + X])
                sp.wait_ge(s.oc, 1)
                out = Loads(sp, s.out)
                for d in range(2):
                    out(e.OH[d, bass.ds(tiles[d] * P, P), :], o[:, 4 * d:4 * d + 4, :].rearrange("p h t -> p (h t)"))
                out.wait()

            @block.vector
            def _(dve):
                step = Chain(dve, s.dve)
                dve.wait_ge(s.gates, 48)
                z = x[:, :, X:2 * X]
                step(dve.tensor_scalar(lb[:, 1, :], lb[:, 0, :], -1.0, 1.0, ALU.mult, ALU.add))
                lbb = lb[:, 0, :].unsqueeze(1).to_broadcast([P, 2, X])
                lbc = lb[:, 1, :].unsqueeze(1).to_broadcast([P, 2, X])
                dve.tensor_scalar(ea[:], z, 0.0, None, ALU.min).then_inc(s.abs, 1)
                dve.tensor_scalar(eb[:], z, 0.0, None, ALU.max).then_inc(s.abs, 1)
                dve.wait_ge(s.e, 2)
                dve.tensor_tensor(t1[:], ea[:], eb[:], ALU.add).then_inc(s.f, 1)
                step(dve.tensor_tensor(kf[:], eb[:], lbc, ALU.mult))
                step(dve.tensor_tensor(eb[:], eb[:], lbb, ALU.mult))
                step(dve.tensor_tensor(ea[:], ea[:], eb[:], ALU.add))
                dve.tensor_scalar(lf[:], ea[:], 2.0 ** -62, None, ALU.max).then_inc(s.f, 1)
                step(dve.tensor_scalar(eb[:], ea[:], 2.0 ** -62, 2.0 ** 60, ALU.min, ALU.mult))
                dve.tensor_scalar(eb[:], eb[:], 2.0 ** -62, None, ALU.max).then_inc(s.f, 1)
                dve.wait_ge(s.ln, 3)
                step(dve.scalar_tensor_tensor(out=lf[:], in0=eb[:], scalar=float(2 * np.log(2.0)), in1=lf[:],
                                              op0=ALU.add, op1=ALU.add))
                dve.tensor_tensor(lf[:], lf[:], t1[:], ALU.subtract).then_inc(s.lf, 1)
                dve.wait_ge(s.ln, 4)
                dve.tensor_tensor(kf[:], kf[:], over[:], ALU.mult).then_inc(s.kf, 1)
                dve.wait_ge(s.diag, 1)
                dve.tensor_tensor(attn[:], heads(ps[:, 2:4, :]), r.ident[:].unsqueeze(1).to_broadcast([P, 8, P]),
                                  ALU.mult).then_inc(s.dm, 1)
                dve.wait_ge(s.eb, 1)
                dve.tensor_tensor(qb[:], qT[:], qb[:], ALU.mult).then_inc(s.qb, 1)
                dve.wait_ge(s.ekd, 1)
                dve.tensor_tensor(kdec[:], hv(kf[:]), kdec[:], ALU.mult).then_inc(s.kdec, 1)
                for v in range(LEVELS + 1):
                    if v < LEVELS:
                        dve.wait_ge(s.exp, v + 1)
                        if v >= 2:
                            dve.wait_ge(s.prod, v - 1)
                        dve.tensor_tensor(ql[:, v % 2], qT[:], ex[:, v % 2], ALU.mult).then_inc(s.ql, 1)
                    if v:
                        u = v - 1
                        dve.wait_ge(s.prod, u + 1)
                        if u >= 2:
                            dve.wait_ge(s.acc, u - 1)
                        b = prod_bank(u)
                        dve.tensor_tensor(four(part[:, u % 2]), four(heads(ps[:, b:b + 2, :])),
                                          per_dir(r.levels_t[:, u]), ALU.mult).then_inc(s.m, 1)
                dve.wait_ge(s.o, 1)
                step(dve.tensor_tensor(S[:], S[:], wide(blast[:]), ALU.mult))
                dve.wait_ge(s.st, 1)
                dve.tensor_tensor(S[:], S[:], heads(ps[:, 0:2, :]), ALU.add).then_inc(s.fin, 1)

            @block.gpsimd
            def _(pool):
                pool.wait_ge(s.tc, 4)
                for v in range(LEVELS + 1):
                    if v < LEVELS:
                        pool.wait_ge(s.exp, v + 1)
                        if v >= 2:
                            pool.wait_ge(s.prod, v - 1)
                        pool.tensor_tensor(kl[:, v % 2], kT[:], ex[:, v % 2], ALU.mult).then_inc(s.kl, 1)
                    if v:
                        pool.wait_ge(s.dm, 1)
                        pool.wait_ge(s.m, v)
                        if v >= 2:
                            pool.wait_ge(s.acc, v - 1)
                        pool.tensor_tensor(attn[:], attn[:], part[:, (v - 1) % 2], ALU.add).then_inc(s.acc, 1)

            @block.scalar
            def _(act):
                act.wait_ge(s.abs, 1)
                act.activation(ea[:], ea[:], ACT.Exp).then_inc(s.e, 1)
                act.wait_ge(s.abs, 2)
                act.activation(eb[:], eb[:], ACT.Exp, scale=-1.0).then_inc(s.e, 1)
                for n, part in enumerate((t1, lf, eb)):
                    act.wait_ge(s.f, n + 1)
                    act.activation(part[:], part[:], ACT.Ln).then_inc(s.ln, 1)
                act.wait_ge(s.ln, 1)
                act.activation(over[:], t1[:], ACT.Exp, scale=-1.0).then_inc(s.ln, 1)
                for n in range(4):
                    kind, d = n // 2, n % 2
                    act.wait_ge(s.t, n + 1)
                    act.copy((qT, kT)[kind][:, 4 * d:4 * d + 4, :].rearrange("p h t -> p (h t)"), ps[:, n, :])\
                       .then_inc(s.tc, 1)
                act.wait_ge(s.bt, 1)
                act.activation(qb[:], heads(ps[:, 4:6, :]), ACT.Exp).then_inc(s.eb, 1)
                act.wait_ge(s.eb, 1)
                act.activation(blast[:, 0:4], ps[:, 4, P - 1:CHUNK:P], ACT.Exp).then_inc(s.pool, 1)
                act.activation(blast[:, 4:8], ps[:, 5, 0:CHUNK:P], ACT.Exp).then_inc(s.pool, 1)
                act.wait_ge(s.kd, 1)
                act.activation(kdec[:], heads(ps[:, 6:8, :]), ACT.Exp).then_inc(s.ekd, 1)
                for v in range(LEVELS):
                    act.wait_ge(s.span, v + 1)
                    if v >= 2:
                        act.wait_ge(s.ql, v - 1)
                        act.wait_ge(s.kl, v - 1)
                    b = span_bank(v)
                    act.activation(ex[:, v % 2], heads(ps[:, b:b + 2, :]), ACT.Exp).then_inc(s.exp, 1)
                act.wait_ge(s.o, 1)
                act.copy(o[:], heads(ps[:, 4:6, :])).then_inc(s.oc, 1)

            @block.tensor
            def _(pe):
                pe.wait_ge(s.load, 64)
                def turn(src, n):
                    for h in range(4):
                        t = pe.transpose(ps[:, n, h * P:(h + 1) * P], src[:, h * P:(h + 1) * P], r.ident[:])
                    t.then_inc(s.t, 1)

                for d in range(2):
                    turn(x[:, d, 0:X], d)
                pe.wait_ge(s.lf, 1)
                for n in range(8):
                    t = pe.matmul(blk(4, n), lf[:, n // 4, head(n)], r.cum[:, n // 4, :], start=True, stop=True)
                t.then_inc(s.bt, 1)
                for d in range(2):
                    t = pe.matmul(ps[:, 6 + d, :], r.after[:, d, :], lf[:, d, :], start=True, stop=True)
                t.then_inc(s.kd, 1)
                pe.wait_ge(s.kf, 1)
                for d in range(2):
                    turn(kf[:, d, :], 2 + d)
                pe.wait_ge(s.tc, 4)
                for n in range(8):
                    t = pe.matmul(blk(2, n), kT[:, n, :], qT[:, n, :], start=True, stop=True)
                t.then_inc(s.diag, 1)

                def spans(v):
                    if v == 0:
                        pe.wait_ge(s.pool, 2)
                    if v >= 2:
                        pe.wait_ge(s.exp, v - 1)
                    for n in range(8):
                        t = pe.matmul(blk(span_bank(v), n), lf[:, n // 4, head(n)], r.spans[:, v, n // 4, :],
                                      start=True, stop=True)
                    t.then_inc(s.span, 1)

                spans(0)
                for v in range(LEVELS):
                    if v + 1 < LEVELS:
                        spans(v + 1)
                    pe.wait_ge(s.ql, v + 1)
                    pe.wait_ge(s.kl, v + 1)
                    if v == 0:
                        pe.wait_ge(s.ekd, 1)
                    if v == 1:
                        pe.wait_ge(s.dm, 1)
                    if v >= 2:
                        pe.wait_ge(s.m, v - 1)
                    for n in range(8):
                        t = pe.matmul(blk(prod_bank(v), n), kl[:, v % 2, n, :], ql[:, v % 2, n, :],
                                      start=True, stop=True)
                    t.then_inc(s.prod, 1)
                pe.wait_ge(s.acc, LEVELS)
                pe.wait_ge(s.qb, 1)
                pe.wait_ge(s.exp, LEVELS)
                for n in range(8):
                    pe.matmul(blk(4, n), qb[:, n, :], S[:, n, :], start=True, stop=False)
                    t = pe.matmul(blk(4, n), attn[:, n, :], x[:, n // 4, 2 * X:][:, head(n)],
                                  start=False, stop=True)
                t.then_inc(s.o, 1)
                pe.wait_ge(s.kdec, 1)
                for n in range(8):
                    t = pe.matmul(blk(0, n), kdec[:, n, :], x[:, n // 4, 2 * X:][:, head(n)], start=True, stop=True)
                t.then_inc(s.st, 1)


def hgrn_pass(nc, e, l):
    with Stage(nc, "hres") as st:
        r = named(ident=st.sb("ident", [P, P]), cum=st.sb("cum", [P, 2, P]), after=st.sb("after", [P, 2, P]),
                            levels_t=st.sb("levels", [P, LEVELS, 2, P]), spans=st.sb("spans", [P, LEVELS, 2, P]),
                            state=st.sb("state", [P, 8, P]))
        by_head = lambda t: t.rearrange("d h k v -> k (d h) v")
        copy_stage(nc, [(r.ident[:], e.ident), (r.cum[:], e.cum), (r.after[:], e.after), (r.levels_t[:], e.levels_t),
                        (r.spans[:], e.spans), (r.state[:], e.zero_state)])
        hgrn_unit(nc, e, l, r, (ROW_CTX, ROW_CTX), (0, 0))
        copy_stage(nc, [(by_head(e.new_hgrn[l]), r.state[:])], then=[(r.state[:], by_head(e.state_hgrn[l]))])
        with nc.Fori(0, LAT_TILES) as i:
            hgrn_unit(nc, e, l, r, (i * P + ROW_LAT, (LAT_TILES - 1 - i) * P + ROW_LAT), (i + 1, LAT_TILES - i))
    gated_norm_stage(nc, e, l, e.OH, COL['hg_g'], e.hg_norm[l], 1024)


RQ_PARTS = ('r', 'k', 'v', 'nkk', 'b', 'lw0', 'lw1', 'gate', 'bonus')
RQ = {name: 512 * n for n, name in enumerate(RQ_PARTS)}


def rwkv_prepare(nc, e, l):
    with Stage(nc, "rprep") as st:
        xs3, mu = st.sb("xs", [P, 3, 3, RW_W]), st.sb("mu", [P, 2, RW_W])
        vec = st.sb("vec", [P, 6, RW])
        w2, a2, g2, ident = st.sb("w2", [P, RW]), st.sb("a2", [64, RW]), st.sb("g2", [P, RW]), st.sb("ident", [P, P])
        lora, loraT = st.sb("lora", [P, 2, P]), st.sb("loraT", [P, 3, P])
        res2, a = st.sb("res", [P, 2, 9, RW]), st.sb("a", [P, RW])
        kk2, t2, ss2 = st.sb("kk", [P, 2, RW]), st.sb("t2", [P, RW]), st.sb("ss", [P, 2, 5, RW_H])
        ps, pt = st.ps("ps", [P, 4, CHUNK]), st.ps("pt", [P, CHUNK])
        names = "mu weights dve pool next shift lora t tc mm w sig lw rv root ss done gate".split()
        s = named(**{n: st.sem(n) for n in names})
        s_load, s_out = [st.sem(f"load{b}") for b in range(3)], [st.sem(f"out{b}") for b in range(2)]
        hv = lambda ap: ap.rearrange("p (h d) -> p h d", h=RW_H)
        hb = lambda ap: ap.unsqueeze(2).to_broadcast([P, RW_H, RW_D])
        o0 = 3 * RW

        def loaded(eng, m):
            eng.wait_ge(s_load[m % 3], 48 * (m // 3 + 1))

        def stored(eng, m):
            if m >= 2:
                eng.wait_ge(s_out[m % 2], 16 * (m // 2))

        with nc.Block() as block:
            @block.sync
            def _(sp):
                def load(m):
                    for j in range(3):
                        sp.dma_start(xs3[:, m % 3, j, :], e.PR[first_row(m) - 1 + j:first_row(m) - 1 + j + P,
                                                               COL['rw']:COL['rw'] + RW_W]).then_inc(s_load[m % 3], 16)

                load(0)
                ld_mu, ld = Loads(sp, s.mu), Loads(sp, s.weights)
                for j in range(2):
                    ld_mu(mu[:, j, :], e.rw_mu[l, j, :].partition_broadcast(P))
                load(1)
                for j, v in enumerate((e.rw_w0[l, 0, :], e.rw_w0[l, 1, :], e.rw_a0[l], e.rw_kk[l], e.rw_ka[l],
                                       e.rw_rk[l])):
                    ld(vec[:, j, :], v.partition_broadcast(P))
                ld(w2[:], e.rw_w2[l])
                ld(a2[:], e.rw_a2[l])
                ld(g2[:], e.rw_g2[l])
                ld(ident[:], e.ident)
                load(2)
                for m in range(TILES):
                    sp.wait_ge(s.done, m + 1)
                    sp.wait_ge(s.gate, m + 1)
                    sp.wait_ge(s.lw, 2 * m + 2)
                    sp.wait_ge(s.rv, 2 * m + 2)
                    sp.dma_start(e.RQ[m * P:(m + 1) * P, :], res2[:, m % 2].rearrange("p a b -> p (a b)"))\
                        .then_inc(s_out[m % 2], 16)
                    if m + 3 < TILES:
                        load(m + 3)
                for b in range(2):
                    sp.wait_ge(s_out[b], 16 * ((TILES + 1 - b) // 2))

            @block.gpsimd
            def _(pool):
                step = Chain(pool, s.pool)
                pool.wait_ge(s.mu, 32)
                for m in range(TILES):
                    xs = xs3[:, m % 3]
                    loaded(pool, m)
                    step(pool.tensor_tensor(xs[:, 2, :], xs[:, 2, :], xs[:, 1, :], ALU.subtract))
                    pool.tensor_tensor(xs[:, 2, :], xs[:, 2, :], mu[:, 1, :], ALU.mult).then_inc(s.next, 1)

            @block.scalar
            def _(act):
                def first(m):
                    xs, res, ss = xs3[:, m % 3], res2[:, m % 2], ss2[:, m % 2]
                    act.wait_ge(s.shift, m + 1)
                    act.activation(lora[:, 0, :], xs[:, 1, o0:o0 + P], ACT.Tanh).then_inc(s.lora, 1)
                    act.activation(lora[:, 1, :], xs[:, 1, o0 + 192:o0 + 192 + P], ACT.Sigmoid).then_inc(s.lora, 1)
                    stored(act, m)
                    for n in (0, 2):
                        act.copy(res[:, n, :], xs[:, 1, n * RW:(n + 1) * RW]).then_inc(s.rv, 1)
                    act.wait_ge(s.t, m + 1)
                    act.copy(loraT[:].rearrange("p a b -> p (a b)")[:, 0:2 * P], pt[:, 0:2 * P]).then_inc(s.tc, 1)
                    act.copy(loraT[0:64, 2, :], pt[0:64, 2 * P:3 * P]).then_inc(s.tc, 1)
                    act.wait_ge(s.ss, m + 1)
                    act.activation(ss[:, 2, :], ss[:, 1, :], ACT.Sqrt).then_inc(s.root, 1)

                def second_half(m):
                    res = res2[:, m % 2]
                    for n, dst in enumerate((res[:, 5, :], res[:, 6, :], a[:])):
                        act.wait_ge(s.w, 3 * m + n + 1)
                        act.activation(dst, dst, ACT.Sigmoid).then_inc(s.sig, 1)
                    for n in (5, 6):
                        act.wait_ge(s.sig, 3 * m + n - 4)
                        act.activation(res[:, n, :], res[:, n, :], ACT.Copy, scale=-float(np.exp(-0.5)))\
                           .then_inc(s.lw, 1)
                    act.wait_ge(s.mm, 4 * m + 4)
                    act.copy(res[:, 7, :], ps[:, 3, :]).then_inc(s.gate, 1)

                first(0)
                for m in range(TILES):
                    if m + 1 < TILES:
                        first(m + 1)
                    second_half(m)

            @block.tensor
            def _(pe):
                pe.wait_ge(s.weights, 16 * 10)
                for m in range(TILES):
                    xs = xs3[:, m % 3]
                    pe.wait_ge(s.lora, 2 * m + 2)
                    pe.transpose(pt[:, 0:P], lora[:, 0, :], ident[:])
                    pe.transpose(pt[:, P:2 * P], lora[:, 1, :], ident[:])
                    pe.transpose(pt[0:64, 2 * P:3 * P], xs[:, 1, o0 + P:o0 + 192], ident[:]).then_inc(s.t, 1)
                    pe.wait_ge(s.tc, 2 * m + 2)
                    if m:
                        pe.wait_ge(s.w, 3 * m)
                        pe.wait_ge(s.gate, m)
                    for d in range(2):
                        r = slice(64 * d, 64 * d + 64)
                        pe.matmul(ps[:, d, :], loraT[r, 0, :], w2[r, :], start=True, stop=True).then_inc(s.mm, 1)
                    pe.matmul(ps[:, 2, :], loraT[0:64, 2, :], a2[:], start=True, stop=True).then_inc(s.mm, 1)
                    pe.matmul(ps[:, 3, :], loraT[:, 1, :], g2[:], start=True, stop=True).then_inc(s.mm, 1)

            @block.vector
            def _(dve):
                step = Chain(dve, s.dve)
                dve.wait_ge(s.mu, 32)

                def first(m):
                    xs, ss, kk = xs3[:, m % 3], ss2[:, m % 2], kk2[:, m % 2]
                    loaded(dve, m)
                    step(dve.tensor_tensor(xs[:, 0, :], xs[:, 0, :], xs[:, 1, :], ALU.subtract))
                    step(dve.tensor_tensor(xs[:, 0, :], xs[:, 0, :], mu[:, 0, :], ALU.mult))
                    dve.wait_ge(s.next, m + 1)
                    step(dve.tensor_tensor(xs[:, 0, :], xs[:, 0, :], xs[:, 2, :], ALU.add))
                    dve.tensor_tensor(xs[:, 1, :], xs[:, 1, :], xs[:, 0, :], ALU.add).then_inc(s.shift, 1)
                    dve.wait_ge(s.shift, m + 1)
                    if m == 0:
                        dve.wait_ge(s.weights, 16 * 10)
                    step(dve.tensor_tensor(kk, xs[:, 1, RW:2 * RW], vec[:, 3, :], ALU.mult))
                    step(dve.tensor_tensor(t2[:], kk, kk, ALU.mult))
                    step(dve.tensor_reduce(ss[:, 0, :], hv(t2[:]), AX.X, ALU.add))
                    dve.tensor_scalar(ss[:, 1, :], ss[:, 0, :], NORM_EPS, None, ALU.add).then_inc(s.ss, 1)

                def second_half(m):
                    xs, ss, kk, res = xs3[:, m % 3], ss2[:, m % 2], kk2[:, m % 2], res2[:, m % 2]
                    r, kr, v = (xs[:, 1, n * RW:(n + 1) * RW] for n in range(3))
                    stored(dve, m)
                    for n, dst in enumerate((res[:, 5, :], res[:, 6, :], a[:])):
                        dve.wait_ge(s.mm, 4 * m + n + 1)
                        dve.tensor_tensor(dst, ps[:, n, :], vec[:, n, :], ALU.add).then_inc(s.w, 1)
                    dve.wait_ge(s.root, m + 1)
                    step(dve.reciprocal(ss[:, 3, :], ss[:, 2, :]))
                    step(dve.tensor_scalar(ss[:, 4, :], ss[:, 3, :], -1.0, None, ALU.mult))
                    step(dve.tensor_tensor(hv(res[:, 3, :]), hv(kk), hb(ss[:, 4, :]), ALU.mult))
                    step(dve.tensor_tensor(hv(kk), hv(kk), hb(ss[:, 3, :]), ALU.mult))
                    dve.wait_ge(s.sig, 3 * m + 3)
                    step(dve.tensor_tensor(res[:, 4, :], kk, a[:], ALU.mult))
                    step(dve.scalar_tensor_tensor(out=a[:], in0=a[:], scalar=-1.0, in1=vec[:, 4, :], op0=ALU.add,
                                                  op1=ALU.mult))
                    step(dve.scalar_tensor_tensor(out=res[:, 1, :], in0=a[:], scalar=1.0, in1=kr, op0=ALU.add,
                                                  op1=ALU.mult))
                    step(dve.tensor_tensor(t2[:], r, res[:, 1, :], ALU.mult))
                    step(dve.tensor_tensor(t2[:], t2[:], vec[:, 5, :], ALU.mult))
                    step(dve.tensor_reduce(ss[:, 0, :], hv(t2[:]), AX.X, ALU.add))
                    dve.tensor_tensor(hv(res[:, 8, :]), hv(v), hb(ss[:, 0, :]), ALU.mult).then_inc(s.done, 1)

                first(0)
                for m in range(TILES):
                    if m + 1 < TILES:
                        first(m + 1)
                    second_half(m)


def rwkv_unit(nc, e, r, tiles):
    H2 = 2 * RW_H
    with Stage(nc, "rw") as st:
        x = st.sb("x", [P, 2, 6, RW])
        big = lambda n: st.sb(n, [P, 8, P])
        ep, em, epx, dec, rt, kt, at, bt = (big(n) for n in ("ep", "em", "epx", "dec", "rt", "kt", "at", "bt"))
        kd, bd, sm, o, rhs, u = (big(n) for n in ("kd", "bd", "sm", "o", "rhs", "u"))
        emid, efin = st.sb("emid", [P, 8]), st.sb("efin", [P, 8])
        nm, inv, invT = (st.sb(n, [P, H2, P]) for n in ("nm", "inv", "invT"))
        w = st.sb("w", [P, 2, 8, 64])
        lev = st.sb("lev", [P, 2, H2, P])
        ps = st.ps("ps", [P, 8, CHUNK])
        names = "lw load rkv out dve exp ex t til N nc A ac B bc C cc sm R rc U uc Y oc dec st fin".split()
        s = named(**{n: st.sem(n) for n in names})
        sd = [named(**{n: st.sem(f"{n}{d}") for n in "lev x xt T W wc D".split()}) for d in range(2)]
        S = r.state
        blk = lambda b, n: ps[:, b + n // 4, (n % 4) * P:(n % 4 + 1) * P]
        order = [8 * (p // 4) + 4 * q + p % 4 for p in range(8) for q in range(2)]
        pair = lambda n: 4 * (n // 8) + n % 4
        lane = lambda n: slice((n // 4 % 2) * RW_D, (n // 4 % 2 + 1) * RW_D)
        hd = lambda ap, n: ap[lane(n), pair(n), :]
        vals = lambda n: x[:, n // 8, 2, :].rearrange("p (a c) -> p a c", a=4)[:, n % 4, lane(n)]
        all4 = lambda b: ps[:, b:b + 4, :].rearrange("p b (h t) -> p (b h) t", h=4)
        of_dir = lambda ap, d: ap[:, 8 * d:8 * d + 8, :]
        over8 = lambda ap: ap.unsqueeze(1).to_broadcast([P, 8, P])
        with nc.Block() as block:
            @block.sync
            def _(sp):
                first, ld = Loads(sp, s.lw), Loads(sp, s.load)
                for d in range(2):
                    first(x[:, d, 5, :], e.RQ[bass.ds(tiles[d] * P, P), (5 + d) * RW:(6 + d) * RW])
                for d in range(2):
                    ld(x[:, d, 3:5, :].rearrange("p a b -> p (a b)"), e.RQ[bass.ds(tiles[d] * P, P), 3 * RW:5 * RW])
                last = Loads(sp, s.rkv)
                for d in range(2):
                    last(x[:, d, 0:3, :].rearrange("p a b -> p (a b)"), e.RQ[bass.ds(tiles[d] * P, P), 0:3 * RW])
                sp.wait_ge(s.oc, 1)
                out = Loads(sp, s.out)
                for d in range(2):
                    out(e.OR[d, bass.ds(tiles[d] * P, P), :], o[:, 4 * d:4 * d + 4, :].rearrange("p h t -> p (h t)"))
                out.wait()

            @block.tensor
            def _(pe):
                pe.wait_ge(s.lw, 32)
                lw = lambda n: x[:, n // 4, 5, (n % 4) * P:(n % 4 + 1) * P]
                for n in range(8):
                    pe.matmul(blk(0, n), lw(n), r.mid[:, n // 4, :], start=True, stop=True)
                    pe.matmul(blk(2, n), lw(n), r.midx[:, n // 4, :], start=True, stop=True)
                for d in range(2):
                    pe.matmul(ps[:, 4 + d, :], r.after[:, d, :], x[:, d, 5, :], start=True, stop=True)
                for n in range(8):
                    m = P // 2 - 1 if n < 4 else P // 2
                    t = pe.matmul(ps[:, 6, n:n + 1], lw(n), r.cum[:, n // 4, m:m + 1], start=True, stop=True)
                t.then_inc(s.exp, 1)
                pe.wait_ge(s.load, 32)
                for b, part in enumerate((3, 4, 1, 0)):
                    pe.wait_ge(s.ex, b + 2)
                    if part == 1:
                        pe.wait_ge(s.rkv, 32)
                    for n in range(8):
                        t = pe.transpose(blk(2 * b, n), x[:, n // 4, part, (n % 4) * P:(n % 4 + 1) * P], r.ident[:])
                    t.then_inc(s.t, 1)
                pe.wait_ge(s.til, 2)
                for n in order:
                    t = pe.matmul(blk(0, n), hd(at, n), hd(bt, n), start=True, stop=True)
                t.then_inc(s.N, 1)
                pe.wait_ge(s.til, 4)
                for n in order:
                    t = pe.matmul(blk(4, n), hd(kt, n), hd(at, n), start=True, stop=True)
                t.then_inc(s.A, 1)
                pe.wait_ge(s.nc, 2)
                for n in order:
                    t = pe.matmul(blk(0, n), hd(bt, n), hd(rt, n), start=True, stop=True)
                t.then_inc(s.B, 1)
                pe.wait_ge(s.ac, 2)
                for n in order:
                    t = pe.matmul(blk(4, n), hd(kt, n), hd(rt, n), start=True, stop=True)
                t.then_inc(s.C, 1)

                def turn_round(d, src):
                    for n in range(8):
                        t = pe.transpose(blk(4 * d + 2, n), src[:, 8 * d + n, :], r.ident[:])
                    t.then_inc(sd[d].T, 1)

                half = lambda b, n: ps[:, b + n // 8, :].rearrange("p (a c) -> p a c", a=4)[:, n % 4, lane(n)]
                for d in range(2):
                    pe.wait_ge(sd[d].x, 1)
                    pe.wait_ge((s.bc, s.cc)[d], 2)
                    turn_round(d, inv)
                for v in range(1, LEVELS):
                    for d in range(2):
                        pe.wait_ge(sd[d].lev, v + 1)
                        pe.wait_ge(sd[d].xt, v)
                        if v == 1 and d == 0:
                            pe.wait_ge(s.cc, 2)
                        for n in range(8):
                            t = pe.matmul(ps[:, 4 * d, 64 * n:64 * n + 64], lev[:, v % 2, 8 * d + n, :],
                                          second(invT[:, 8 * d + n, :], v, d), start=True, stop=True)
                        t.then_inc(sd[d].W, 1)
                        if v > 1:
                            turn_round(d, invT)
                    for d in range(2):
                        pe.wait_ge(sd[d].wc, v)
                        pe.wait_ge(sd[d].x, v)
                        for n in range(8):
                            t = pe.matmul(ps[:, 4 * d + 1, 64 * n:64 * n + 64], inv[:, 8 * d + n, :], w[:, d, n, :],
                                          start=True, stop=True)
                        t.then_inc(sd[d].D, 1)
                pe.wait_ge(s.sm, 1)
                for p in range(8):
                    pe.matmul(blk(2, p), at[:, p, :], sm[:, p, :], start=True, stop=True)
                    for n in (order[2 * p], order[2 * p + 1]):
                        t = pe.matmul(half(2, n), r.aak[:, n, :], vals(n), start=False, stop=True,
                                      skip_group_check=True)
                t.then_inc(s.R, 1)
                for d in range(2):
                    pe.wait_ge(sd[d].xt, LEVELS)
                pe.wait_ge(s.rc, 1)
                flat = lambda ap, n: ap[:, pair(n), lane(n)]
                for n in range(H2):
                    t = pe.matmul(half(6, n), invT[:, n, :], flat(rhs, n), start=True, stop=True)
                t.then_inc(s.U, 1)
                pe.wait_ge(s.uc, 1)
                for p in range(8):
                    pe.matmul(blk(4, p), rt[:, p, :], sm[:, p, :], start=True, stop=True)
                    for n in (order[2 * p], order[2 * p + 1]):
                        pe.matmul(half(4, n), r.ark[:, n, :], vals(n), start=False, stop=True,
                                  skip_group_check=True)
                        t = pe.matmul(half(4, n), r.arb[:, n, :], flat(u, n), start=False, stop=True,
                                      skip_group_check=True)
                t.then_inc(s.Y, 1)
                pe.wait_ge(s.dec, 2)
                for p in range(8):
                    pe.matmul(blk(0, p), kd[:, p, :], x[:, p // 4, 2, (p % 4) * P:(p % 4 + 1) * P],
                              start=True, stop=False)
                    t = pe.matmul(blk(0, p), bd[:, p, :], u[:, p, :], start=False, stop=True)
                t.then_inc(s.st, 1)

            @block.scalar
            def _(act):
                act.wait_ge(s.exp, 1)
                act.activation(ep[:], heads(ps[:, 0:2, :]), ACT.Exp).then_inc(s.ex, 1)
                act.activation(em[:], heads(ps[:, 0:2, :]), ACT.Exp, scale=-1.0).then_inc(s.ex, 1)
                act.activation(epx[:], heads(ps[:, 2:4, :]), ACT.Exp).then_inc(s.ex, 1)
                act.activation(dec[:], heads(ps[:, 4:6, :]), ACT.Exp).then_inc(s.ex, 1)
                act.activation(emid[:], ps[:, 6, 0:8], ACT.Exp).then_inc(s.ex, 1)
                act.wait_ge(s.N, 1)
                for d in range(2):
                    act.copy(of_dir(nm, d), of_dir(all4(0), d)).then_inc(s.nc, 1)
                for d in range(2):
                    act.wait_ge(sd[d].T, 1)
                    act.copy(of_dir(invT, d), heads(ps[:, 4 * d + 2:4 * d + 4, :])).then_inc(sd[d].xt, 1)
                for v in range(1, LEVELS):
                    for d in range(2):
                        act.wait_ge(sd[d].W, v)
                        act.copy(w[:, d].rearrange("p n c -> p (n c)"), ps[:, 4 * d, :]).then_inc(sd[d].wc, 1)
                        if v > 1:
                            act.wait_ge(sd[d].T, v)
                            act.copy(of_dir(inv, d), heads(ps[:, 4 * d + 2:4 * d + 4, :])).then_inc(sd[d].x, 1)
                act.wait_ge(s.R, 1)
                act.copy(rhs[:], heads(ps[:, 2:4, :])).then_inc(s.rc, 1)
                act.wait_ge(s.U, 1)
                act.copy(u[:], heads(ps[:, 6:8, :])).then_inc(s.uc, 1)
                act.wait_ge(s.Y, 1)
                act.copy(o[:], heads(ps[:, 4:6, :])).then_inc(s.oc, 1)

            @block.gpsimd
            def _(pool):
                pool.wait_ge(s.ex, 4)
                pool.wait_ge(s.load, 32)
                pool.wait_ge(s.rkv, 32)
                for dst, part in ((kd, 1), (bd, 4)):
                    pool.tensor_tensor(four(dst[:]), x[:, :, part, :].rearrange("p d (h t) -> p d h t", h=4),
                                       four(dec[:]), ALU.mult).then_inc(s.dec, 1)
                for v in range(LEVELS):
                    for d in range(2):
                        if v == 0:
                            pool.wait_ge(s.nc, d + 1)
                        elif v == 2:
                            pool.wait_ge(sd[d].x, 1)
                        elif v > 2:
                            pool.wait_ge(sd[d].W, v - 2)
                        pool.tensor_tensor(of_dir(lev[:, v % 2], d), of_dir(nm, d), over8(r.levels[:, v, d, :]),
                                           ALU.mult).then_inc(sd[d].lev, 1)

            @block.vector
            def _(dve):
                step = Chain(dve, s.dve)
                for b, (dst, ex) in enumerate(((at, epx), (bt, em), (kt, em), (rt, ep))):
                    dve.wait_ge(s.ex, 5)
                    dve.wait_ge(s.t, b + 1)
                    dve.tensor_tensor(dst[:], heads(ps[:, 2 * b:2 * b + 2, :]), ex[:], ALU.mult).then_inc(s.til, 1)
                dve.tensor_tensor(sm[:], S[:], wide(emid[:]), ALU.mult).then_inc(s.sm, 1)
                step(dve.tensor_tensor(efin[:, 0:4], ep[:, 0:4, P - 1], emid[:, 0:4], ALU.mult))
                step(dve.tensor_tensor(efin[:, 4:8], ep[:, 4:8, 0], emid[:, 4:8], ALU.mult))
                step(dve.tensor_tensor(S[:], S[:], wide(efin[:]), ALU.mult))

                def keep(done, mask, dst, b, out):
                    dve.wait_ge(done, 1)
                    for d in range(2):
                        dve.copy_predicated(of_dir(dst, d), over8(mask[:, d, :]), of_dir(all4(b), d)).then_inc(out, 1)

                keep(s.A, r.before_u, r.aak, 4, s.ac)
                for d in range(2):
                    dve.wait_ge(sd[d].lev, 1)
                    dve.tensor_tensor(of_dir(inv, d), over8(r.ident[:]), of_dir(lev[:, 0], d), ALU.add)\
                       .then_inc(sd[d].x, 1)
                keep(s.B, r.cum_u, r.arb, 0, s.bc)
                keep(s.C, r.cum_u, r.ark, 4, s.cc)
                for v in range(1, LEVELS):
                    for d in range(2):
                        dve.wait_ge(sd[d].D, v)
                        dve.wait_ge(sd[d].xt, v)
                        part = second(of_dir(invT, d), v, d)
                        change = ps[:, 4 * d + 1, :].rearrange("p (n a b) -> p n a b", n=8, b=1 << v)
                        dve.tensor_tensor(part, part, change, ALU.add).then_inc(sd[d].xt, 1)
                dve.wait_ge(s.st, 1)
                for q in range(2):
                    h = slice(64 * q, 64 * q + 64)
                    dve.tensor_tensor(S[h, :, h], S[h, :, h], heads(ps[:, 0:2, :])[h, :, h], ALU.add)\
                       .then_inc(s.fin, 1)


def rwkv_finish(nc, e, l):
    G = RW_H * TILES
    with Stage(nc, "rfin") as st:
        o, gb = st.sb("o", [P, 2, TILES, RW]), st.sb("gb", [P, TILES, 2, RW])
        gn, sq, ss = st.sb("gn", [P, 2, RW]), st.sb("sq", [P, TILES, RW]), st.sb("ss", [P, 5, G])
        s = named(**{n: st.sem(n) for n in "load out dve ss root done".split()})
        s_o = st.sem("o")
        by_tile = lambda ap: ap.rearrange("(m p) c -> p m c", p=P)
        hv = lambda ap: ap.rearrange("p m (h d) -> p (m h) d", h=RW_H)
        hb = lambda ap: ap.unsqueeze(2).to_broadcast([P, G, RW_D])
        tb = lambda ap: ap.unsqueeze(1).to_broadcast([P, TILES, RW])
        with nc.Block() as block:
            @block.sync
            def _(sp):
                for d in range(2):
                    sp.dma_start(o[:, d], by_tile(e.OR[d])).then_inc(s_o, 16)
                ld = Loads(sp, s.load)
                ld(gb[:].rearrange("p m a b -> p m (a b)"), by_tile(e.RQ[:, RQ['gate']:RQ['gate'] + 2 * RW]))
                ld(gn[:, 0, :], e.rw_gn_w[l].partition_broadcast(P))
                ld(gn[:, 1, :], e.rw_gn_b[l].partition_broadcast(P))
                sp.wait_ge(s.done, 1)
                sp.dma_start(by_tile(e.Y[:, 1536:2048]), sq[:]).then_inc(s.out, 16)
                sp.wait_ge(s.out, 16)

            @block.scalar
            def _(act):
                act.wait_ge(s.ss, 1)
                act.activation(ss[:, 3, :], ss[:, 2, :], ACT.Sqrt).then_inc(s.root, 1)

            @block.vector
            def _(dve):
                step = Chain(dve, s.dve)
                dve.wait_ge(s_o, 32)
                y = o[:, 0]
                step(dve.tensor_tensor(y, y, o[:, 1], ALU.add))
                step(dve.tensor_reduce(ss[:, 0, :], hv(y), AX.X, ALU.add))
                step(dve.tensor_scalar(ss[:, 1, :], ss[:, 0, :], 1.0 / RW_D, None, ALU.mult))
                step(dve.tensor_tensor(hv(y), hv(y), hb(ss[:, 1, :]), ALU.subtract))
                step(dve.tensor_tensor(sq[:], y, y, ALU.mult))
                step(dve.tensor_reduce(ss[:, 0, :], hv(sq[:]), AX.X, ALU.add))
                dve.tensor_scalar(ss[:, 2, :], ss[:, 0, :], 1.0 / RW_D, RW_GN_EPS, ALU.mult, ALU.add)\
                   .then_inc(s.ss, 1)
                dve.wait_ge(s.root, 1)
                step(dve.reciprocal(ss[:, 4, :], ss[:, 3, :]))
                step(dve.tensor_tensor(hv(y), hv(y), hb(ss[:, 4, :]), ALU.mult))
                dve.wait_ge(s.load, 48)
                step(dve.tensor_tensor(y, y, tb(gn[:, 0, :]), ALU.mult))
                step(dve.tensor_tensor(y, y, tb(gn[:, 1, :]), ALU.add))
                step(dve.tensor_tensor(y, y, gb[:, :, 1, :], ALU.add))
                dve.tensor_tensor(sq[:], y, gb[:, :, 0, :], ALU.mult).then_inc(s.done, 1)


def rwkv_pass(nc, e, l):
    rwkv_prepare(nc, e, l)
    with Stage(nc, "rres") as st:
        m = lambda n, dt=F32: st.sb(n, [P, 2, P], dt)
        r = named(ident=st.sb("ident", [P, P]), cum=m("cum"), after=m("after"), mid=m("mid"),
                            midx=m("midx"), cum_u=m("cumu", I32), before_u=m("beforeu", I32),
                            levels=st.sb("levels", [P, LEVELS, 2, P]), state=st.sb("state", [P, 8, P]),
                            aak=st.sb("aak", [P, 16, P]), arb=st.sb("arb", [P, 16, P]), ark=st.sb("ark", [P, 16, P]))
        s_zero = st.sem("zero")
        with nc.Block() as block:
            @block.vector
            def _(dve):
                for t in (r.aak, r.arb, r.ark):
                    dve.memset(t[:], 0.0).then_inc(s_zero, 1)
        half = lambda q: slice(64 * q, 64 * q + 64)
        copy_stage(nc, [
            (r.ident[:], e.ident), (r.cum[:], e.cum), (r.after[:], e.after), (r.mid[:], e.mid), (r.midx[:], e.midx),
            (r.cum_u[:], e.cum_u), (r.before_u[:], e.before_u), (r.levels[:], e.levels),
            (r.state[:], e.zero_state)])
        rwkv_unit(nc, e, r, (0, 0))
        copy_stage(nc, [(e.new_rwkv[l, q], r.state[half(q), :, half(q)]) for q in range(2)],
                   then=[(r.state[half(q), :, half(q)], e.state_rwkv[l, q]) for q in range(2)])
        with nc.Fori(0, LAT_TILES) as i:
            rwkv_unit(nc, e, r, (i + 1, LAT_TILES - i))
    rwkv_finish(nc, e, l)


def constants():
    j, t = np.arange(P)[:, None], np.arange(P)[None]
    mirror = lambda m: np.stack([m, m[::-1, ::-1]], 1).astype(np.float32)
    cum = mirror(j <= t)
    levels, spans = [], []
    for v in range(LEVELS):
        s = 1 << v
        levels.append(mirror((j // (2 * s) == t // (2 * s)) & ((j // s) % 2 == 1) & ((t // s) % 2 == 0)))
        mid = (t // (2 * s)) * 2 * s + s - 1
        spans.append(mirror(((t > mid) & (j > mid) & (j <= t)) | ((t <= mid) & (j > t) & (j <= mid))))
    levels, spans = np.stack(levels, 1), np.stack(spans, 1)
    mid = [mirror(((j >= P // 2) & (j <= t - k)).astype(np.float32) - ((j < P // 2) & (j > t - k))) for k in (0, 1)]
    inv = 10000.0 ** (-np.arange(32, dtype=np.float32) / 32)
    rope = np.zeros((CTX + LAT, 2, 2, 32), np.float32)
    rope[:, 0] = 1.0
    pos = np.arange(LAT)
    for a, grid in enumerate((pos // GRID_W, pos % GRID_W)):
        angle = grid.astype(np.float32)[:, None] * inv[None]
        rope[CTX:, 0, a], rope[CTX:, 1, a] = np.cos(angle), np.sin(angle)
    key_shift = np.zeros((32, GRID_W, P), np.float32)
    for ck in range(GRID_W):
        for p in range(P):
            cq = p % GRID_W
            first = min(max(cq - NA_WC // 2, 0), GRID_W - NA_WC)
            key_shift[0, ck, p] = 0.0 if first <= ck < first + NA_WC else -1e30
            if 0 <= ck - cq + NA_WC - 1 < 2 * NA_WC - 1:
                key_shift[ck - cq + NA_WC, ck, p] = 1.0
    return {
        "ident": np.eye(P, dtype=np.float32), "ones": np.ones((P, P), np.float32), "cum": cum, "after": 1 - cum,
        "levels": levels, "levels_t": np.ascontiguousarray(levels[:, :, ::-1]), "spans": spans,
        "mid": mid[0], "midx": mid[1], "cum_u": cum.astype(np.int32),
        "before_u": (cum * (1 - np.eye(P, dtype=np.float32)[:, None])).astype(np.int32),
        "zero_state": np.zeros((P, 8, P), np.float32), "rope": rope.reshape(CTX + LAT, P),
        "key_shift": key_shift.reshape(32, GRID_W * P),
        "layer_base": np.arange(DEPTH, dtype=np.float32).reshape(DEPTH, 1, 1).repeat(P, 1) * N_EXPERTS,
        "iota16": np.tile(np.arange(TOPK, dtype=np.float32), (P, 1)),
    }


def end_stage(nc, e):
    copy_stage(nc, [(e.y_prompt, e.X[0:CTX, :]), (e.y_sample, e.X[CTX:, :])])


def build(nc, e):
    with ExitStack() as ctx:
        s_rows = [ctx.enter_context(nc.semaphore(f"rows{n}")) for n in range(SLOTS)]
        start_stage(nc, e)
        with nc.Fori(0, DEPTH) as l:
            mod_stage(nc, e, l)
            project_stage(nc, e, l, 0, e.w_in[l], IN_W, e.PR[ROW_LAT:ROW_LAT + LAT, :], e.PR[ROW_CTX:ROW_CTX + CTX, :])
            attention_stage(nc, e, l)
            gdn_pass(nc, e, l)
            hgrn_pass(nc, e, l)
            rwkv_pass(nc, e, l)
            merge_stage(nc, e, l)
            project_stage(nc, e, l, 3, e.peer_wq[l], 2 * HEADS * HALF, e.QH[CTX:, :], e.QH[0:CTX, :])
            route_stage(nc, e, l, 0)
            with Stage(nc, "experts") as st:
                row = st.sb("row", [P, SLOTS, D])
                expert_stage(nc, e, l, 0, row, s_rows, first=True, last=False)
                with nc.Fori(1, TILES - 1) as i:
                    expert_stage(nc, e, l, i, row, s_rows, first=False, last=False)
                expert_stage(nc, e, l, TILES - 1, row, s_rows, first=False, last=True)
        end_stage(nc, e)


SCRATCH = {
    "X": (CTX + LAT, D), "PR": (P_ROWS, IN_W), "MOD": (TILES, 6 * D), "LB": (DEPTH, 512), "Y": (CTX + LAT, 2048),
    "GQ": (CTX + LAT, 1552), "OG": (2, CTX + LAT, 512), "OH": (2, CTX + LAT, 512), "OR": (2, CTX + LAT, 512),
    "RQ": (CTX + LAT, 9 * RW), "QH": (CTX + LAT, 2048), "G": (CTX + LAT, PICKS),
}
OUTPUTS = {
    "y_prompt": (CTX, D), "y_sample": (LAT, D), "new_gdn": (DEPTH, 2, GD_H, P, P), "new_hgrn": (DEPTH, 2, HG_H, P, P),
    "new_rwkv": (DEPTH, 2, RW_D, 8, RW_D), "new_k": (DEPTH, NA_H, CTX, NA_D), "new_v": (DEPTH, NA_H, CTX, NA_D),
}


def kernel(**inputs):
    import concourse.bacc as _bacc
    from concourse.bass_utils import run_bass_kernel_spmd as _run

    a = {k: np.ascontiguousarray(v) for k, v in inputs.items()}
    arrays = constants()
    for k in ("w_mod", "b_mod", "w_in", "gdn_conv", "gdn_norm", "hg_lb_logits", "hg_norm", "rw_mu", "rw_w0", "rw_a0",
              "rw_a2", "rw_g2", "rw_kk", "rw_ka", "rw_gn_w", "rw_gn_b", "w_branch", "w_out", "ln1_g", "ln1_b",
              "ln2_g", "ln2_b", "peer_wq"):
        arrays[k] = a[k]
    arrays.update(
        x_prompt=a["x_prompt"][0], x_sample=a["x_sample"][0],
        c_cols=np.stack([a["c_ctx"], a["c"][0]], -1).reshape(KD, P, 2).transpose(1, 0, 2),
        gdn_A_log=a["gdn_A_log"].reshape(DEPTH, 8), gdn_dt_bias=a["gdn_dt_bias"].reshape(DEPTH, 8),
        rw_rk=a["rw_rk"].reshape(DEPTH, RW), rw_w2=a["rw_w2"].reshape(DEPTH, P, RW),
        rpb_t=a["na_rpb"].transpose(0, 3, 1, 2).reshape(DEPTH, 2 * NA_WC - 1, -1),
        cache_k=a["cache_k_na"][0], cache_v=a["cache_v_na"][0],
        state_gdn=a["state_gdn"][0], state_hgrn=a["state_hgrn"][0],
        state_rwkv=a["state_rwkv"][0].reshape(DEPTH, 2, 4, 2, RW_D, RW_D).transpose(0, 3, 5, 1, 2, 4)
        .reshape(DEPTH, 2, RW_D, 8, RW_D),
        keys_t=a["peer_keys"].reshape(DEPTH, 2 * HEADS, NKEYS, HALF).transpose(0, 3, 1, 2),
        peer_u=a["peer_u"].reshape(DEPTH * N_EXPERTS, D), peer_v=a["peer_v"].reshape(DEPTH * N_EXPERTS, D))
    arrays = {f"in_{k}": np.ascontiguousarray(v) for k, v in arrays.items()}

    Stage.count = 0
    nc = _bacc.Bacc("TRN2", target_bir_lowering=False, num_devices=1)
    e = {k[3:]: nc.dram_tensor(k, v.shape, mybir.dt.from_np(v.dtype), kind="ExternalInput").ap()
         for k, v in arrays.items()}
    e.update({k: nc.dram_tensor(f"scratch_{k}", v, F32).ap() for k, v in SCRATCH.items()})
    e["EIDX"] = nc.dram_tensor("scratch_EIDX", (CTX + LAT, PICKS), I32).ap()
    e.update({k: nc.dram_tensor(f"out_{k}", v, F32, kind="ExternalOutput").ap() for k, v in OUTPUTS.items()})
    build(nc, named(**e))
    got = _run(nc, [arrays], core_ids=[0]).results[0]
    out = {k: got[f"out_{k}"] for k in OUTPUTS}
    rwkv = out["new_rwkv"].reshape(DEPTH, 2, RW_D, 2, 4, RW_D).transpose(0, 3, 4, 1, 5, 2)
    return (out["y_prompt"][None], out["y_sample"][None], out["new_gdn"][None], out["new_hgrn"][None],
            np.ascontiguousarray(rwkv.reshape(1, DEPTH, 2, RW_H, RW_D, RW_D)), out["new_k"][None],
            out["new_v"][None])
```
